# Optimizing a Trainium2 kernel written in Bass

```python
import math
import jax, jax.numpy as jnp
from jax import lax
import numpy as np

D_MODEL = 1024
BATCH = 1
SEQ = 256
DEPTH = 2

HEAD_DIM = 64
ROPE_THETA = 10000.0
EPS = 1e-6
SWA_WIDTH = D_MODEL // 2
SWA_Q_HEADS = SWA_WIDTH // HEAD_DIM
SWA_KV_HEADS = SWA_Q_HEADS // 4
SWA_GROUP = SWA_Q_HEADS // SWA_KV_HEADS
WINDOW = 128
BLOCK = 128
DIFF_V_DIM = 2 * HEAD_DIM
DIFF_WIDTH = D_MODEL - SWA_WIDTH
DIFF_HEADS = DIFF_WIDTH // DIFF_V_DIM
MIX_WIDTH = SWA_WIDTH + DIFF_WIDTH
COL_QA = SWA_Q_HEADS * HEAD_DIM
COL_KA = SWA_KV_HEADS * HEAD_DIM
COL_VA = SWA_KV_HEADS * HEAD_DIM
COL_QD = DIFF_HEADS * 2 * HEAD_DIM
COL_KD = DIFF_HEADS * 2 * HEAD_DIM
COL_VD = DIFF_HEADS * DIFF_V_DIM
IN_COLS = COL_QA + COL_KA + COL_VA + COL_QD + COL_KD + COL_VD
SPLITS = [COL_QA, COL_QA + COL_KA, COL_QA + COL_KA + COL_VA,
          COL_QA + COL_KA + COL_VA + COL_QD,
          COL_QA + COL_KA + COL_VA + COL_QD + COL_KD]
D_FF = 3584
N_EXPERTS = 8
TOP_K = 2
MOE_ROWS = 256
N_DENSE = (DEPTH + 1) // 2
N_MOE = DEPTH // 2
N_MOD = 6

kernel_name = "hybrid_swa_sink_diffattn_moe_adaln_encoder"

def rms_norm(x, g):
    xf = x.astype(jnp.float32)
    y = xf * lax.rsqrt(jnp.mean(xf * xf, axis=-1, keepdims=True) + EPS)
    return (y * g.astype(jnp.float32)).astype(x.dtype)

def rope_tables(positions):
    inv = 1.0 / (ROPE_THETA ** (jnp.arange(0, HEAD_DIM, 2, dtype=jnp.float32) / HEAD_DIM))
    ang = positions.astype(jnp.float32)[..., None] * inv
    return jnp.cos(ang)[:, :, None, :], jnp.sin(ang)[:, :, None, :]

def apply_rope(t, cos, sin):
    t1, t2 = jnp.split(t.astype(jnp.float32), 2, axis=-1)
    return jnp.concatenate([t1 * cos - t2 * sin, t2 * cos + t1 * sin], axis=-1).astype(t.dtype)

def window_attention(q, k, v, sink):
    B, S = q.shape[0], q.shape[1]
    nb = S // BLOCK
    qb = q.reshape(B, nb, BLOCK, SWA_KV_HEADS, SWA_GROUP, HEAD_DIM)

    def band(t):
        tb = t.reshape(B, nb, BLOCK, SWA_KV_HEADS, HEAD_DIM)
        tp = jnp.pad(tb, ((0, 0), (1, 1), (0, 0), (0, 0), (0, 0)))
        return jnp.concatenate([tp[:, :-2], tp[:, 1:-1], tp[:, 2:]], axis=2)

    kb, vb = band(k), band(v)
    q_pos = jnp.arange(S).reshape(nb, BLOCK)
    k_pos = (jnp.arange(nb)[:, None] - 1) * BLOCK + jnp.arange(3 * BLOCK)[None, :]
    kp = k_pos[:, None, :]
    valid = (jnp.abs(q_pos[:, :, None] - kp) <= WINDOW) & (kp >= 0) & (kp < S)
    s = jnp.einsum('bnqhgd,bnkhd->bnhgqk', qb, kb,
                   preferred_element_type=jnp.float32) * (HEAD_DIM ** -0.5)
    s = jnp.where(valid[None, :, None, None], s, -jnp.inf)
    sk = sink.astype(jnp.float32).reshape(1, 1, SWA_KV_HEADS, SWA_GROUP, 1, 1)
    m = jnp.maximum(s.max(axis=-1, keepdims=True), sk)
    p = jnp.exp(s - m)
    p = p / (p.sum(axis=-1, keepdims=True) + jnp.exp(sk - m))
    o = jnp.einsum('bnhgqk,bnkhd->bnqhgd', p.astype(v.dtype), vb)
    return o.reshape(B, S, SWA_WIDTH)

def diff_attention(q, k, v, lam, subln_g, lambda_init):
    B, S = q.shape[0], q.shape[1]
    nb = S // BLOCK
    qb = jnp.moveaxis(q.reshape(B, nb, BLOCK, DIFF_HEADS, 2, HEAD_DIM), 1, 0)

    def one_block(q_blk):
        s = jnp.einsum('bqhcd,bkhcd->bhcqk', q_blk, k,
                       preferred_element_type=jnp.float32) * (HEAD_DIM ** -0.5)
        p = jax.nn.softmax(s, axis=-1)
        a = p[:, :, 0] - lam * p[:, :, 1]
        return jnp.einsum('bhqk,bkhe->bqhe', a.astype(v.dtype), v)

    o = lax.map(one_block, qb)
    o = jnp.moveaxis(o, 0, 1).reshape(B, S, DIFF_HEADS, DIFF_V_DIM)
    o = rms_norm(o, subln_g) * (1.0 - lambda_init)
    return o.reshape(B, S, DIFF_WIDTH)

def token_mixer(h, cos, sin, w_in, w_out, sink, lq1, lk1, lq2, lk2, subln_g, lambda_init):
    B, S = h.shape[0], h.shape[1]
    proj = h @ w_in
    qa, ka, va, qd, kd, vd = jnp.split(proj, SPLITS, axis=-1)
    qa = apply_rope(qa.reshape(B, S, SWA_Q_HEADS, HEAD_DIM), cos, sin)
    ka = apply_rope(ka.reshape(B, S, SWA_KV_HEADS, HEAD_DIM), cos, sin)
    va = va.reshape(B, S, SWA_KV_HEADS, HEAD_DIM)
    qd = apply_rope(qd.reshape(B, S, 2 * DIFF_HEADS, HEAD_DIM), cos, sin).reshape(B, S, DIFF_HEADS, 2, HEAD_DIM)
    kd = apply_rope(kd.reshape(B, S, 2 * DIFF_HEADS, HEAD_DIM), cos, sin).reshape(B, S, DIFF_HEADS, 2, HEAD_DIM)
    vd = vd.reshape(B, S, DIFF_HEADS, DIFF_V_DIM)
    lam = (jnp.exp(jnp.sum(lq1.astype(jnp.float32) * lk1.astype(jnp.float32)))
           - jnp.exp(jnp.sum(lq2.astype(jnp.float32) * lk2.astype(jnp.float32))) + lambda_init)
    ya = window_attention(qa, ka, va, sink)
    yd = diff_attention(qd, kd, vd, lam, subln_g, lambda_init)
    return jnp.concatenate([ya, yd], axis=-1) @ w_out

def swiglu(h, w_gate, w_up, w_down):
    return (jax.nn.silu(h @ w_gate) * (h @ w_up)) @ w_down

def moe_swiglu(h, router_w, w_gate, w_up, w_down):
    B, S, D = h.shape
    xt = h.reshape(-1, D)
    N = xt.shape[0]
    logits = jnp.dot(xt, router_w, preferred_element_type=jnp.float32)
    top_val, top_idx = lax.top_k(logits, TOP_K)
    top_w = jax.nn.softmax(top_val, axis=-1)
    flat_e = top_idx.reshape(-1)
    flat_tok = jnp.repeat(jnp.arange(N, dtype=jnp.int32), TOP_K)
    flat_w = top_w.reshape(-1)
    order = jnp.argsort(flat_e)
    sorted_e = flat_e[order]
    counts = jnp.bincount(flat_e, length=N_EXPERTS)
    starts = jnp.cumsum(counts) - counts
    padded = (counts + MOE_ROWS - 1) // MOE_ROWS * MOE_ROWS
    pad_ends = jnp.cumsum(padded)
    pad_starts = pad_ends - padded
    dest = pad_starts[sorted_e] + jnp.arange(N * TOP_K) - starts[sorted_e]
    P = (N * TOP_K + MOE_ROWS - 1) // MOE_ROWS * MOE_ROWS + N_EXPERTS * MOE_ROWS
    n_chunks = P // MOE_ROWS
    buf_tok = jnp.full((P,), N, jnp.int32).at[dest].set(flat_tok[order])
    buf_w = jnp.zeros((P,), jnp.float32).at[dest].set(flat_w[order])
    chunk_e = jnp.minimum(jnp.searchsorted(pad_ends, jnp.arange(n_chunks) * MOE_ROWS, side='right'),
                          N_EXPERTS - 1)
    xs = xt[jnp.minimum(buf_tok, N - 1)].reshape(n_chunks, MOE_ROWS, D)

    def expert_block(args):
        xc, e = args
        return swiglu(xc, w_gate[e], w_up[e], w_down[e])

    ys = lax.map(expert_block, (xs, chunk_e)).reshape(P, D)
    out = jnp.zeros((N, D), ys.dtype).at[buf_tok].add(ys * buf_w[:, None].astype(ys.dtype), mode='drop')
    return out.reshape(B, S, D)

def setup_inputs(seed: int = 0) -> dict:
    key = jax.random.key(seed)
    ks = jax.random.split(key, 24)
    f32 = jnp.float32
    nrm = lambda k, shape, s: jax.random.normal(k, shape, f32) * s
    D, F, E = D_MODEL, D_FF, N_EXPERTS
    return {
        "x": nrm(ks[0], (BATCH, SEQ, D), 1.0),
        "c": nrm(ks[1], (BATCH, D), 1.0),
        "positions": jnp.broadcast_to(jnp.arange(SEQ, dtype=jnp.int32)[None, :], (BATCH, SEQ)),
        "ada_w": nrm(ks[2], (DEPTH, D, N_MOD * D), D ** -0.5),
        "ada_b": nrm(ks[3], (DEPTH, N_MOD * D), 0.02),
        "norm_mix_g": 1.0 + nrm(ks[4], (DEPTH, D), 0.02),
        "norm_ffn_g": 1.0 + nrm(ks[5], (DEPTH, D), 0.02),
        "w_in": nrm(ks[6], (DEPTH, D, IN_COLS), D ** -0.5),
        "w_out": nrm(ks[7], (DEPTH, MIX_WIDTH, D), MIX_WIDTH ** -0.5),
        "sink": nrm(ks[8], (DEPTH, SWA_Q_HEADS), 0.5),
        "lam_q1": nrm(ks[9], (DEPTH, HEAD_DIM), 0.1),
        "lam_k1": nrm(ks[10], (DEPTH, HEAD_DIM), 0.1),
        "lam_q2": nrm(ks[11], (DEPTH, HEAD_DIM), 0.1),
        "lam_k2": nrm(ks[12], (DEPTH, HEAD_DIM), 0.1),
        "subln_g": 1.0 + nrm(ks[13], (DEPTH, DIFF_V_DIM), 0.02),
        "ffn_w_gate": nrm(ks[14], (N_DENSE, D, F), D ** -0.5),
        "ffn_w_up": nrm(ks[15], (N_DENSE, D, F), D ** -0.5),
        "ffn_w_down": nrm(ks[16], (N_DENSE, F, D), F ** -0.5),
        "router_w": nrm(ks[17], (N_MOE, D, E), D ** -0.5),
        "moe_w_gate": nrm(ks[18], (N_MOE, E, D, F), D ** -0.5),
        "moe_w_up": nrm(ks[19], (N_MOE, E, D, F), D ** -0.5),
        "moe_w_down": nrm(ks[20], (N_MOE, E, F, D), F ** -0.5),
        "final_g": 1.0 + nrm(ks[21], (D,), 0.02),
    }

def reference(x, c, positions, ada_w, ada_b, norm_mix_g, norm_ffn_g, w_in, w_out, sink,
              lam_q1, lam_k1, lam_q2, lam_k2, subln_g, ffn_w_gate, ffn_w_up, ffn_w_down,
              router_w, moe_w_gate, moe_w_up, moe_w_down, final_g):
    cos, sin = rope_tables(positions)
    c_act = jax.nn.silu(c)
    for layer in range(DEPTH):
        mod = c_act @ ada_w[layer] + ada_b[layer]
        sh_m, sc_m, g_m, sh_f, sc_f, g_f = [t[:, None, :] for t in jnp.split(mod, N_MOD, axis=-1)]
        lambda_init = 0.8 - 0.6 * math.exp(-0.3 * layer)
        h = rms_norm(x, norm_mix_g[layer]) * (1.0 + sc_m) + sh_m
        x = x + g_m * token_mixer(h, cos, sin, w_in[layer], w_out[layer], sink[layer],
                                  lam_q1[layer], lam_k1[layer], lam_q2[layer], lam_k2[layer],
                                  subln_g[layer], lambda_init)
        h = rms_norm(x, norm_ffn_g[layer]) * (1.0 + sc_f) + sh_f
        if layer % 2 == 0:
            i = layer // 2
            y = swiglu(h, ffn_w_gate[i], ffn_w_up[i], ffn_w_down[i])
        else:
            i = layer // 2
            y = moe_swiglu(h, router_w[i], moe_w_gate[i], moe_w_up[i], moe_w_down[i])
        x = x + g_f * y
    return rms_norm(x, final_g)


_drawn_inputs = setup_inputs


def setup_inputs(seed=0):
    import zlib

    import numpy as np

    out = dict(_drawn_inputs(seed))
    spreads = {}
    factors = {'norm_mix_g': 2.72,
     'sink': 64.0,
     'lam_q1': 4.274,
     'lam_q2': 2.974,
     'subln_g': 3.343,
     'final_g': 7.581}
    for name, (base, spread) in spreads.items():
        noise = np.random.default_rng([zlib.crc32(name.encode()), seed]).standard_normal(out[name].shape)
        drawn = base * np.exp(spread * noise) if base else spread * noise
        out[name] = __import__('jax').numpy.asarray(drawn.astype(out[name].dtype))
    for name, factor in factors.items():
        out[name] = (out[name] * factor).astype(out[name].dtype)
    return out
```

```python
import math
from contextlib import ExitStack

import numpy as np

import concourse.bass as bass
from concourse import mybir

ALU = mybir.AluOpType
ACT = mybir.ActivationFunctionType
AX_X = mybir.AxisListType.X
F32 = mybir.dt.float32
F32R = mybir.dt.float32r
BF16 = mybir.dt.bfloat16
I32 = mybir.dt.int32
U32 = mybir.dt.uint32

P = 128
D = 1024
SEQ = 256
DEPTH = 2
NT = SEQ // P
KD = D // P
HEAD = 64
HALF = HEAD // 2
EPS = 1e-6
N_WIN = 8
N_DIFF = 4
WIN_WIDTH = 512
IN_COLS = 2304
D_FF = 3584
BLOCK = 512
NB = D_FF // BLOCK
HB = BLOCK // 2
N_EXP = 8
MAX_OVER = 3
N_SLOT = N_EXP + MAX_OVER
SCALE = HEAD ** -0.5
MASKED = -1e30
ROUNDER = 12582912.0
TWO_PI_PARTS = (6.28125, 0.0019350051879882812, 3.0199159819567e-07)

CH = 4096
PART = CH // 2
PARTS = 6
IN_CHUNKS = 5
OUT_CHUNKS = 2
ADA_CHUNKS = 12
RING = 3

IN_PARTS, OUT_PARTS = 2 * IN_CHUNKS, 2 * OUT_CHUNKS
IN_BASE = [0, IN_PARTS + OUT_PARTS + NB * PARTS]
OUT_BASE = [b + IN_PARTS for b in IN_BASE]
FF_BASE = [b + OUT_PARTS for b in OUT_BASE]

UNITS = 16
ROPE_GROUPS = [[(0, 8, 0)], [(0, 2, 4), (256, 4, 6)], [(0, 8, 8)], [(0, 4, 12)], []]
V_GROUPS = [[], [(128, 128, 0)], [], [(256, 256, 128)], [(0, 256, 384)]]
QK_TILES = 14


class Count:

    def __init__(self, sem):
        self.sem, self.n = sem, 0

    def mark(self, instruction):
        instruction.then_inc(self.sem, 1)
        self.n += 1
        return self.n


def plan_ring():
    loads, holder, plan = [0] * RING, [None] * RING, {}

    def put(name, slot, holds):
        plan[name] = (slot, holder[slot], loads[slot] + 16)
        loads[slot] += 16
        holder[slot] = holds

    for n in range(ADA_CHUNKS):
        put(("ada", 0, n), n % RING, ("ada", n + 1))
    for c in range(IN_CHUNKS):
        put(("in", 0, c), c % RING, ("split", IN_BASE[0] + 2 * c + 2))
    for c in range(OUT_CHUNKS):
        put(("out", 0, c), (IN_CHUNKS + c) % RING, ("split", OUT_BASE[0] + 2 * c + 2))
    for n in range(ADA_CHUNKS):
        put(("ada", 1, n), (IN_CHUNKS + OUT_CHUNKS + n) % RING, ("ada", ADA_CHUNKS + n + 1))
    plan["dense"] = list(loads)
    for c, dmas in enumerate((2, 2, 1)):
        loads[c] += 16 * dmas * NB
        holder[c] = ("split", FF_BASE[0] + PARTS * (NB - 1) + 2 * c + 2)
    for c in range(IN_CHUNKS):
        put(("in", 1, c), (c + 2) % RING, ("split", IN_BASE[1] + 2 * c + 2))
    for c in range(OUT_CHUNKS):
        put(("out", 1, c), (IN_CHUNKS + c + 2) % RING, ("split", OUT_BASE[1] + 2 * c + 2))
    plan["experts"] = list(loads)
    return plan


def build(nc, x_in, c_in, positions, inv_freq, ada_w, ada_b, mix_g, ffn_g, w_in, w_out, sink,
          lam_q1, lam_k1, lam_q2, lam_k2, subln_g, w_gate, w_up, w_down,
          router_w, moe_gate, moe_up, moe_down, final_g, out):
    plan = plan_ring()
    with ExitStack() as ctx:
        top = [(nc.sbuf_base + 63) // 64 * 64]

        def region(nbytes):
            at = top[0]
            top[0] += (nbytes + 31) // 32 * 32
            return at

        def place(name, shape, dtype, at=None):
            words = int(np.prod(shape[1:]))
            size = words * (2 if dtype == BF16 else 4)
            return nc.alloc_sbuf_tensor_at(name, shape, dtype, offset=region(size) if at is None else at)

        W = place("weights", [P, RING, CH], F32)
        Hg = place("weights_hi", [P, 2, CH], F32R)
        Lg = place("weights_lo", [P, 2, CH], F32R)
        at = region(2 * CH * 4)
        Hd = place("down_hi", [P, CH], F32R, at)
        Ld = place("down_lo", [P, CH], F32R, at + CH * 4)
        qk = place("qk", [P, NT, QK_TILES * P], F32, at)
        qkT = place("qkT", [P, QK_TILES, SEQ], F32, at + NT * QK_TILES * P * 4)
        x = place("x", [P, NT, D], F32)
        xn = place("xn", [P, NT, D], F32)
        hTh = place("hT_hi", [P, KD, SEQ], F32R)
        hTl = place("hT_lo", [P, KD, SEQ], F32R)
        at = region(3 * 512 * 4)
        modrow = place("modrow", [P, 3, 512], F32, at)
        ysb = place("ysb", [P, D], F32, at)
        gate = place("gate", [P, 2, D], F32)
        fing = place("fing", [P, D], F32)
        at = region(17 * 1024)
        v = place("v", [P, NT, 640], F32, at)
        scores = place("scores", [P, 2, 2, SEQ], F32, at + 5120)
        rope_a = place("rope_a", [P, 512], F32, at + 5120)
        rope_b = place("rope_b", [P, 512], F32, at + 5120 + 2048)
        E = place("E", [P, 2, 2, SEQ], F32, at + 9216)
        tmp = place("tmp", [P, 2, 512], F32, at + 9216)
        PT = place("PT", [P, 2, 4, P], F32, at + 13312)
        lamv = place("lamv", [P, 4, DEPTH * HEAD], F32, at + 13312)
        subg = place("subg", [P, DEPTH, P], F32, at + 15360)
        vecrows = place("vecrows", [40, P], F32, at + 5120)
        ang = place("ang", [P, NT, HALF], F32, at + 16384)
        turns = place("turns", [P, NT, HALF], F32, at + 16640)
        arg = place("arg", [P, 2, NT, HALF], F32, at + 16896)
        sg = place("sg", [P, 2, HB], F32, at)
        act_sb = place("act", [P, 2, HB], F32, at + 2048)
        aTh = place("actT_hi", [P, 2, 2, P], F32R, at + 4096)
        aTl = place("actT_lo", [P, 2, 2, P], F32R, at + 6144)
        xsT = place("xsT", [P, KD, P], F32, at + 8192)
        pick = place("pick", [P, NT, P], F32, at + 12288)
        pickw = place("pickw", [P, NT, P], F32, at + 13312)
        pickT = place("pickT", [P, NT, P], F32, at + 14336)
        ident = place("ident", [P, P], F32)
        iota_row = place("iota_row", [P, P], F32)
        ones = place("ones", [P, P], F32)
        before = place("before", [P, P], F32)
        mask = place("mask", [P, NT, SEQ], F32)
        zeros = place("zeros", [P, 512], BF16)
        vcols = place("vcols", [P, 40], F32)
        c_rep = place("c_rep", [P, KD, 32], F32)
        pos_i = place("pos_i", [P, NT], I32)
        pos_f = place("pos_f", [P, NT], F32)
        inv = place("inv", [P, HALF], F32)
        cosF = place("cosF", [P, NT, 2, HALF], F32)
        sinS = place("sinS", [P, NT, 2, HALF], F32)
        sinks = place("sinks", [P, DEPTH * N_WIN], F32)
        negsink = place("negsink", [P, DEPTH * N_WIN], F32)
        lams = place("lams", [P, 2, DEPTH], F32)
        lame = place("lame", [P, 2, DEPTH], F32)
        neglam = place("neglam", [P, DEPTH], F32)
        subgs = place("subgs", [P, DEPTH, P], F32)
        rw = place("rw", [P, KD, N_EXP], F32)
        rwh = place("rwh", [P, KD, N_EXP], F32R)
        rwl = place("rwl", [P, KD, N_EXP], F32R)
        modc = place("modc", [P, DEPTH, 6, KD], F32)
        A = place("A", [P, DEPTH, 2, KD], F32)
        half_neg = place("half_neg", [P, 8], F32)
        ssq = place("ssq", [P, NT], F32)
        ms = place("ms", [P, NT], F32)
        rstd = place("rstd", [P, NT], F32)
        ssq_d = place("ssq_d", [P, NT * N_DIFF], F32)
        ms_d = place("ms_d", [P, NT * N_DIFF], F32)
        rstd_d = place("rstd_d", [P, NT * N_DIFF], F32)
        mx = place("mx", [P, 2, 2], F32)
        negm = place("negm", [P, 2, 2], F32)
        sinkm = place("sinkm", [P, 2, 2], F32)
        sinke = place("sinke", [P, 2, 2], F32)
        sums = place("sums", [P, 2, 2], F32)
        den = place("den", [P, 2, 2], F32)
        rec = place("rec", [P, 2, 2], F32)
        nl = place("nl", [P, 2], F32)
        lg = place("lg", [P, NT, N_EXP], F32)
        mv = place("mv", [P, NT, 8], F32)
        mi = place("mi", [P, NT, 8], U32)
        mf = place("mf", [P, NT, 8], F32)
        oh = place("oh", [P, NT, 2, N_EXP], F32)
        dlt = place("dlt", [P, NT], F32)
        edl = place("edl", [P, NT], F32)
        den2 = place("den2", [P, NT], F32)
        w12 = place("w12", [P, 2, NT], F32)
        chosen = place("chosen", [P, NT, N_EXP], F32)
        wtmp = place("wtmp", [P, NT, N_EXP], F32)
        posS = place("posS", [P, NT, N_SLOT + 1], F32)
        wS = place("wS", [P, NT, N_SLOT + 1], F32)
        over = place("over", [P, N_EXP], F32)
        rank = place("rank", [P, N_EXP + 1], F32)
        sel = place("sel", [P, MAX_OVER, N_EXP], F32)
        prod = place("prod", [P, 5, N_EXP], F32)
        posr = place("posr", [P, NT], F32)
        tabf = place("tabf", [P, 2, 4], F32)
        table = place("table", [P, 2, 4], I32)
        done_mark = place("done_mark", [P, 1], F32)
        assert top[0] <= nc.sbuf_usable_end, top[0]

        ps = ctx.enter_context(nc.psum_tensor("ps", [P, 8, 512], F32))

        def sem(name):
            return ctx.enter_context(nc.semaphore(name))

        w_loaded = [sem(f"w_loaded{i}") for i in range(RING)]
        x_loaded, consts_loaded, late_loaded = sem("x_loaded"), sem("consts_loaded"), sem("late_loaded")
        bias_loaded, table_ready = sem("bias_loaded"), sem("table_ready")
        setup_done, vec_silu, vec_ps, vec_cols = sem("setup_done"), sem("vec_silu"), sem("vec_ps"), sem("vec_cols")
        arg_ready, sin_done, lam_dot, lam_exp = sem("arg_ready"), sem("sin_done"), sem("lam_dot"), sem("lam_exp")
        tables_done = sem("tables_done")
        hi_done, lo_done, lop_done, parts_used = sem("hi_done"), sem("lo_done"), sem("lop_done"), sem("parts_used")
        ada_used, mod_ready, cols_ps, cols_ready = sem("ada_used"), sem("mod_ready"), sem("cols_ps"), sem("cols_ready")
        gates_ps, gates_ready = sem("gates_ps"), sem("gates_ready")
        sq_done, ms_done, rstd_done, xn_done = sem("sq_done"), sem("ms_done"), sem("rstd_done"), sem("xn_done")
        tr_ps, tr_copied, tr_hi, tr_lo = sem("tr_ps"), sem("tr_copied"), sem("tr_hi"), sem("tr_lo")
        proj_ps, rope_done = sem("proj_ps"), sem("rope_done")
        qkT_ps, qkT_even, qkT_odd = sem("qkT_ps"), sem("qkT_even"), sem("qkT_odd")
        s_ps, max_done, exp_done, probs_done = sem("s_ps"), sem("max_done"), sem("exp_done"), sem("probs_done")
        pt_ps, pt_done, o_ps, o_done = sem("pt_ps"), sem("pt_done"), sem("o_ps"), sem("o_done")
        dsq_done, dms_done, drstd_done, mix_done = sem("dsq_done"), sem("dms_done"), sem("drstd_done"), sem("mix_done")
        wo_ps, x_mixed = sem("wo_ps"), sem("x_mixed")
        gu_ps, silu_done, act_done = sem("gu_ps"), sem("silu_done"), sem("act_done")
        at_ps, at_hi, at_lo = sem("at_ps"), sem("at_hi"), sem("at_lo")
        x_ffn = sem("x_ffn")
        rw_hi, rw_lo, logit_ps = sem("rw_hi"), sem("rw_lo"), sem("logit_ps")
        gap_ready, gap_exp, chosen_ready, pos_ps, routed = (
            sem("gap_ready"), sem("gap_exp"), sem("chosen_ready"), sem("pos_ps"), sem("routed"))
        pick_ready, gather_ps, xs_ready = sem("pick_ready"), sem("gather_ps"), sem("xs_ready")
        slot_hi, slot_lo, pickw_ready = sem("slot_hi"), sem("slot_lo"), sem("pickw_ready")
        pickT_ps, pickT_ready, y_ready = sem("pickT_ps"), sem("pickT_ready"), sem("y_ready")
        comb_ps, x_added, moe_done = sem("comb_ps"), sem("x_added"), sem("moe_done")
        dve_step, out_ready, out_written = sem("dve_step"), sem("out_ready"), sem("out_written")

        def bias_loads(layer):
            src = ada_b[layer].rearrange("(r g n) -> g r n", r=3, g=4)
            return [(modrow[32 * g:32 * g + 32, :, :], src[g].partition_broadcast(32)) for g in range(4)]

        const_loads = [
            (vecrows[0:KD, :], c_in[0].rearrange("(k p) -> k p", p=P)),
            (vecrows[KD:3 * KD, :], mix_g.rearrange("l (k p) -> (l k) p", p=P)),
            (vecrows[3 * KD:5 * KD, :], ffn_g.rearrange("l (k p) -> (l k) p", p=P)),
            (pos_i[:], positions[0].rearrange("(t p) -> p t", p=P)),
            (inv[:], inv_freq[0].partition_broadcast(P)),
            (sinks[:], sink.rearrange("l h -> (l h)").partition_broadcast(P)),
            (subg[:], subln_g.rearrange("l n -> (l n)").partition_broadcast(P)),
        ] + [(lamv[:, i, :], lam.rearrange("l n -> (l n)").partition_broadcast(P))
             for i, lam in enumerate((lam_q1, lam_k1, lam_q2, lam_k2))]
        CONSTS = 16 * len(const_loads)
        SETUP = 10

        ada_v = ada_w.rearrange("l (q k p) (r n) -> l r q p k n", k=2, p=P, r=3)
        in_v = w_in.rearrange("l (k p) n -> l p k n", p=P)
        out_v = w_out.rearrange("l (k p) n -> l p k n", p=P)

        def ff_views(g, u, d):
            return (g.rearrange("e (k p) (j n) -> e j p k n", p=P, n=BLOCK),
                    u.rearrange("e (k p) (j n) -> e j p k n", p=P, n=BLOCK),
                    d.rearrange("e (j k p) n -> e j p k n", p=P, k=BLOCK // P))

        dense_v, moe_v = ff_views(w_gate, w_up, w_down), ff_views(moe_gate[0], moe_up[0], moe_down[0])

        hg_ff = [t[:].rearrange("p c (k g n) -> p c k g n", k=4, g=2) for t in (Hg, Lg)]
        hd_ff = [t[:].rearrange("p (k n) -> p k n", n=D) for t in (Hd, Ld)]

        def split_views(hslot, off, n, pool):
            a, b = (off + n * 3 // 4, off + n) if pool else (off, off + n * 3 // 4)
            return slice(a, b)

        def halves(hslot):
            return (Hg[:, hslot, :], Lg[:, hslot, :]) if hslot < 2 else (Hd[:], Ld[:])

        def straight_parts(kind, layer, c):
            base = IN_BASE[layer] + 2 * c + (IN_PARTS if kind == "out" else 0)
            n = PART if kind == "out" or c < IN_CHUNKS - 1 else PART // 2
            i = c + (IN_CHUNKS if kind == "out" else 0)
            for h in range(2):
                if kind == "out" and c == 1:
                    freed = base - 2
                elif i >= 2:
                    freed = base + h - 3
                elif layer:
                    freed = FF_BASE[0] + PARTS * (NB - 1) + 2 * i + h + 1
                else:
                    freed = 0
                yield base + h, plan[(kind, layer, c)][0], i % 2, h * n, n, freed

        block = ctx.enter_context(nc.Block())

        GU0 = {4: 0, 2: 3 * NB}
        U0 = {4: 0, 2: 4 * NB}

        @block.sync
        def _(sp):
            def free(holder):
                if holder is None:
                    return
                what, value = holder
                if what == "ada":
                    sp.wait_ge(ada_used, value)
                else:
                    sp.wait_ge(hi_done, value)
                    sp.wait_ge(lo_done, value)
                    sp.wait_ge(lop_done, value)

            def load(name, dst, src):
                slot, holder, _ = plan[name]
                free(holder)
                sp.dma_start(dst, src).then_inc(w_loaded[slot], 16)

            def ada(layer):
                for n in range(ADA_CHUNKS):
                    slot = plan[("ada", layer, n)][0]
                    load(("ada", layer, n), W[:, slot, :].rearrange("p (k n) -> p k n", k=2),
                         ada_v[layer, n // 4, n % 4])

            def mixer(layer):
                for c in range(IN_CHUNKS):
                    n = 512 if c < IN_CHUNKS - 1 else 256
                    slot = plan[("in", layer, c)][0]
                    load(("in", layer, c), W[:, slot, 0:KD * n].rearrange("p (k n) -> p k n", k=KD),
                         in_v[layer, :, :, 512 * c:512 * c + n])
                for c in range(OUT_CHUNKS):
                    slot = plan[("out", layer, c)][0]
                    load(("out", layer, c), W[:, slot, :].rearrange("p (k n) -> p k n", k=KD),
                         out_v[layer, :, :, 512 * c:512 * c + 512])

            def blocks(views, e, base, first):
                gate_v, up_v, down_v = views
                with sp.Fori(0, NB) as j:
                    for c in range(2):
                        value = (first + j) * PARTS + (base - PARTS + 2 * c + 2)
                        sp.wait_ge(hi_done, value)
                        sp.wait_ge(lo_done, value)
                        sp.wait_ge(lop_done, value)
                        dst = W[:, c, :].rearrange("p (k g n) -> p k g n", k=4, g=2)
                        for g, view in enumerate((gate_v, up_v)):
                            src = view[bass.ds(e, 1), bass.ds(j, 1), :, 4 * c:4 * c + 4, :]
                            sp.dma_start(dst[:, :, g, :], src.rearrange("a b p k n -> p (a b k) n")).then_inc(
                                w_loaded[c], 16)
                    value = (first + j) * PARTS + base
                    sp.wait_ge(hi_done, value)
                    sp.wait_ge(lo_done, value)
                    sp.wait_ge(lop_done, value)
                    src = down_v[bass.ds(e, 1), bass.ds(j, 1), :, :, :]
                    sp.dma_start(W[:, 2, :].rearrange("p (k n) -> p k n", n=D),
                                 src.rearrange("a b p k n -> p (a b k) n")).then_inc(w_loaded[2], 16)

            ada(0)
            mixer(0)
            ada(1)
            sp.wait_ge(ada_used, 2 * ADA_CHUNKS)
            blocks(dense_v, 0, FF_BASE[0], 0)
            mixer(1)
            with sp.Fori(0, N_EXP) as s:
                blocks(moe_v, s, FF_BASE[1], s * NB)
            sp.wait_ge(table_ready, 1)
            with sp.Fori(0, MAX_OVER) as o:
                used = sp.value_load(table[0:1, 1, bass.ds(o, 1)], min_val=0, max_val=1)
                with sp.If(used > 0):
                    e = sp.value_load(table[0:1, 0, bass.ds(o, 1)], min_val=0, max_val=N_EXP - 1)
                    blocks(moe_v, e, FF_BASE[1], (o + N_EXP) * NB)
            sp.wait_ge(out_ready, NT)
            sp.dma_start(out[0].rearrange("(t p) n -> p t n", p=P), xn[:]).then_inc(out_written, 16)
            sp.wait_ge(out_written, 16)

        @block.gpsimd
        def _(pool):
            pool.memset(ident[:], 0.0).then_inc(setup_done, 1)
            pool.memset(mask[:], 0.0).then_inc(setup_done, 1)
            pool.memset(ones[:], 1.0).then_inc(setup_done, 1)
            pool.memset(zeros[:], 0.0).then_inc(setup_done, 1)
            pool.memset(half_neg[:], -0.5).then_inc(setup_done, 1)
            pool.wait_ge(setup_done, 5)
            pool.affine_select(out=ident[:], in_=ident[:], compare_op=ALU.not_equal, fill=1.0, base=0,
                               pattern=[[-1, P]], channel_multiplier=1).then_inc(setup_done, 1)
            pool.affine_select(out=before[:], in_=ones[:], compare_op=ALU.is_gt, fill=0.0, base=0,
                               pattern=[[1, P]], channel_multiplier=-1).then_inc(setup_done, 1)
            pool.affine_select(out=mask[:, 0, P:], in_=mask[:, 0, P:], compare_op=ALU.is_ge, fill=MASKED,
                               base=0, pattern=[[-1, P]], channel_multiplier=1).then_inc(setup_done, 1)
            pool.affine_select(out=mask[:, 1, :P], in_=mask[:, 1, :P], compare_op=ALU.is_ge, fill=MASKED,
                               base=0, pattern=[[1, P]], channel_multiplier=-1).then_inc(setup_done, 1)
            pool.iota(iota_row[:], pattern=[[1, P]], base=0, channel_multiplier=0,
                      allow_small_or_imprecise_dtypes=True).then_inc(setup_done, 1)

            def low(q, wslot, hslot, off, n):
                at = split_views(hslot, off, n, True)
                hi, lo = halves(hslot)
                pool.wait_ge(hi_done, q + 1)
                pool.tensor_tensor(lo[:, at], W[:, wslot, at], hi[:, at].bitcast(F32),
                                   ALU.subtract).then_inc(lop_done, 1)

            def straight(kind, layer, c):
                for q, wslot, hslot, off, n, _ in straight_parts(kind, layer, c):
                    low(q, wslot, hslot, off, n)

            def blocks(base, first):
                with pool.Fori(0, NB) as j:
                    for i in range(PARTS):
                        low((first + j) * PARTS + (base + i), i // 2, i // 2, (i % 2) * PART, PART)

            def norm(n):
                pool.wait_ge(ms_done, n + 1)
                pool.tensor_tensor(rstd[:], ms[:], half_neg[:, 0:NT], ALU.pow).then_inc(rstd_done, 1)

            for layer in range(DEPTH):
                if layer:
                    for c in range(2):
                        straight("in", layer, c)
                norm(2 * layer)
                for c in range(0 if not layer else 2, IN_CHUNKS):
                    straight("in", layer, c)
                for c in range(OUT_CHUNKS):
                    straight("out", layer, c)
                pool.wait_ge(dms_done, layer + 1)
                pool.tensor_tensor(rstd_d[:], ms_d[:], half_neg[:], ALU.pow).then_inc(drstd_done, 1)
                norm(2 * layer + 1)
                if layer == 0:
                    blocks(FF_BASE[0], 0)
            with pool.Fori(0, N_EXP) as s:
                blocks(FF_BASE[1], s * NB)
            pool.wait_ge(table_ready, 1)
            with pool.Fori(0, MAX_OVER) as o:
                used = pool.value_load(table[0:1, 1, bass.ds(o, 1)], min_val=0, max_val=1)
                with pool.If(used > 0):
                    blocks(FF_BASE[1], (o + N_EXP) * NB)
            norm(4)

        @block.scalar
        def _(act):
            for dst, src in bias_loads(0):
                act.dma_start(dst, src).then_inc(bias_loaded, 16)
            for dst, src in const_loads:
                act.dma_start(dst, src, allow_slow_non_contiguous=True).then_inc(consts_loaded, 16)
            act.dma_start(x[:], x_in[0].rearrange("(t p) n -> p t n", p=P)).then_inc(x_loaded, 16)
            act.dma_start(rw[:], router_w[0].rearrange("(k p) e -> p k e", p=P)).then_inc(late_loaded, 16)
            act.dma_start(fing[:], final_g.partition_broadcast(P)).then_inc(late_loaded, 16)
            act.wait_ge(consts_loaded, CONSTS)
            act.activation(vecrows[0:KD, :], vecrows[0:KD, :], ACT.Silu).then_inc(vec_silu, 1)
            act.wait_ge(arg_ready, 1)
            act.activation(cosF[:, :, 0, :], arg[:, 1], ACT.Sin).then_inc(sin_done, 1)
            act.activation(cosF[:, :, 1, :], arg[:, 1], ACT.Sin).then_inc(sin_done, 1)
            act.activation(sinS[:, :, 1, :], arg[:, 0], ACT.Sin).then_inc(sin_done, 1)
            act.wait_ge(lam_dot, 1)
            act.activation(lame[:], lams[:], ACT.Exp).then_inc(lam_exp, 1)

            def high(q, wslot, hslot, off, n, loaded, freed):
                act.wait_ge(w_loaded[wslot], loaded)
                if not isinstance(freed, int) or freed > 0:
                    act.wait_ge(parts_used, freed)
                act.activation(halves(hslot)[0][:, off:off + n], W[:, wslot, off:off + n],
                               ACT.Copy).then_inc(hi_done, 1)

            def straight(kind, layer, c):
                for q, wslot, hslot, off, n, freed in straight_parts(kind, layer, c):
                    high(q, wslot, hslot, off, n, plan[(kind, layer, c)][2], freed)

            def square(n):
                for t in range(NT):
                    act.activation(xn[:, t, :], x[:, t, :], ACT.Square,
                                   accum_out=ssq[:, t:t + 1]).then_inc(sq_done, 1)

            def split_transposed(n):
                for kk in range(KD // 2):
                    act.wait_ge(tr_copied, 4 * n + kk + 1)
                    act.activation(hTh[:, 2 * kk:2 * kk + 2, :],
                                   tmp[:, kk % 2, :].rearrange("p (k n) -> p k n", k=2),
                                   ACT.Copy).then_inc(tr_hi, 1)

            def gates(layer):
                for i in range(4):
                    act.wait_ge(gates_ps, 4 * layer + i + 1)
                    act.activation(gate[:, i // 2, (i % 2) * 512:(i % 2) * 512 + 512], ps[:, 4 + i, :],
                                   ACT.Copy).then_inc(gates_ready, 1)

            def attention(layer):
                for m in range(0, QK_TILES // 2, 2):
                    act.wait_ge(qkT_ps, 7 * layer + m + 1)
                    act.activation(qkT[:, 2 * m:2 * m + 2, :], ps[:, 2, :].rearrange("p (m n) -> p m n", m=2),
                                   ACT.Copy).then_inc(qkT_even, 1)
                for i in range(UNITS + 1):
                    if i < UNITS:
                        u, par, m = UNITS * layer + i, i % 2, i % 8
                        act.wait_ge(max_done, u + 1)
                        for h in range(2):
                            src = scores[:, par, h, :] if m < 4 else ps[:, 4 + 2 * par + h, 0:SEQ]
                            e = act.activation(E[:, par, h, :], src, ACT.Exp, bias=negm[:, par, h:h + 1],
                                               scale=SCALE, accum_out=sums[:, par, h:h + 1])
                        if m < 4:
                            e = act.activation(sinke[:, par, :], sinkm[:, par, :], ACT.Exp)
                        e.then_inc(exp_done, 1)
                    if i >= 1:
                        u, par, m = UNITS * layer + i - 1, (i - 1) % 2, (i - 1) % 8
                        n = 4 if m < 4 else 2
                        act.wait_ge(pt_ps, u + 1)
                        if i >= 3:
                            act.wait_ge(o_ps, u - 1)
                        act.activation(PT[:, par, 0:n, :], ps[:, 3, 0:n * P].rearrange("p (k n) -> p k n", k=n),
                                       ACT.Copy).then_inc(pt_done, 1)
                for t in range(NT):
                    for h in range(N_DIFF):
                        act.wait_ge(o_done, UNITS * layer + 8 * t + 8)
                        act.activation(tmp[:, t, h * P:h * P + P], xn[:, t, WIN_WIDTH + h * P:WIN_WIDTH + h * P + P],
                                       ACT.Square,
                                       accum_out=ssq_d[:, N_DIFF * t + h:N_DIFF * t + h + 1]).then_inc(dsq_done, 1)

            def blocks(base, first, loads, nu):
                with act.Fori(0, NB) as j:
                    for i in range(PARTS):
                        per = 32 if i < 4 else 16
                        high(None, i // 2, i // 2, (i % 2) * PART, PART,
                             (first + j) * per + (loads[i // 2] + per),
                             (first + j) * PARTS + (base + i - 5))
                    for i in range(nu):
                        par = i % 2
                        if i < nu - 1:
                            act.wait_ge(gu_ps, (first + j) * (nu - 1) + (GU0[nu] + i + 1))
                        else:
                            act.wait_ge(parts_used, (first + j) * PARTS + (base + 4))
                        act.activation(sg[:, par, :], ps[:, 4 + par, 0:HB], ACT.Silu).then_inc(silu_done, 1)
                        act.wait_ge(at_ps, (first + j) * nu + (U0[nu] + i + 1))
                        act.activation(aTh[:, par, :, :], ps[:, 6 + par, 0:2 * P].rearrange("p (k n) -> p k n", k=2),
                                       ACT.Copy).then_inc(at_hi, 1)

            def gathered(n):
                act.wait_ge(gather_ps, n)
                for k in range(KD):
                    a = act.activation(xsT[:, k, :], ps[:, 2 + k // 4, (k % 4) * P:(k % 4) * P + P], ACT.Identity,
                                       bias=modc[:, 1, 3, k:k + 1], scale=A[:, 1, 1, k:k + 1])
                a.then_inc(xs_ready, 1)

            def slot(s):
                act.wait_ge(xs_ready, s + 1)
                act.wait_ge(parts_used, s * (NB * PARTS) + (FF_BASE[1] - 2))
                act.activation(hTh[:, :, 0:P], xsT[:], ACT.Copy).then_inc(slot_hi, 1)
                blocks(FF_BASE[1], s * NB, plan["experts"], 2)
                act.wait_ge(slot_lo, s + 1)
                gathered(s + 2)
                act.wait_ge(pickT_ps, s + 1)
                act.activation(pickT[:], ps[:, 4, 0:NT * P].rearrange("p (t n) -> p t n", t=NT),
                               ACT.Copy).then_inc(pickT_ready, 1)

            for layer in range(DEPTH):
                if layer:
                    for c in range(2):
                        straight("in", layer, c)
                    act.wait_ge(x_ffn, 4)
                gates(layer)
                if not layer:
                    act.wait_ge(x_loaded, 16)
                square(2 * layer)
                split_transposed(3 * layer)
                for c in range(0 if not layer else 2, IN_CHUNKS):
                    straight("in", layer, c)
                for c in range(OUT_CHUNKS):
                    straight("out", layer, c)
                if not layer:
                    act.wait_ge(gates_ps, 4)
                    act.wait_ge(cols_ps, 1)
                    for dst, src in bias_loads(1):
                        act.dma_start(dst, src).then_inc(bias_loaded, 16)
                attention(layer)
                split_transposed(3 * layer + 1)
                act.wait_ge(x_mixed, 4 * layer + 4)
                square(2 * layer + 1)
                split_transposed(3 * layer + 2)
                if not layer:
                    act.wait_ge(parts_used, FF_BASE[0])
                    blocks(FF_BASE[0], 0, plan["dense"], 4)
                else:
                    act.wait_ge(late_loaded, 32)
                    act.activation(rwh[:], rw[:], ACT.Copy).then_inc(rw_hi, 1)
                    act.wait_ge(gap_ready, 1)
                    act.activation(edl[:], dlt[:], ACT.Exp).then_inc(gap_exp, 1)
            act.wait_ge(parts_used, FF_BASE[1])
            gathered(1)
            with act.Fori(0, N_EXP) as s:
                slot(s)
            act.wait_ge(table_ready, 1)
            with act.Fori(0, MAX_OVER) as o:
                used = act.value_load(table[0:1, 1, bass.ds(o, 1)], min_val=0, max_val=1)
                with act.If(used > 0):
                    slot(o + N_EXP)
            act.wait_ge(moe_done, 1)
            square(4)

        @block.vector
        def _(dve):
            step = Count(dve_step)

            def then(instruction):
                dve.wait_ge(dve_step, step.mark(instruction))

            def low(q, wslot, hslot, off, n):
                at = split_views(hslot, off, n, False)
                hi, lo = halves(hslot)
                dve.wait_ge(hi_done, q + 1)
                dve.tensor_tensor(lo[:, at], W[:, wslot, at], hi[:, at].bitcast(F32),
                                  ALU.subtract).then_inc(lo_done, 1)

            def straight(kind, layer, c):
                for q, wslot, hslot, off, n, _ in straight_parts(kind, layer, c):
                    low(q, wslot, hslot, off, n)

            def setup():
                dve.wait_ge(consts_loaded, CONSTS)
                then(dve.tensor_copy(pos_f[:], pos_i[:]))
                for t in range(NT):
                    i = dve.tensor_scalar(ang[:, t, :], inv[:], pos_f[:, t:t + 1], None, ALU.mult)
                then(i)
                for which, quarter in ((0, 0.0), (1, 0.25)):
                    then(dve.tensor_scalar(turns[:], ang[:], 1.0 / (2 * math.pi), quarter, ALU.mult, ALU.add))
                    then(dve.tensor_scalar(turns[:], turns[:], ROUNDER, None, ALU.add))
                    then(dve.tensor_scalar(turns[:], turns[:], -ROUNDER, None, ALU.add))
                    src = ang[:]
                    for part in TWO_PI_PARTS:
                        then(dve.scalar_tensor_tensor(out=arg[:, which], in0=turns[:], scalar=-part, in1=src,
                                                      op0=ALU.mult, op1=ALU.add))
                        src = arg[:, which]
                    then(dve.tensor_scalar(arg[:, which], src, quarter * 2 * math.pi, None, ALU.add))
                    i = dve.tensor_scalar(arg[:, which], src, 3.1415925, -3.1415925, ALU.min, ALU.max)
                    if which:
                        i.then_inc(arg_ready, 1)
                    else:
                        then(i)
                for i in range(2):
                    then(dve.tensor_tensor(lamv[:, 2 * i, :], lamv[:, 2 * i, :], lamv[:, 2 * i + 1, :], ALU.mult))
                    last = dve.reduce_sum(lams[:, i, :], lamv[:, 2 * i, :].rearrange("p (l n) -> p l n", l=DEPTH), AX_X)
                last.then_inc(lam_dot, 1)
                dve.wait_ge(lam_exp, 1)
                then(dve.tensor_tensor(neglam[:], lame[:, 1, :], lame[:, 0, :], ALU.subtract))
                for layer in range(DEPTH):
                    start = 0.8 - 0.6 * math.exp(-0.3 * layer)
                    dve.tensor_scalar(neglam[:, layer:layer + 1], neglam[:, layer:layer + 1], -start, None, ALU.add)
                    dve.tensor_scalar(subgs[:, layer, :], subg[:, layer, :], 1.0 - start, None, ALU.mult)
                dve.tensor_scalar(negsink[:], sinks[:], -1.0, None, ALU.mult)
                dve.wait_ge(sin_done, 3)
                then(dve.tensor_scalar(sinS[:, :, 0, :], sinS[:, :, 1, :], -1.0, None, ALU.mult))

            def columns():
                dve.wait_ge(vec_ps, 1)
                then(dve.tensor_copy(vcols[:], ps[:, 3, 0:40]))
                dve.tensor_copy(c_rep[:], vcols[:, 0:KD].unsqueeze(2).broadcast_to([P, KD, 32])).then_inc(vec_cols, 1)

            def mod_round(layer, r):
                dve.wait_ge(ada_used, ADA_CHUNKS * layer + 4 * r + 4)
                dve.wait_ge(bias_loaded, 64 * (layer + 1))
                dve.tensor_tensor(modrow[:, r, :], ps[:, 2, :], modrow[:, r, :], ALU.add).then_inc(mod_ready, 1)

            def mod_columns(layer):
                dve.wait_ge(cols_ps, layer + 1)
                then(dve.tensor_copy(modc[:, layer], ps[:, 3, 0:6 * KD].rearrange("p (a k) -> p a k", a=6)))
                for f in range(2):
                    g = KD * (1 + 2 * f + layer)
                    i = dve.scalar_tensor_tensor(out=A[:, layer, f, :], in0=modc[:, layer, 3 * f + 1, :], scalar=1.0,
                                                 in1=vcols[:, g:g + KD], op0=ALU.add, op1=ALU.mult)
                i.then_inc(cols_ready, 1)
                dve.wait_ge(cols_ready, layer + 1)

            def normalise(n):
                dve.wait_ge(sq_done, 2 * n + 2)
                dve.tensor_scalar(ms[:], ssq[:], 1.0 / D, EPS, ALU.mult, ALU.add).then_inc(ms_done, 1)
                dve.wait_ge(rstd_done, n + 1)
                if n < 4:
                    for t in range(NT):
                        dve.tensor_scalar(xn[:, t, :], x[:, t, :], rstd[:, t:t + 1], None, ALU.mult).then_inc(xn_done, 1)
                else:
                    for t in range(NT):
                        dve.scalar_tensor_tensor(out=xn[:, t, :], in0=x[:, t, :], scalar=rstd[:, t:t + 1],
                                                 in1=fing[:], op0=ALU.mult, op1=ALU.mult).then_inc(out_ready, 1)

            def split_transposed(n, f):
                for kk in range(KD // 2):
                    dve.wait_ge(tr_ps, 4 * n + kk + 1)
                    if kk >= 2:
                        dve.wait_ge(tr_hi, 4 * n + kk - 1)
                        dve.wait_ge(tr_lo, 4 * n + kk - 1)
                    if f is None:
                        i = dve.tensor_copy(tmp[:, kk % 2, :], ps[:, 2 + kk % 2, :])
                    else:
                        for h in range(2):
                            k = 2 * kk + h
                            i = dve.tensor_scalar(tmp[:, kk % 2, h * SEQ:h * SEQ + SEQ],
                                                  ps[:, 2 + kk % 2, h * SEQ:h * SEQ + SEQ],
                                                  A[:, n // 3, f, k:k + 1], modc[:, n // 3, 3 * f, k:k + 1],
                                                  ALU.mult, ALU.add)
                    i.then_inc(tr_copied, 1)
                    dve.wait_ge(tr_hi, 4 * n + kk + 1)
                    dve.tensor_tensor(hTl[:, 2 * kk:2 * kk + 2, :],
                                      tmp[:, kk % 2, :].rearrange("p (k n) -> p k n", k=2),
                                      hTh[:, 2 * kk:2 * kk + 2, :].bitcast(F32), ALU.subtract).then_inc(tr_lo, 1)

            def rope(layer, c, t):
                if t == 0:
                    dve.wait_ge(proj_ps, IN_CHUNKS * layer + c + 1)
                else:
                    dve.wait_ge(parts_used, IN_BASE[layer] + 2 * c + 2)
                bank = ps[:, (2 * c + t) % 2, :]
                done = 2 * (IN_CHUNKS * layer + c) + t
                if done:
                    dve.wait_ge(rope_done, done)
                last = None
                for col, heads, tile in ROPE_GROUPS[c]:
                    if last is not None:
                        then(last)
                    src = bank[:, col:col + heads * HEAD].rearrange("p (h a n) -> p h a n", h=heads, a=2)
                    a = rope_a[:, 0:heads * HEAD].rearrange("p (h a n) -> p h a n", h=heads, a=2)
                    b = rope_b[:, 0:heads * HEAD].rearrange("p (h a n) -> p h a n", h=heads, a=2)
                    wide = [P, heads, HALF]
                    for s in range(2):
                        dve.tensor_tensor(a[:, :, s, :], src[:, :, s, :],
                                          cosF[:, t, s, :].unsqueeze(1).broadcast_to(wide), ALU.mult)
                        i = dve.tensor_tensor(b[:, :, s, :], src[:, :, 1 - s, :],
                                              sinS[:, t, s, :].unsqueeze(1).broadcast_to(wide), ALU.mult)
                    then(i)
                    last = dve.tensor_tensor(qk[:, t, tile * P:tile * P + heads * HEAD],
                                             rope_a[:, 0:heads * HEAD], rope_b[:, 0:heads * HEAD], ALU.add)
                    if tile == 4:
                        for h in range(2):
                            at = (tile + 1) * P + (1 - h) * HEAD
                            last = dve.tensor_tensor(qk[:, t, at:at + HEAD], rope_a[:, h * HEAD:h * HEAD + HEAD],
                                                     rope_b[:, h * HEAD:h * HEAD + HEAD], ALU.add)
                for col, n, to in V_GROUPS[c]:
                    last = dve.tensor_copy(v[:, t, to:to + n], bank[:, col:col + n])
                last.then_inc(rope_done, 1)

            def maxima(layer, i):
                u, par, m, t = UNITS * layer + i, i % 2, i % 8, i // 8
                dve.wait_ge(s_ps, u + 1)
                raw = ps[:, 4 + 2 * par:6 + 2 * par, 0:SEQ]
                if m < 4:
                    h = N_WIN * layer + 2 * m
                    then(dve.tensor_tensor(scores[:, par], raw, mask[:, t, :].unsqueeze(1).broadcast_to([P, 2, SEQ]),
                                           ALU.add))
                    then(dve.reduce_max(mx[:, par, :], scores[:, par], AX_X))
                    then(dve.scalar_tensor_tensor(out=negm[:, par, :], in0=mx[:, par, :], scalar=-SCALE,
                                                  in1=negsink[:, h:h + 2], op0=ALU.mult, op1=ALU.min))
                    dve.tensor_tensor(sinkm[:, par, :], sinks[:, h:h + 2], negm[:, par, :],
                                      ALU.add).then_inc(max_done, 1)
                else:
                    then(dve.reduce_max(mx[:, par, :], raw, AX_X))
                    dve.tensor_scalar(negm[:, par, :], mx[:, par, :], -SCALE, None, ALU.mult).then_inc(max_done, 1)

            def probabilities(layer, i):
                u, par, m = UNITS * layer + i, i % 2, i % 8
                dve.wait_ge(exp_done, u + 1)
                if u >= 2:
                    dve.wait_ge(o_done, u - 1)
                if m < 4:
                    then(dve.tensor_tensor(den[:, par, :], sums[:, par, :], sinke[:, par, :], ALU.add))
                    dve.reciprocal(rec[:, par, :], den[:, par, :]).then_inc(probs_done, 1)
                else:
                    then(dve.reciprocal(rec[:, par, :], sums[:, par, :]))
                    then(dve.scalar_tensor_tensor(out=nl[:, par:par + 1], in0=sums[:, par, 0:1],
                                                  scalar=rec[:, par, 1:2], in1=neglam[:, layer:layer + 1],
                                                  op0=ALU.mult, op1=ALU.mult))
                    dve.scalar_tensor_tensor(out=E[:, par, 0, :], in0=E[:, par, 1, :], scalar=nl[:, par:par + 1],
                                             in1=E[:, par, 0, :], op0=ALU.mult, op1=ALU.add).then_inc(probs_done, 1)

            def head_out(layer, i):
                u, par, m, t = UNITS * layer + i, i % 2, i % 8, i // 8
                dve.wait_ge(o_ps, u + 1)
                dst = xn[:, t, m * P:m * P + P]
                if m < 4:
                    i = dve.tensor_tensor(dst.rearrange("p (h n) -> p h n", h=2),
                                          ps[:, par, 0:P].rearrange("p (h n) -> p h n", h=2),
                                          rec[:, par, :].unsqueeze(2).broadcast_to([P, 2, HEAD]), ALU.mult)
                else:
                    i = dve.tensor_scalar(dst, ps[:, par, 0:P], rec[:, par, 0:1], None, ALU.mult)
                i.then_inc(o_done, 1)

            def attention(layer):
                for m in range(1, QK_TILES // 2, 2):
                    dve.wait_ge(qkT_ps, 7 * layer + m + 1)
                    dve.tensor_copy(qkT[:, 2 * m:2 * m + 2, :],
                                    ps[:, 3, :].rearrange("p (m n) -> p m n", m=2)).then_inc(qkT_odd, 1)
                for i in range(UNITS + 2):
                    if i < UNITS:
                        maxima(layer, i)
                    if 1 <= i <= UNITS:
                        probabilities(layer, i - 1)
                    if i >= 2:
                        head_out(layer, i - 2)
                    if not layer and i % 4 == 3 and i < 12:
                        mod_round(1, i // 4)
                if not layer:
                    mod_columns(1)
                dve.wait_ge(dsq_done, NT * N_DIFF * (layer + 1))
                dve.tensor_scalar(ms_d[:], ssq_d[:], 1.0 / P, EPS, ALU.mult, ALU.add).then_inc(dms_done, 1)
                dve.wait_ge(drstd_done, layer + 1)
                for t in range(NT):
                    for h in range(N_DIFF):
                        o = xn[:, t, WIN_WIDTH + h * P:WIN_WIDTH + h * P + P]
                        n = N_DIFF * t + h
                        dve.scalar_tensor_tensor(out=o, in0=o, scalar=rstd_d[:, n:n + 1], in1=subgs[:, layer, :],
                                                 op0=ALU.mult, op1=ALU.mult).then_inc(mix_done, 1)

            def mixed(layer):
                for c in range(OUT_CHUNKS):
                    for t in range(NT):
                        if t == 0:
                            dve.wait_ge(wo_ps, OUT_CHUNKS * layer + c + 1)
                        else:
                            dve.wait_ge(parts_used, OUT_BASE[layer] + 2 * c + 2)
                        cols = slice(512 * c, 512 * c + 512)
                        then(dve.tensor_tensor(tmp[:, t, :], ps[:, 4 + 2 * c + t, :], gate[:, 0, cols], ALU.mult))
                        dve.tensor_tensor(x[:, t, cols], x[:, t, cols], tmp[:, t, :], ALU.add).then_inc(x_mixed, 1)

            def blocks(base, first, nu):
                with dve.Fori(0, NB) as j:
                    for i in range(PARTS):
                        low((first + j) * PARTS + (base + i), i // 2, i // 2, (i % 2) * PART, PART)
                    for i in range(nu):
                        par = i % 2
                        dve.wait_ge(silu_done, (first + j) * nu + (U0[nu] + i + 1))
                        dve.tensor_tensor(act_sb[:, par, :], sg[:, par, :], ps[:, 4 + par, HB:2 * HB],
                                          ALU.mult).then_inc(act_done, 1)
                        dve.wait_ge(at_hi, (first + j) * nu + (U0[nu] + i + 1))
                        dve.tensor_tensor(aTl[:, par, :, :],
                                          ps[:, 6 + par, 0:2 * P].rearrange("p (k n) -> p k n", k=2),
                                          aTh[:, par, :, :].bitcast(F32), ALU.subtract).then_inc(at_lo, 1)

            def dense_out():
                dve.wait_ge(parts_used, FF_BASE[0] + NB * PARTS)
                for t in range(NT):
                    for h in range(2):
                        cols = slice(512 * h, 512 * h + 512)
                        then(dve.tensor_tensor(tmp[:, h, :], ps[:, 2 * t + h, :], gate[:, 1, cols], ALU.mult))
                        dve.tensor_tensor(x[:, t, cols], x[:, t, cols], tmp[:, h, :], ALU.add).then_inc(x_ffn, 1)

            def route():
                dve.wait_ge(logit_ps, 1)
                then(dve.tensor_copy(lg[:], ps[:, 4, 0:NT * N_EXP].rearrange("p (t e) -> p t e", t=NT)))
                for t in range(NT):
                    then(dve.max(mv[:, t, :], lg[:, t, :]))
                    then(dve.max_index(mi[:, t, :], mv[:, t, :], lg[:, t, :]))
                then(dve.tensor_copy(mf[:], mi[:]))
                dve.tensor_tensor(dlt[:], mv[:, :, 1], mv[:, :, 0], ALU.subtract).then_inc(gap_ready, 1)
                for t in range(NT):
                    for r in range(2):
                        i = dve.tensor_scalar(oh[:, t, r, :], iota_row[:, 0:N_EXP], mf[:, t, r:r + 1], None,
                                              ALU.is_equal)
                then(i)
                dve.tensor_tensor(chosen[:], oh[:, :, 0, :], oh[:, :, 1, :], ALU.add).then_inc(chosen_ready, 1)
                dve.wait_ge(gap_exp, 1)
                then(dve.tensor_scalar(den2[:], edl[:], 1.0, None, ALU.add))
                then(dve.reciprocal(w12[:, 0, :], den2[:]))
                then(dve.tensor_tensor(w12[:, 1, :], w12[:, 0, :], edl[:], ALU.mult))
                for t in range(NT):
                    then(dve.tensor_scalar(wtmp[:, t, :], oh[:, t, 0, :], w12[:, 0, t:t + 1], None, ALU.mult))
                    then(dve.scalar_tensor_tensor(out=wS[:, t, 0:N_EXP], in0=oh[:, t, 1, :], scalar=w12[:, 1, t:t + 1],
                                                  in1=wtmp[:, t, :], op0=ALU.mult, op1=ALU.add))
                dve.wait_ge(pos_ps, 1)
                for t in range(NT):
                    then(dve.scalar_tensor_tensor(out=wtmp[:, t, :], in0=ps[:, 5, t * N_EXP:t * N_EXP + N_EXP],
                                                  scalar=1.0, in1=chosen[:, t, :], op0=ALU.add, op1=ALU.mult))
                    then(dve.tensor_scalar(posS[:, t, 0:N_EXP], wtmp[:, t, :], -1.0, None, ALU.add))
                then(dve.tensor_scalar(over[:], ps[:, 5, 2 * N_EXP:3 * N_EXP], float(P), None, ALU.is_gt))
                then(dve.memset(rank[:, 0:1], 0.0))
                for e in range(N_EXP):
                    then(dve.tensor_tensor(rank[:, e + 1:e + 2], rank[:, e:e + 1], over[:, e:e + 1], ALU.add))
                then(dve.memset(tabf[:], 0.0))
                for o in range(MAX_OVER):
                    s = N_EXP + o
                    then(dve.scalar_tensor_tensor(out=sel[:, o, :], in0=rank[:, 0:N_EXP], scalar=float(o),
                                                  in1=over[:], op0=ALU.is_equal, op1=ALU.mult))
                    for t in range(NT):
                        dve.tensor_tensor(prod[:, t, :], sel[:, o, :], posS[:, t, 0:N_EXP], ALU.mult)
                        dve.tensor_tensor(prod[:, NT + t, :], sel[:, o, :], wS[:, t, 0:N_EXP], ALU.mult)
                    then(dve.tensor_tensor(prod[:, 4, :], sel[:, o, :], iota_row[:, 0:N_EXP], ALU.mult))
                    dve.reduce_sum(posr[:], prod[:, 0:NT, :], AX_X)
                    dve.reduce_sum(wS[:, :, s], prod[:, NT:2 * NT, :], AX_X)
                    then(dve.reduce_sum(tabf[:, 0, o:o + 1], prod[:, 4, :], AX_X))
                    dve.tensor_scalar(posS[:, :, s], posr[:], -float(P), None, ALU.add)
                    then(dve.tensor_scalar(tabf[:, 1, o:o + 1], rank[:, N_EXP:N_EXP + 1], float(o), None, ALU.is_gt))
                dve.memset(posS[:, :, N_SLOT:], -1.0)
                then(dve.memset(wS[:, :, N_SLOT:], 0.0))
                dve.tensor_copy(table[:], tabf[:]).then_inc(table_ready, 1)

            def picks(dst, s, weighted):
                for t in range(NT):
                    if weighted:
                        i = dve.tensor_scalar(dst[:, t, :], iota_row[:], posS[:, t, bass.ds(s, 1)],
                                              wS[:, t, bass.ds(s, 1)], ALU.is_equal, ALU.mult)
                    else:
                        i = dve.tensor_scalar(dst[:, t, :], iota_row[:], posS[:, t, bass.ds(s, 1)], None, ALU.is_equal)
                return i

            def slot(s):
                dve.wait_ge(gather_ps, s + 1)
                picks(pick, s + 1, False).then_inc(pick_ready, 1)
                dve.wait_ge(slot_hi, s + 1)
                dve.tensor_tensor(hTl[:, :, 0:P], xsT[:], hTh[:, :, 0:P].bitcast(F32),
                                  ALU.subtract).then_inc(slot_lo, 1)
                picks(pickw, s, True).then_inc(pickw_ready, 1)
                blocks(FF_BASE[1], s * NB, 2)
                dve.wait_ge(parts_used, s * (NB * PARTS) + (FF_BASE[1] + NB * PARTS))
                for h in range(2):
                    i = dve.tensor_tensor(ysb[:, 512 * h:512 * h + 512], ps[:, h, :],
                                          gate[:, 1, 512 * h:512 * h + 512], ALU.mult)
                i.then_inc(y_ready, 1)
                for i in range(4):
                    t, cols = i // 2, slice(512 * (i % 2), 512 * (i % 2) + 512)
                    dve.wait_ge(comb_ps, s * 4 + (i + 1))
                    dve.wait_ge(x_added, s * 4 + 4)
                    bank = (6, 7, 0, 1)[i]
                    dve.tensor_tensor(x[:, t, cols], x[:, t, cols], ps[:, bank, :], ALU.add).then_inc(x_added, 1)

            dve.wait_ge(setup_done, SETUP)
            setup()
            columns()
            for layer in range(DEPTH):
                if not layer:
                    for r in range(3):
                        mod_round(0, r)
                    mod_columns(0)
                    dve.wait_ge(x_loaded, 16)
                else:
                    for c in range(2):
                        straight("in", layer, c)
                    dense_out()
                normalise(2 * layer)
                split_transposed(3 * layer, 0)
                if not layer:
                    for c in range(2):
                        straight("in", layer, c)
                for c in range(IN_CHUNKS):
                    for t in range(NT):
                        rope(layer, c, t)
                    if c + 2 < IN_CHUNKS:
                        straight("in", layer, c + 2)
                    else:
                        straight("out", layer, c + 2 - IN_CHUNKS)
                attention(layer)
                split_transposed(3 * layer + 1, None)
                dve.wait_ge(gates_ready, 4 * layer + 4)
                mixed(layer)
                dve.wait_ge(x_mixed, 4 * layer + 4)
                normalise(2 * layer + 1)
                split_transposed(3 * layer + 2, 1)
                if not layer:
                    blocks(FF_BASE[0], 0, 4)
                else:
                    dve.wait_ge(rw_hi, 1)
                    dve.tensor_tensor(rwl[:], rw[:], rwh[:].bitcast(F32), ALU.subtract).then_inc(rw_lo, 1)
                    route()
            picks(pick, 0, False).then_inc(pick_ready, 1)
            dve.memset(done_mark[:], 0.0).then_inc(x_added, 4)
            with dve.Fori(0, N_EXP) as s:
                slot(s)
            dve.wait_ge(table_ready, 1)
            with dve.Fori(0, MAX_OVER) as o:
                used = dve.value_load(table[0:1, 1, bass.ds(o, 1)], min_val=0, max_val=1)
                with dve.If(used > 0):
                    slot(o + N_EXP)
            dve.memset(done_mark[:], 0.0).then_inc(moe_done, 1)
            dve.wait_ge(moe_done, 1)
            dve.wait_ge(late_loaded, 32)
            normalise(4)

        @block.tensor
        def _(pe):
            def ada_chunk(layer, n):
                slot, _, loaded = plan[("ada", layer, n)]
                r, q = n // 4, n % 4
                pe.wait_ge(w_loaded[slot], loaded)
                if q == 0 and r:
                    pe.wait_ge(mod_ready, 3 * layer + r)
                for kk in range(2):
                    k = 2 * q + kk
                    for g in range(4):
                        mm = pe.matmul(ps[32 * g:32 * g + 32, 2, :], c_rep[:, k, :],
                                       W[:, slot, kk * 2048 + g * 512:kk * 2048 + g * 512 + 512],
                                       start=(k == 0), stop=(k == KD - 1))
                mm.then_inc(ada_used, 1)

            def mod_columns(layer):
                pe.wait_ge(mod_ready, 3 * layer + 3)
                for r in range(3):
                    for i in range(4):
                        mm = pe.matmul(ps[:, 3, 16 * r + i:16 * r + i + 13:4], modrow[:, r, i * P:i * P + P],
                                       ident[:, 0:P:32], start=True, stop=True)
                mm.then_inc(cols_ps, 1)

            def gates(layer):
                for i, chunk in enumerate((4, 5, 10, 11)):
                    g, r = chunk % 4, chunk // 4
                    pe.matmul(ps[:, 4 + i, :], ones[32 * g:32 * g + 1, :], modrow[32 * g:32 * g + 1, r, :],
                              start=True, stop=True).then_inc(gates_ps, 1)

            def transpose_all(n):
                for kk in range(KD // 2):
                    if kk >= 2:
                        pe.wait_ge(tr_copied, 4 * n + kk - 1)
                    for h in range(2):
                        for t in range(NT):
                            at = (2 * kk + h) * P
                            mm = pe.transpose(ps[:, 2 + kk % 2, h * SEQ + t * P:h * SEQ + t * P + P],
                                              xn[:, t, at:at + P], ident[:])
                    mm.then_inc(tr_ps, 1)

            def wait_part(q):
                pe.wait_ge(hi_done, q + 1)
                pe.wait_ge(lo_done, q + 1)
                pe.wait_ge(lop_done, q + 1)

            def three(dst, stat_hi, stat_lo, hi, lo, start, stop):
                pe.matmul(dst, stat_hi, hi, start=start, stop=False, skip_group_check=True)
                pe.matmul(dst, stat_hi, lo, start=False, stop=False, skip_group_check=True)
                return pe.matmul(dst, stat_lo, hi, start=False, stop=stop, skip_group_check=True)

            def project(kind, layer, c):
                parts = list(straight_parts(kind, layer, c))
                hslot, n = parts[0][2], parts[0][4] // 4
                hi, lo = (h[:, 0:KD * n].rearrange("p (k n) -> p k n", k=KD) for h in halves(hslot))
                for t in range(NT):
                    if kind == "in":
                        i = 2 * c + t
                        if i >= 2:
                            pe.wait_ge(rope_done, 2 * IN_CHUNKS * layer + i - 1)
                        bank = i % 2
                    else:
                        bank = 4 + 2 * c + t
                    tok = slice(t * P, t * P + P)
                    for k in range(KD):
                        if t == 0 and k % 4 == 0:
                            wait_part(parts[k // 4][0])
                        mm = three(ps[:, bank, 0:n], hTh[:, k, tok], hTl[:, k, tok], hi[:, k, :], lo[:, k, :],
                                   k == 0, k == KD - 1)
                        if t and k % 4 == 3:
                            mm.then_inc(parts_used, 1)
                    if t == 0:
                        mm.then_inc(proj_ps if kind == "in" else wo_ps, 1)

            def attention(layer):
                pe.wait_ge(rope_done, 2 * IN_CHUNKS * (layer + 1))
                for m in range(QK_TILES // 2):
                    if m >= 2:
                        s, per = (qkT_even, 4) if m % 2 == 0 else (qkT_odd, 3)
                        pe.wait_ge(s, per * layer + m // 2)
                    for h in range(2):
                        for t in range(NT):
                            mm = pe.transpose(ps[:, 2 + m % 2, h * SEQ + t * P:h * SEQ + t * P + P],
                                              qk[:, t, (2 * m + h) * P:(2 * m + h) * P + P], ident[:])
                    mm.then_inc(qkT_ps, 1)
                pe.wait_ge(qkT_even, 4 * layer + 4)
                pe.wait_ge(qkT_odd, 3 * layer + 3)
                for i in range(UNITS + 2):
                    if i < UNITS:
                        u, par, m, t = UNITS * layer + i, i % 2, i % 8, i // 8
                        if i >= 2:
                            pe.wait_ge(exp_done, u - 1)
                        for h in range(2):
                            if m < 4:
                                q_tile, k_tile = m, 4 + (m // 2 + h) % 2
                            else:
                                q_tile, k_tile = 2 + m, 6 + m
                            rows = slice(HEAD * h, HEAD * h + HEAD)
                            mm = pe.matmul(ps[:, 4 + 2 * par + h, 0:SEQ], qkT[rows, q_tile, t * P:t * P + P],
                                           qkT[rows, k_tile, :], start=True, stop=True)
                        mm.then_inc(s_ps, 1)
                    if 1 <= i <= UNITS:
                        u, par, m = UNITS * layer + i - 1, (i - 1) % 2, (i - 1) % 8
                        pe.wait_ge(probs_done, u + 1)
                        if i >= 2:
                            pe.wait_ge(pt_done, u)
                        for n in range(4 if m < 4 else 2):
                            mm = pe.transpose(ps[:, 3, n * P:n * P + P],
                                              E[:, par, n // 2, (n % 2) * P:(n % 2) * P + P], ident[:])
                        mm.then_inc(pt_ps, 1)
                    if i >= 2:
                        u, par, m = UNITS * layer + i - 2, i % 2, (i - 2) % 8
                        pe.wait_ge(pt_done, u + 1)
                        if i >= 4:
                            pe.wait_ge(o_done, u - 1)
                        for h in range(2 if m < 4 else 1):
                            width = HEAD if m < 4 else P
                            col = (m // 2) * HEAD if m < 4 else P + (m - 4) * P
                            for kt in range(NT):
                                mm = pe.matmul(ps[:, par, h * width:h * width + width], PT[:, par, 2 * h + kt, :],
                                               v[:, kt, col:col + width], start=(kt == 0), stop=(kt == NT - 1))
                        mm.then_inc(o_ps, 1)
                    if not layer and i < ADA_CHUNKS:
                        if i == 0:
                            pe.wait_ge(cols_ready, 1)
                            pe.wait_ge(bias_loaded, 128)
                        ada_chunk(1, i)
                if not layer:
                    mod_columns(1)

            def gate_up(i, nu, ks, base, b):
                half, t = (i // 2, i % 2) if nu == 4 else (i, 0)
                tok = slice(t * P, t * P + P)
                cols = slice(half * HB, half * HB + HB)
                for k in ks:
                    if i == 0 and k % 2 == 0:
                        wait_part(b * PARTS + (base + k // 2))
                    mm = three(ps[:, 4 + i % 2, :].rearrange("p (g n) -> p g n", g=2), hTh[:, k, tok], hTl[:, k, tok],
                               hg_ff[0][:, k // 4, k % 4, :, cols], hg_ff[1][:, k // 4, k % 4, :, cols],
                               k == 0, k == KD - 1)
                    if i == nu - 1 and k % 2 == 1:
                        mm.then_inc(parts_used, 1)
                    elif i < nu - 1 and k == KD - 1:
                        mm.then_inc(gu_ps, 1)

            def turn(i, nu, b):
                pe.wait_ge(act_done, b * nu + (U0[nu] + i + 1))
                for n in range(2):
                    mm = pe.transpose(ps[:, 6 + i % 2, n * P:n * P + P], act_sb[:, i % 2, n * P:n * P + P], ident[:])
                mm.then_inc(at_ps, 1)

            def down(i, nu, ns, base, b):
                half, t = (i // 2, i % 2) if nu == 4 else (i, 0)
                if 0 in ns:
                    pe.wait_ge(at_hi, b * nu + (U0[nu] + i + 1))
                    pe.wait_ge(at_lo, b * nu + (U0[nu] + i + 1))
                    if i % (nu // 2) == 0:
                        wait_part(b * PARTS + (base + 4 + half))
                for n in ns:
                    k = 2 * half + n
                    for h in range(2):
                        cols = slice(512 * h, 512 * h + 512)
                        mm = three(ps[:, 2 * t + h, :], aTh[:, i % 2, n, :], aTl[:, i % 2, n, :],
                                   hd_ff[0][:, k, cols], hd_ff[1][:, k, cols], False, False)
                if i == nu - 1 or (i == nu - 2 and ns == ((1,) if nu == 2 else (0,))):
                    mm.then_inc(parts_used, 1)

            def blocks(base, first, nu):
                for bank in range(2 * (nu // 2)):
                    pe.matmul(ps[:, bank, :], zeros[:, 0:P], zeros[:], start=True, stop=False, skip_group_check=True)
                with pe.Fori(0, NB) as j:
                    b = first + j
                    gate_up(0, nu, range(KD), base, b)
                    for i in range(1, nu):
                        gate_up(i, nu, range(0, KD // 2), base, b)
                        turn(i - 1, nu, b)
                        gate_up(i, nu, range(KD // 2, KD), base, b)
                        if i < nu - 1:
                            down(i - 1, nu, (0, 1), base, b)
                    down(nu - 2, nu, (0,), base, b)
                    turn(nu - 1, nu, b)
                    down(nu - 2, nu, (1,), base, b)
                    down(nu - 1, nu, (0, 1), base, b)

            def route():
                pe.wait_ge(tr_lo, 4 * 5 + 4)
                pe.wait_ge(rw_lo, 1)
                for t in range(NT):
                    tok = slice(t * P, t * P + P)
                    for k in range(KD):
                        for i, (a, w) in enumerate(((hTh, rwh), (hTh, rwl), (hTl, rwh), (hTl, rwl))):
                            mm = pe.matmul(ps[:, 4, t * N_EXP:t * N_EXP + N_EXP], a[:, k, tok], w[:, k, :],
                                           start=(k == 0 and i == 0), stop=(k == KD - 1 and i == 3))
                mm.then_inc(logit_ps, 1)
                pe.wait_ge(chosen_ready, 1)
                at = [slice(i * N_EXP, i * N_EXP + N_EXP) for i in range(3)]
                pe.matmul(ps[:, 5, at[0]], before[:], chosen[:, 0, :], start=True, stop=True)
                for i, first in ((1, ones), (2, ones)):
                    pe.matmul(ps[:, 5, at[i]], first[:], chosen[:, 0, :], start=True, stop=False)
                    mm = pe.matmul(ps[:, 5, at[i]], (before if i == 1 else ones)[:], chosen[:, 1, :],
                                   start=False, stop=True)
                mm.then_inc(pos_ps, 1)

            def gather(n):
                pe.wait_ge(pick_ready, n)
                for k in range(KD):
                    for t in range(NT):
                        mm = pe.matmul(ps[:, 2 + k // 4, (k % 4) * P:(k % 4) * P + P], xn[:, t, k * P:k * P + P],
                                       pick[:, t, :], start=(t == 0), stop=(t == NT - 1))
                mm.then_inc(gather_ps, 1)

            def slot(s):
                pe.wait_ge(xs_ready, s + 1)
                gather(s + 2)
                pe.wait_ge(x_added, s * 4 + 4)
                pe.wait_ge(slot_lo, s + 1)
                blocks(FF_BASE[1], s * NB, 2)
                pe.wait_ge(pickw_ready, s + 1)
                for t in range(NT):
                    mm = pe.transpose(ps[:, 4, t * P:t * P + P], pickw[:, t, :], ident[:])
                mm.then_inc(pickT_ps, 1)
                pe.wait_ge(pickT_ready, s + 1)
                pe.wait_ge(y_ready, s + 1)
                for i in range(4):
                    cols = slice(512 * (i % 2), 512 * (i % 2) + 512)
                    pe.matmul(ps[:, (6, 7, 0, 1)[i], :], pickT[:, i // 2, :], ysb[:, cols],
                              start=True, stop=True).then_inc(comb_ps, 1)

            pe.wait_ge(setup_done, SETUP)
            pe.wait_ge(vec_silu, 1)
            pe.transpose(ps[:, 3, 0:40], vecrows[:], ident[0:40, 0:40]).then_inc(vec_ps, 1)
            pe.wait_ge(vec_cols, 1)
            for layer in range(DEPTH):
                if not layer:
                    for n in range(ADA_CHUNKS):
                        ada_chunk(0, n)
                if not layer:
                    mod_columns(0)
                gates(layer)
                pe.wait_ge(cols_ready, layer + 1)
                pe.wait_ge(xn_done, 4 * layer + 2)
                transpose_all(3 * layer)
                pe.wait_ge(tr_lo, 4 * (3 * layer) + 4)
                for c in range(IN_CHUNKS):
                    project("in", layer, c)
                attention(layer)
                pe.wait_ge(mix_done, NT * N_DIFF * (layer + 1))
                transpose_all(3 * layer + 1)
                pe.wait_ge(tr_lo, 4 * (3 * layer + 1) + 4)
                for c in range(OUT_CHUNKS):
                    project("out", layer, c)
                pe.wait_ge(xn_done, 4 * layer + 4)
                transpose_all(3 * layer + 2)
                pe.wait_ge(tr_lo, 4 * (3 * layer + 2) + 4)
                if not layer:
                    blocks(FF_BASE[0], 0, 4)
                else:
                    route()
            gather(1)
            with pe.Fori(0, N_EXP) as s:
                slot(s)
            pe.wait_ge(table_ready, 1)
            with pe.Fori(0, MAX_OVER) as o:
                used = pe.value_load(table[0:1, 1, bass.ds(o, 1)], min_val=0, max_val=1)
                with pe.If(used > 0):
                    slot(o + N_EXP)


_INS = ["x", "c", "positions", "inv_freq", "ada_w", "ada_b", "norm_mix_g", "norm_ffn_g", "w_in", "w_out",
        "sink", "lam_q1", "lam_k1", "lam_q2", "lam_k2", "subln_g", "ffn_w_gate", "ffn_w_up", "ffn_w_down",
        "router_w", "moe_w_gate", "moe_w_up", "moe_w_down", "final_g"]


def kernel(**inputs):
    import concourse.bacc as _bacc
    from concourse.bass_utils import run_bass_kernel_spmd as _run

    nc = _bacc.Bacc("TRN2", target_bir_lowering=False, num_devices=1, dynamic_dma_scratch_size=1024)
    freq = 1.0 / (10000.0 ** (np.arange(0, HEAD, 2, dtype=np.float32) / HEAD))
    data = dict(inputs, inv_freq=freq.astype(np.float32).reshape(1, HALF))
    arrays, args = {}, []
    for name in _INS:
        a = np.ascontiguousarray(data[name])
        arrays[f"in_{name}_dram"] = a
        args.append(nc.dram_tensor(f"in_{name}_dram", a.shape, mybir.dt.from_np(a.dtype), kind="ExternalInput").ap())
    out = nc.dram_tensor("out_0_dram", (1, SEQ, D), F32, kind="ExternalOutput").ap()
    build(nc, *args, out)
    r = _run(nc, [arrays], core_ids=[0])
    return r.results[0]["out_0_dram"]
```

```python
import math
from contextlib import ExitStack

import numpy as np

import concourse.bass as bass
from concourse import mybir

ALU = mybir.AluOpType
ACT = mybir.ActivationFunctionType
AX_X = mybir.AxisListType.X
F32 = mybir.dt.float32
F32R = mybir.dt.float32r
I32 = mybir.dt.int32
U32 = mybir.dt.uint32

P = 128
D = 1024
SEQ = 256
DEPTH = 2
NT = SEQ // P
KD = D // P
HEAD = 64
HALF = HEAD // 2
EPS = 1e-6
N_WIN = 8
N_DIFF = 4
WIN_WIDTH = 512
IN_COLS = 2304
D_FF = 3584
BLOCK = 512
NB = D_FF // BLOCK
HB = BLOCK // 2
N_EXP = 8
MAX_OVER = 3
N_SLOT = N_EXP + MAX_OVER
SCALE = HEAD ** -0.5
MASKED = -1e30
ROUNDER = 12582912.0
TWO_PI_PARTS = (6.28125, 0.0019350051879882812, 3.0199159819567e-07)

CH = 4096
PART = CH // 2
PARTS = 6
IN_CHUNKS = 5
OUT_CHUNKS = 2
ADA_CHUNKS = 12
RING = 3
ADA_FIRST = 4
ADA_LATER = [[(0, n) for n in range(ADA_FIRST, ADA_CHUNKS)] + [(1, n) for n in range(ADA_FIRST)],
             [(1, n) for n in range(ADA_FIRST, ADA_CHUNKS)]]
ADA_STEP = [0, 0, 1] + [2 * (i - 2) for i in range(3, ADA_CHUNKS)]

IN_PARTS, OUT_PARTS = 2 * IN_CHUNKS, 2 * OUT_CHUNKS
IN_BASE = [0, IN_PARTS + OUT_PARTS + NB * PARTS]
OUT_BASE = [b + IN_PARTS for b in IN_BASE]
FF_BASE = [b + OUT_PARTS for b in OUT_BASE]

UNITS = 16
ROPE_GROUPS = [[(0, 8, 0)], [(0, 2, 4), (256, 4, 6)], [(0, 8, 8)], [(0, 4, 12)], []]
V_GROUPS = [[], [(128, 128, 0)], [], [(256, 256, 128)], [(0, 256, 384)]]
QK_TILES = 14


class Count:

    def __init__(self, sem):
        self.sem, self.n = sem, 0

    def mark(self, instruction):
        instruction.then_inc(self.sem, 1)
        self.n += 1
        return self.n


def plan_ring():
    loads, holder, plan = [0] * RING, [None] * RING, {}

    def put(name, slot, holds):
        plan[name] = (slot, holder[slot], loads[slot] + 16)
        loads[slot] += 16
        holder[slot] = holds

    def mixer(layer, at):
        for c in range(IN_CHUNKS):
            put(("in", layer, c), (at + c) % RING, ("split", IN_BASE[layer] + 2 * c + 2))
        for c in range(OUT_CHUNKS):
            put(("out", layer, c), (at + IN_CHUNKS + c) % RING, ("split", OUT_BASE[layer] + 2 * c + 2))
        for i, (of, n) in enumerate(ADA_LATER[layer]):
            put(("ada", of, n), (at + IN_CHUNKS + OUT_CHUNKS + i) % RING, ("ada", ADA_CHUNKS * of + n + 1))

    for n in range(ADA_FIRST):
        put(("ada", 0, n), n % RING, ("ada", n + 1))
    mixer(0, ADA_FIRST)
    plan["dense"] = list(loads)
    for c, dmas in enumerate((2, 2, 1)):
        loads[c] += 16 * dmas * NB
        holder[c] = ("split", FF_BASE[0] + PARTS * (NB - 1) + 2 * c + 2)
    mixer(1, 0)
    plan["experts"] = list(loads)
    return plan


def build(nc, x_in, c_in, positions, inv_freq, ada_w, ada_b, mix_g, ffn_g, w_in, w_out, sink,
          lam_q1, lam_k1, lam_q2, lam_k2, subln_g, w_gate, w_up, w_down,
          router_w, moe_gate, moe_up, moe_down, final_g, out):
    plan = plan_ring()
    with ExitStack() as ctx:
        top = [(nc.sbuf_base + 63) // 64 * 64]

        def region(nbytes):
            at = top[0]
            top[0] += (nbytes + 31) // 32 * 32
            return at

        def place(name, shape, dtype, at=None):
            words = int(np.prod(shape[1:]))
            size = words * 4
            return nc.alloc_sbuf_tensor_at(name, shape, dtype, offset=region(size) if at is None else at)

        W = place("weights", [P, RING, CH], F32)
        Hg = place("weights_hi", [P, 2, CH], F32R)
        Lg = place("weights_lo", [P, 2, CH], F32R)
        at = region(2 * CH * 4)
        Hd = place("down_hi", [P, CH], F32R, at)
        Ld = place("down_lo", [P, CH], F32R, at + CH * 4)
        qk = place("qk", [P, NT, QK_TILES * P], F32, at)
        qkT = place("qkT", [P, QK_TILES, SEQ], F32, at + NT * QK_TILES * P * 4)
        x = place("x", [P, NT, D], F32)
        xn = place("xn", [P, NT, D], F32)
        hTh = place("hT_hi", [P, KD, SEQ], F32R)
        hTl = place("hT_lo", [P, KD, SEQ], F32R)
        at = region(3 * 512 * 4)
        modrow = place("modrow", [P, 3, 512], F32, at)
        ysb = place("ysb", [P, D], F32, at)
        gate = place("gate", [P, 2, D], F32)
        fing = place("fing", [P, D], F32)
        at = at_work = region(17 * 1024)
        v = place("v", [P, NT, 640], F32, at)
        scores = place("scores", [P, 2, 2, SEQ], F32, at + 5120)
        rope_a = place("rope_a", [P, 512], F32, at + 5120)
        rope_b = place("rope_b", [P, 512], F32, at + 5120 + 2048)
        E = place("E", [P, 2, 2, SEQ], F32, at + 9216)
        tmp = place("tmp", [P, 2, 512], F32, at + 9216)
        PT = place("PT", [P, 2, 4, P], F32, at + 13312)
        lamv = place("lamv", [P, 4, DEPTH * HEAD], F32, at + 13312)
        subg = place("subg", [P, DEPTH, P], F32, at + 15360)
        vecrows = place("vecrows", [40, P], F32, at + 5120)
        ang = place("ang", [P, NT, HALF], F32, at + 16384)
        turns = place("turns", [P, NT, HALF], F32, at + 16640)
        arg = place("arg", [P, 2, NT, HALF], F32, at + 16896)
        sg = place("sg", [P, 2, HB], F32, at)
        act_sb = place("act", [P, 2, HB], F32, at + 2048)
        aTh = place("actT_hi", [P, 2, 2, P], F32R, at + 4096)
        aTl = place("actT_lo", [P, 2, 2, P], F32R, at + 6144)
        xsT = place("xsT", [P, KD, P], F32, at + 8192)
        pick = place("pick", [P, NT, P], F32, at + 12288)
        pickw = place("pickw", [P, NT, P], F32, at + 13312)
        pickT = place("pickT", [P, NT, P], F32, at + 14336)
        ident = place("ident", [P, P], F32)
        iota_row = place("iota_row", [P, P], F32)
        ones = place("ones", [P, P], F32)
        before = place("before", [P, P], F32)
        mask = place("mask", [P, NT, SEQ], F32)
        vcols = place("vcols", [P, 40], F32)
        c_rep = place("c_rep", [P, KD, 32], F32)
        pos_i = place("pos_i", [P, NT], I32)
        pos_f = place("pos_f", [P, NT], F32)
        inv = place("inv", [P, HALF], F32)
        cosF = place("cosF", [P, NT, 2, HALF], F32)
        sinS = place("sinS", [P, NT, 2, HALF], F32)
        sinks = place("sinks", [P, DEPTH * N_WIN], F32)
        negsink = place("negsink", [P, DEPTH * N_WIN], F32)
        lams = place("lams", [P, 2, DEPTH], F32)
        lame = place("lame", [P, 2, DEPTH], F32)
        neglam = place("neglam", [P, DEPTH], F32)
        subgs = place("subgs", [P, DEPTH, P], F32)
        rw = place("rw", [P, KD, N_EXP], F32)
        rwh = place("rwh", [P, KD, N_EXP], F32R)
        rwl = place("rwl", [P, KD, N_EXP], F32R)
        modc = place("modc", [P, DEPTH, 6, KD], F32)
        A = place("A", [P, DEPTH, 2, KD], F32)
        half_neg = place("half_neg", [P, 8], F32)
        ssq = place("ssq", [P, NT], F32)
        ms = place("ms", [P, NT], F32)
        rstd = place("rstd", [P, NT], F32)
        ssq_d = place("ssq_d", [P, NT * N_DIFF], F32)
        ms_d = place("ms_d", [P, NT * N_DIFF], F32)
        rstd_d = place("rstd_d", [P, NT * N_DIFF], F32)
        mx = place("mx", [P, 4, 2], F32)
        negm = place("negm", [P, 4, 2], F32)
        sinkm = place("sinkm", [P, 4, 2], F32)
        sinke = place("sinke", [P, 4, 2], F32)
        sums = place("sums", [P, 4, 2], F32)
        den = place("den", [P, 4, 2], F32)
        rec = place("rec", [P, 4, 2], F32)
        nl = place("nl", [P, 4], F32)
        lgT = place("lgT", [N_EXP, SEQ], F32, at_work + 5120)
        lg = place("lg", [P, NT, N_EXP], F32)
        mv = place("mv", [P, NT, 8], F32)
        mi = place("mi", [P, NT, 8], U32)
        mf = place("mf", [P, NT, 8], F32)
        oh = place("oh", [P, NT, 2, N_EXP], F32)
        dlt = place("dlt", [P, NT], F32)
        edl = place("edl", [P, NT], F32)
        den2 = place("den2", [P, NT], F32)
        w12 = place("w12", [P, 2, NT], F32)
        chosen = place("chosen", [P, NT, N_EXP], F32)
        wtmp = place("wtmp", [P, NT, N_EXP], F32)
        posS = place("posS", [P, NT, N_SLOT + 1], F32)
        wS = place("wS", [P, NT, N_SLOT + 1], F32)
        over = place("over", [P, N_EXP], F32)
        rank = place("rank", [P, N_EXP + 1], F32)
        sel = place("sel", [P, MAX_OVER, N_EXP], F32)
        prod = place("prod", [P, 5, N_EXP], F32)
        posr = place("posr", [P, NT], F32)
        tabf = place("tabf", [P, 2, 4], F32)
        table = place("table", [P, 2, 4], I32)
        done_mark = place("done_mark", [P, 1], F32)
        assert top[0] <= nc.sbuf_usable_end, top[0]

        ps = ctx.enter_context(nc.psum_tensor("ps", [P, 8, 512], F32))

        def sem(name):
            return ctx.enter_context(nc.semaphore(name))

        w_loaded = [sem(f"w_loaded{i}") for i in range(RING)]
        rows_loaded, x_loaded, consts_loaded, late_loaded = sem("rows_loaded"), sem("x_loaded"), sem("consts_loaded"), sem("late_loaded")
        bias_loaded, table_ready = sem("bias_loaded"), sem("table_ready")
        setup_done, vec_silu, vec_ps, vec_cols = sem("setup_done"), sem("vec_silu"), sem("vec_ps"), sem("vec_cols")
        arg_ready, sin_done, lam_dot, lam_exp = sem("arg_ready"), sem("sin_done"), sem("lam_dot"), sem("lam_exp")
        tables_done = sem("tables_done")
        hi_done, lo_done, lop_done, parts_used = sem("hi_done"), sem("lo_done"), sem("lop_done"), sem("parts_used")
        ada_used, mod_ready, cols_ps, cols_ready = sem("ada_used"), sem("mod_ready"), sem("cols_ps"), sem("cols_ready")
        gates_ps, gates_ready = sem("gates_ps"), sem("gates_ready")
        sq_done, ms_done, rstd_done, xn_done = sem("sq_done"), sem("ms_done"), sem("rstd_done"), sem("xn_done")
        tr_ps, tr_copied, tr_hi, tr_lo = sem("tr_ps"), sem("tr_copied"), sem("tr_hi"), sem("tr_lo")
        proj_ps, rope_done = sem("proj_ps"), sem("rope_done")
        qkT_ps, qkT_even, qkT_odd = sem("qkT_ps"), sem("qkT_even"), sem("qkT_odd")
        s_ps, max_done, exp_done, probs_done = sem("s_ps"), sem("max_done"), sem("exp_done"), sem("probs_done")
        pt_ps, pt_done, o_ps, o_done = sem("pt_ps"), sem("pt_done"), sem("o_ps"), sem("o_done")
        dsq_done, dms_done, drstd_done, mix_done = sem("dsq_done"), sem("dms_done"), sem("drstd_done"), sem("mix_done")
        wo_ps, x_mixed = sem("wo_ps"), sem("x_mixed")
        gu_ps, silu_done, act_done = sem("gu_ps"), sem("silu_done"), sem("act_done")
        at_ps, at_hi, at_lo = sem("at_ps"), sem("at_hi"), sem("at_lo")
        x_ffn = sem("x_ffn")
        rw_hi, rw_lo, logit_ps, logits_copied = (
            sem("rw_hi"), sem("rw_lo"), sem("logit_ps"), sem("logits_copied"))
        gap_ready, gap_exp, chosen_ready, pos_ps, routed = (
            sem("gap_ready"), sem("gap_exp"), sem("chosen_ready"), sem("pos_ps"), sem("routed"))
        pick_ready, gather_ps, xs_ready = sem("pick_ready"), sem("gather_ps"), sem("xs_ready")
        slot_hi, slot_lo, pickw_ready = sem("slot_hi"), sem("slot_lo"), sem("pickw_ready")
        pickT_ps, pickT_ready, y_ready = sem("pickT_ps"), sem("pickT_ready"), sem("y_ready")
        comb_ps, x_added, moe_done = sem("comb_ps"), sem("x_added"), sem("moe_done")
        dve_step, out_ready, out_written = sem("dve_step"), sem("out_ready"), sem("out_written")

        def bias_loads(layer, rounds):
            src = ada_b[layer].rearrange("(r g n) -> g r n", r=3, g=4)
            return [(modrow[32 * g:32 * g + 32, rounds, :], src[g][rounds].partition_broadcast(32))
                    for g in range(4)]

        row_loads = [
            (vecrows[0:KD, :], c_in[0].rearrange("(k p) -> k p", p=P)),
            (vecrows[KD:3 * KD, :], mix_g.rearrange("l (k p) -> (l k) p", p=P)),
            (vecrows[3 * KD:5 * KD, :], ffn_g.rearrange("l (k p) -> (l k) p", p=P)),
        ]
        const_loads = [
            (pos_i[:], positions[0].rearrange("(t p) -> p t", p=P)),
            (inv[:], inv_freq[0].partition_broadcast(P)),
            (sinks[:], sink.rearrange("l h -> (l h)").partition_broadcast(P)),
            (subg[:], subln_g.rearrange("l n -> (l n)").partition_broadcast(P)),
        ] + [(lamv[:, i, :], lam.rearrange("l n -> (l n)").partition_broadcast(P))
             for i, lam in enumerate((lam_q1, lam_k1, lam_q2, lam_k2))]
        CONSTS = 16 * len(const_loads)
        SETUP = 9

        ada_v = ada_w.rearrange("l (q k p) (r n) -> l r q p k n", k=2, p=P, r=3)
        in_v = w_in.rearrange("l (k p) n -> l p k n", p=P)
        out_v = w_out.rearrange("l (k p) n -> l p k n", p=P)

        def ff_views(g, u, d):
            return (g.rearrange("e (k p) (j n) -> e j p k n", p=P, n=BLOCK),
                    u.rearrange("e (k p) (j n) -> e j p k n", p=P, n=BLOCK),
                    d.rearrange("e (j k p) n -> e j p k n", p=P, k=BLOCK // P))

        dense_v, moe_v = ff_views(w_gate, w_up, w_down), ff_views(moe_gate[0], moe_up[0], moe_down[0])

        hg_ff = [t[:].rearrange("p c (k g n) -> p c k g n", k=4, g=2) for t in (Hg, Lg)]
        hd_ff = [t[:].rearrange("p (k n) -> p k n", n=D) for t in (Hd, Ld)]

        def split_views(hslot, off, n, pool):
            a, b = (off + n * 3 // 4, off + n) if pool else (off, off + n * 3 // 4)
            return slice(a, b)

        def halves(hslot):
            return (Hg[:, hslot, :], Lg[:, hslot, :]) if hslot < 2 else (Hd[:], Ld[:])

        def straight_parts(kind, layer, c):
            base = IN_BASE[layer] + 2 * c + (IN_PARTS if kind == "out" else 0)
            n = PART if kind == "out" or c < IN_CHUNKS - 1 else PART // 2
            i = c + (IN_CHUNKS if kind == "out" else 0)
            for h in range(2):
                if kind == "out" and c == 1:
                    freed = base - 2
                elif i >= 2:
                    freed = base + h - 3
                elif layer:
                    freed = FF_BASE[0] + PARTS * (NB - 1) + 2 * i + h + 1
                else:
                    freed = 0
                yield base + h, plan[(kind, layer, c)][0], i % 2, h * n, n, freed

        block = ctx.enter_context(nc.Block())

        NEW_KINDS = [[(0, (0, 2))], [(0, (2, 6)), (1, (0, 2))], [(1, (2, 6))]]

        GU0 = {4: 0, 2: 3 * NB}
        U0 = {4: 0, 2: 4 * NB}

        @block.sync
        def _(sp):
            def free(holder):
                if holder is None:
                    return
                what, value = holder
                if what == "ada":
                    sp.wait_ge(ada_used, value)
                else:
                    sp.wait_ge(hi_done, value)
                    sp.wait_ge(lo_done, value)
                    sp.wait_ge(lop_done, value)

            def load(name, dst, src):
                slot, holder, _ = plan[name]
                free(holder)
                sp.dma_start(dst, src).then_inc(w_loaded[slot], 16)

            def ada(chunks):
                for layer, n in chunks:
                    slot = plan[("ada", layer, n)][0]
                    load(("ada", layer, n), W[:, slot, :].rearrange("p (k n) -> p k n", k=2),
                         ada_v[layer, n // 4, n % 4])

            def mixer(layer):
                for c in range(IN_CHUNKS):
                    n = 512 if c < IN_CHUNKS - 1 else 256
                    slot = plan[("in", layer, c)][0]
                    load(("in", layer, c), W[:, slot, 0:KD * n].rearrange("p (k n) -> p k n", k=KD),
                         in_v[layer, :, :, 512 * c:512 * c + n])
                for c in range(OUT_CHUNKS):
                    slot = plan[("out", layer, c)][0]
                    load(("out", layer, c), W[:, slot, :].rearrange("p (k n) -> p k n", k=KD),
                         out_v[layer, :, :, 512 * c:512 * c + 512])

            def blocks(views, e, base, first):
                gate_v, up_v, down_v = views
                with sp.Fori(0, NB) as j:
                    for c in range(2):
                        value = (first + j) * PARTS + (base - PARTS + 2 * c + 2)
                        sp.wait_ge(hi_done, value)
                        sp.wait_ge(lo_done, value)
                        sp.wait_ge(lop_done, value)
                        dst = W[:, c, :].rearrange("p (k g n) -> p k g n", k=4, g=2)
                        for g, view in enumerate((gate_v, up_v)):
                            src = view[bass.ds(e, 1), bass.ds(j, 1), :, 4 * c:4 * c + 4, :]
                            sp.dma_start(dst[:, :, g, :], src.rearrange("a b p k n -> p (a b k) n")).then_inc(
                                w_loaded[c], 16)
                    value = (first + j) * PARTS + base
                    sp.wait_ge(hi_done, value)
                    sp.wait_ge(lo_done, value)
                    sp.wait_ge(lop_done, value)
                    src = down_v[bass.ds(e, 1), bass.ds(j, 1), :, :, :]
                    sp.dma_start(W[:, 2, :].rearrange("p (k n) -> p k n", n=D),
                                 src.rearrange("a b p k n -> p (a b k) n")).then_inc(w_loaded[2], 16)

            ada([(0, n) for n in range(ADA_FIRST)])
            mixer(0)
            ada(ADA_LATER[0])
            sp.wait_ge(ada_used, ADA_CHUNKS + ADA_FIRST)
            blocks(dense_v, 0, FF_BASE[0], 0)
            mixer(1)
            ada(ADA_LATER[1])
            sp.wait_ge(ada_used, 2 * ADA_CHUNKS)
            with sp.Fori(0, N_EXP) as s:
                blocks(moe_v, s, FF_BASE[1], s * NB)
            sp.wait_ge(table_ready, 1)
            with sp.Fori(0, MAX_OVER) as o:
                used = sp.value_load(table[0:1, 1, bass.ds(o, 1)], min_val=0, max_val=1)
                with sp.If(used > 0):
                    e = sp.value_load(table[0:1, 0, bass.ds(o, 1)], min_val=0, max_val=N_EXP - 1)
                    blocks(moe_v, e, FF_BASE[1], (o + N_EXP) * NB)
            sp.wait_ge(out_ready, NT)
            sp.dma_start(out[0].rearrange("(t p) n -> p t n", p=P), xn[:]).then_inc(out_written, 16)
            sp.wait_ge(out_written, 16)

        @block.gpsimd
        def _(pool):
            pool.memset(ident[:], 0.0).then_inc(setup_done, 1)
            pool.memset(mask[:], 0.0).then_inc(setup_done, 1)
            pool.memset(ones[:], 1.0).then_inc(setup_done, 1)
            pool.memset(half_neg[:], -0.5).then_inc(setup_done, 1)
            pool.wait_ge(setup_done, 4)
            pool.affine_select(out=ident[:], in_=ident[:], compare_op=ALU.not_equal, fill=1.0, base=0,
                               pattern=[[-1, P]], channel_multiplier=1).then_inc(setup_done, 1)
            pool.affine_select(out=before[:], in_=ones[:], compare_op=ALU.is_gt, fill=0.0, base=0,
                               pattern=[[1, P]], channel_multiplier=-1).then_inc(setup_done, 1)
            pool.affine_select(out=mask[:, 0, P:], in_=mask[:, 0, P:], compare_op=ALU.is_ge, fill=MASKED,
                               base=0, pattern=[[-1, P]], channel_multiplier=1).then_inc(setup_done, 1)
            pool.affine_select(out=mask[:, 1, :P], in_=mask[:, 1, :P], compare_op=ALU.is_ge, fill=MASKED,
                               base=0, pattern=[[1, P]], channel_multiplier=-1).then_inc(setup_done, 1)
            pool.iota(iota_row[:], pattern=[[1, P]], base=0, channel_multiplier=0,
                      allow_small_or_imprecise_dtypes=True).then_inc(setup_done, 1)

            def low(q, wslot, hslot, off, n):
                at = split_views(hslot, off, n, True)
                hi, lo = halves(hslot)
                pool.wait_ge(hi_done, q + 1)
                pool.tensor_tensor(lo[:, at], W[:, wslot, at], hi[:, at].bitcast(F32),
                                   ALU.subtract).then_inc(lop_done, 1)

            def straight(kind, layer, c):
                for q, wslot, hslot, off, n, _ in straight_parts(kind, layer, c):
                    low(q, wslot, hslot, off, n)

            def blocks(base, first):
                with pool.Fori(0, NB) as j:
                    for i in range(PARTS):
                        low((first + j) * PARTS + (base + i), i // 2, i // 2, (i % 2) * PART, PART)

            def norm(n):
                pool.wait_ge(ms_done, n + 1)
                pool.tensor_tensor(rstd[:], ms[:], half_neg[:, 0:NT], ALU.pow).then_inc(rstd_done, 1)

            for layer in range(DEPTH):
                if layer:
                    for c in range(2):
                        straight("in", layer, c)
                norm(2 * layer)
                for c in range(0 if not layer else 2, IN_CHUNKS):
                    straight("in", layer, c)
                for c in range(OUT_CHUNKS):
                    straight("out", layer, c)
                pool.wait_ge(dms_done, layer + 1)
                pool.tensor_tensor(rstd_d[:], ms_d[:], half_neg[:], ALU.pow).then_inc(drstd_done, 1)
                norm(2 * layer + 1)
                if layer == 0:
                    blocks(FF_BASE[0], 0)
            with pool.Fori(0, N_EXP) as s:
                blocks(FF_BASE[1], s * NB)
            pool.wait_ge(table_ready, 1)
            with pool.Fori(0, MAX_OVER) as o:
                used = pool.value_load(table[0:1, 1, bass.ds(o, 1)], min_val=0, max_val=1)
                with pool.If(used > 0):
                    blocks(FF_BASE[1], (o + N_EXP) * NB)
            norm(4)

        @block.scalar
        def _(act):
            for dst, src in row_loads:
                act.dma_start(dst, src).then_inc(rows_loaded, 16)
            for t in range(NT):
                act.dma_start(x[:, t, :], x_in[0, t * P:t * P + P, :]).then_inc(x_loaded, 16)
            for dst, src in bias_loads(0, slice(0, 3)):
                act.dma_start(dst, src).then_inc(bias_loaded, 16)
            for dst, src in const_loads:
                act.dma_start(dst, src, allow_slow_non_contiguous=True).then_inc(consts_loaded, 16)
            act.dma_start(rw[:], router_w[0].rearrange("(k p) e -> p k e", p=P)).then_inc(late_loaded, 16)
            act.dma_start(fing[:], final_g.partition_broadcast(P)).then_inc(late_loaded, 16)
            act.wait_ge(rows_loaded, 16 * len(row_loads))
            act.activation(vecrows[0:KD, :], vecrows[0:KD, :], ACT.Silu).then_inc(vec_silu, 1)
            act.wait_ge(x_loaded, 16 * NT)
            for t in range(NT):
                act.activation(xn[:, t, :], x[:, t, :], ACT.Square, accum_out=ssq[:, t:t + 1]).then_inc(sq_done, 1)
            act.wait_ge(arg_ready, 1)
            act.activation(cosF[:, :, 0, :], arg[:, 1], ACT.Sin).then_inc(sin_done, 1)
            act.activation(cosF[:, :, 1, :], arg[:, 1], ACT.Sin).then_inc(sin_done, 1)
            act.activation(sinS[:, :, 1, :], arg[:, 0], ACT.Sin).then_inc(sin_done, 1)
            act.wait_ge(lam_dot, 1)
            act.activation(lame[:], lams[:], ACT.Exp).then_inc(lam_exp, 1)

            def high(q, wslot, hslot, off, n, loaded, freed):
                act.wait_ge(w_loaded[wslot], loaded)
                if not isinstance(freed, int) or freed > 0:
                    act.wait_ge(parts_used, freed)
                act.activation(halves(hslot)[0][:, off:off + n], W[:, wslot, off:off + n],
                               ACT.Copy).then_inc(hi_done, 1)

            def straight(kind, layer, c):
                for q, wslot, hslot, off, n, freed in straight_parts(kind, layer, c):
                    high(q, wslot, hslot, off, n, plan[(kind, layer, c)][2], freed)

            def square(n):
                for t in range(NT):
                    act.activation(xn[:, t, :], x[:, t, :], ACT.Square,
                                   accum_out=ssq[:, t:t + 1]).then_inc(sq_done, 1)

            def split_transposed(n):
                for kk in range(KD // 2):
                    act.wait_ge(tr_copied, 4 * n + kk + 1)
                    act.activation(hTh[:, 2 * kk:2 * kk + 2, :],
                                   tmp[:, kk % 2, :].rearrange("p (k n) -> p k n", k=2),
                                   ACT.Copy).then_inc(tr_hi, 1)

            def gates(layer):
                for i in range(4):
                    act.wait_ge(gates_ps, 4 * layer + i + 1)
                    act.activation(gate[:, i // 2, (i % 2) * 512:(i % 2) * 512 + 512], ps[:, 4 + i, :],
                                   ACT.Copy).then_inc(gates_ready, 1)

            def attention(layer):
                for m in range(0, QK_TILES // 2, 2):
                    act.wait_ge(qkT_ps, 7 * layer + m + 1)
                    act.activation(qkT[:, 2 * m:2 * m + 2, :], ps[:, 2, :].rearrange("p (m n) -> p m n", m=2),
                                   ACT.Copy).then_inc(qkT_even, 1)
                for i in range(UNITS + 2):
                    if i < UNITS:
                        u, par, q, m = UNITS * layer + i, i % 2, i % 4, i % 8
                        act.wait_ge(max_done, u + 1)
                        if i >= 2:
                            act.wait_ge(pt_ps, u - 1)
                        for h in range(2):
                            src = scores[:, par, h, :] if m < 4 else ps[:, 4 + 2 * par + h, 0:SEQ]
                            e = act.activation(E[:, par, h, :], src, ACT.Exp, bias=negm[:, q, h:h + 1],
                                               scale=SCALE, accum_out=sums[:, q, h:h + 1])
                        if m < 4:
                            e = act.activation(sinke[:, q, :], sinkm[:, q, :], ACT.Exp)
                        e.then_inc(exp_done, 1)
                    if i >= 2:
                        u, par, m = UNITS * layer + i - 2, i % 2, (i - 2) % 8
                        n = 4 if m < 4 else 2
                        act.wait_ge(pt_ps, u + 1)
                        if i >= 4:
                            act.wait_ge(o_ps, u - 1)
                        act.activation(PT[:, par, 0:n, :], ps[:, 3, 0:n * P].rearrange("p (k n) -> p k n", k=n),
                                       ACT.Copy).then_inc(pt_done, 1)
                for t in range(NT):
                    for h in range(N_DIFF):
                        act.wait_ge(o_done, UNITS * layer + 8 * t + 8)
                        act.activation(tmp[:, t, h * P:h * P + P], xn[:, t, WIN_WIDTH + h * P:WIN_WIDTH + h * P + P],
                                       ACT.Square,
                                       accum_out=ssq_d[:, N_DIFF * t + h:N_DIFF * t + h + 1]).then_inc(dsq_done, 1)

            def blocks(base, first, loads, nu, ahead=None, last=None):
                def part(b, i):
                    per = 32 if i < 4 else 16
                    high(None, i // 2, i // 2, (i % 2) * PART, PART,
                         b * per + (loads[i // 2] + per), b * PARTS + (base + i - 5))

                def silu(b, i):
                    if i < nu - 1:
                        act.wait_ge(gu_ps, b * (nu - 1) + (GU0[nu] + i + 1))
                    else:
                        act.wait_ge(parts_used, b * PARTS + (base + 4))
                    act.activation(sg[:, i % 2, :], ps[:, 4 + i % 2, 0:HB], ACT.Silu).then_inc(silu_done, 1)

                def turned(b, i):
                    act.wait_ge(at_ps, b * nu + (U0[nu] + i + 1))
                    act.activation(aTh[:, i % 2, :, :],
                                   ps[:, 6 + i % 2, 0:2 * P].rearrange("p (k n) -> p k n", k=2),
                                   ACT.Copy).then_inc(at_hi, 1)

                def one(b, is_first, is_last):
                    if is_first:
                        for i in range(4):
                            part(b, i)
                        silu(b, 0)
                        part(b, 4)
                    else:
                        part(b, 4)
                        part(b, 5)
                        if is_last and ahead:
                            ahead()
                        silu(b, 0)
                    for i in range(1, nu - 1):
                        turned(b, i - 1)
                        silu(b, i)
                    if is_first:
                        turned(b, nu - 2)
                        part(b, 5)
                        part(b + 1, 0)
                    elif is_last:
                        turned(b, nu - 2)
                    else:
                        part(b + 1, 0)
                        turned(b, nu - 2)
                    if not is_last:
                        part(b + 1, 1)
                    silu(b, nu - 1)
                    if not is_last:
                        part(b + 1, 2)
                    elif last:
                        last()
                    turned(b, nu - 1)
                    if not is_last:
                        part(b + 1, 3)

                one(first + 0, True, False)
                with act.Fori(0, NB - 2) as j:
                    one(first + (j + 1), False, False)
                one(first + (NB - 1), False, True)

            def gathered(n):
                act.wait_ge(gather_ps, n)
                for k in range(KD):
                    a = act.activation(xsT[:, k, :], ps[:, 2 + k // 4, (k % 4) * P:(k % 4) * P + P], ACT.Identity,
                                       bias=modc[:, 1, 3, k:k + 1], scale=A[:, 1, 1, k:k + 1])
                a.then_inc(xs_ready, 1)
                act.wait_ge(xs_ready, n)

            def input_high():
                act.activation(hTh[:, :, 0:P], xsT[:], ACT.Copy).then_inc(slot_hi, 1)

            def slot(s):
                def turned_rows():
                    act.wait_ge(pickT_ps, s + 1)
                    act.activation(pickT[:], ps[:, 2, 0:NT * P].rearrange("p (t n) -> p t n", t=NT),
                                   ACT.Copy).then_inc(pickT_ready, 1)
                    act.wait_ge(slot_lo, s + 1)

                def next_input():
                    gathered(s + 2)
                    input_high()

                blocks(FF_BASE[1], s * NB, plan["experts"], 2, turned_rows, next_input)

            for layer in range(DEPTH):
                if layer:
                    for c in range(2):
                        straight("in", layer, c)
                    act.wait_ge(x_ffn, 4)
                    square(2 * layer)
                split_transposed(3 * layer)
                for c in range(0 if not layer else 2, IN_CHUNKS):
                    straight("in", layer, c)
                for c in range(OUT_CHUNKS):
                    straight("out", layer, c)
                if not layer:
                    act.wait_ge(cols_ps, 1)
                    for dst, src in bias_loads(1, slice(0, 1)):
                        act.dma_start(dst, src).then_inc(bias_loaded, 16)
                attention(layer)
                gates(layer)
                if not layer:
                    act.wait_ge(cols_ps, 2)
                    for dst, src in bias_loads(1, slice(1, 3)):
                        act.dma_start(dst, src).then_inc(bias_loaded, 16)
                split_transposed(3 * layer + 1)
                act.wait_ge(x_mixed, 4 * layer + 4)
                square(2 * layer + 1)
                split_transposed(3 * layer + 2)
                if not layer:
                    act.wait_ge(parts_used, FF_BASE[0])
                    blocks(FF_BASE[0], 0, plan["dense"], 4)
                else:
                    act.wait_ge(late_loaded, 32)
                    act.activation(rwh[:], rw[:], ACT.Copy).then_inc(rw_hi, 1)
                    act.wait_ge(gap_ready, 1)
                    act.activation(edl[:], dlt[:], ACT.Exp).then_inc(gap_exp, 1)
            act.wait_ge(parts_used, FF_BASE[1])
            gathered(1)
            input_high()
            slot(0)
            with act.Fori(0, N_EXP - 1) as s:
                slot(s + 1)
            act.wait_ge(table_ready, 1)
            with act.Fori(0, MAX_OVER) as o:
                used = act.value_load(table[0:1, 1, bass.ds(o, 1)], min_val=0, max_val=1)
                with act.If(used > 0):
                    slot(o + N_EXP)
            act.wait_ge(moe_done, 1)
            square(4)

        @block.vector
        def _(dve):
            step = Count(dve_step)

            def then(instruction):
                dve.wait_ge(dve_step, step.mark(instruction))

            def low(q, wslot, hslot, off, n):
                at = split_views(hslot, off, n, False)
                hi, lo = halves(hslot)
                dve.wait_ge(hi_done, q + 1)
                dve.tensor_tensor(lo[:, at], W[:, wslot, at], hi[:, at].bitcast(F32),
                                  ALU.subtract).then_inc(lo_done, 1)

            def straight(kind, layer, c):
                for q, wslot, hslot, off, n, _ in straight_parts(kind, layer, c):
                    low(q, wslot, hslot, off, n)

            def setup():
                dve.wait_ge(consts_loaded, CONSTS)
                then(dve.tensor_copy(pos_f[:], pos_i[:]))
                for t in range(NT):
                    i = dve.tensor_scalar(ang[:, t, :], inv[:], pos_f[:, t:t + 1], None, ALU.mult)
                then(i)
                for which, quarter in ((0, 0.0), (1, 0.25)):
                    then(dve.tensor_scalar(turns[:], ang[:], 1.0 / (2 * math.pi), quarter, ALU.mult, ALU.add))
                    then(dve.tensor_scalar(turns[:], turns[:], ROUNDER, None, ALU.add))
                    then(dve.tensor_scalar(turns[:], turns[:], -ROUNDER, None, ALU.add))
                    src = ang[:]
                    for part in TWO_PI_PARTS:
                        then(dve.scalar_tensor_tensor(out=arg[:, which], in0=turns[:], scalar=-part, in1=src,
                                                      op0=ALU.mult, op1=ALU.add))
                        src = arg[:, which]
                    then(dve.tensor_scalar(arg[:, which], src, quarter * 2 * math.pi, None, ALU.add))
                    i = dve.tensor_scalar(arg[:, which], src, 3.1415925, -3.1415925, ALU.min, ALU.max)
                    if which:
                        i.then_inc(arg_ready, 1)
                    else:
                        then(i)
                for i in range(2):
                    then(dve.tensor_tensor(lamv[:, 2 * i, :], lamv[:, 2 * i, :], lamv[:, 2 * i + 1, :], ALU.mult))
                    last = dve.reduce_sum(lams[:, i, :], lamv[:, 2 * i, :].rearrange("p (l n) -> p l n", l=DEPTH), AX_X)
                last.then_inc(lam_dot, 1)
                dve.wait_ge(lam_exp, 1)
                then(dve.tensor_tensor(neglam[:], lame[:, 1, :], lame[:, 0, :], ALU.subtract))
                for layer in range(DEPTH):
                    start = 0.8 - 0.6 * math.exp(-0.3 * layer)
                    dve.tensor_scalar(neglam[:, layer:layer + 1], neglam[:, layer:layer + 1], -start, None, ALU.add)
                    dve.tensor_scalar(subgs[:, layer, :], subg[:, layer, :], 1.0 - start, None, ALU.mult)
                dve.tensor_scalar(negsink[:], sinks[:], -1.0, None, ALU.mult)
                dve.wait_ge(sin_done, 3)
                then(dve.tensor_scalar(sinS[:, :, 0, :], sinS[:, :, 1, :], -1.0, None, ALU.mult))

            def columns():
                dve.wait_ge(vec_ps, 1)
                then(dve.tensor_copy(vcols[:], ps[:, 3, 0:40]))
                dve.tensor_copy(c_rep[:], vcols[:, 0:KD].unsqueeze(2).broadcast_to([P, KD, 32])).then_inc(vec_cols, 1)

            def mod_round(layer, r):
                dve.wait_ge(ada_used, ADA_CHUNKS * layer + 4 * r + 4)
                dve.wait_ge(bias_loaded, 64 * (1 + layer + (1 if layer and r else 0)))
                dve.tensor_tensor(modrow[:, r, :], ps[:, 2, :], modrow[:, r, :], ALU.add).then_inc(mod_ready, 1)

            def mod_columns(n):
                dve.wait_ge(cols_ps, n + 1)
                for layer, (a, b) in NEW_KINDS[n]:
                    i = dve.tensor_copy(modc[:, layer, a:b], ps[:, 3, KD * a:KD * b].rearrange(
                        "p (a k) -> p a k", a=b - a))
                then(i)
                for layer, (a, b) in NEW_KINDS[n]:
                    f = 0 if a == 0 else 1
                    g = KD * (1 + 2 * f + layer)
                    i = dve.scalar_tensor_tensor(out=A[:, layer, f, :], in0=modc[:, layer, 3 * f + 1, :], scalar=1.0,
                                                 in1=vcols[:, g:g + KD], op0=ALU.add, op1=ALU.mult)
                i.then_inc(cols_ready, 1)
                dve.wait_ge(cols_ready, n + 1)

            def normalise(n):
                dve.wait_ge(sq_done, 2 * n + 2)
                dve.tensor_scalar(ms[:], ssq[:], 1.0 / D, EPS, ALU.mult, ALU.add).then_inc(ms_done, 1)
                dve.wait_ge(rstd_done, n + 1)
                if n < 4:
                    for t in range(NT):
                        dve.tensor_scalar(xn[:, t, :], x[:, t, :], rstd[:, t:t + 1], None, ALU.mult).then_inc(xn_done, 1)
                else:
                    for t in range(NT):
                        dve.scalar_tensor_tensor(out=xn[:, t, :], in0=x[:, t, :], scalar=rstd[:, t:t + 1],
                                                 in1=fing[:], op0=ALU.mult, op1=ALU.mult).then_inc(out_ready, 1)

            def split_transposed(n, f):
                for kk in range(KD // 2):
                    dve.wait_ge(tr_ps, 4 * n + kk + 1)
                    if kk >= 2:
                        dve.wait_ge(tr_hi, 4 * n + kk - 1)
                        dve.wait_ge(tr_lo, 4 * n + kk - 1)
                    if f is None:
                        i = dve.tensor_copy(tmp[:, kk % 2, :], ps[:, 2 + kk % 2, :])
                    else:
                        for h in range(2):
                            k = 2 * kk + h
                            i = dve.tensor_scalar(tmp[:, kk % 2, h * SEQ:h * SEQ + SEQ],
                                                  ps[:, 2 + kk % 2, h * SEQ:h * SEQ + SEQ],
                                                  A[:, n // 3, f, k:k + 1], modc[:, n // 3, 3 * f, k:k + 1],
                                                  ALU.mult, ALU.add)
                    i.then_inc(tr_copied, 1)
                    dve.wait_ge(tr_hi, 4 * n + kk + 1)
                    dve.tensor_tensor(hTl[:, 2 * kk:2 * kk + 2, :],
                                      tmp[:, kk % 2, :].rearrange("p (k n) -> p k n", k=2),
                                      hTh[:, 2 * kk:2 * kk + 2, :].bitcast(F32), ALU.subtract).then_inc(tr_lo, 1)

            def rope(layer, c, t):
                if t == 0:
                    dve.wait_ge(proj_ps, IN_CHUNKS * layer + c + 1)
                else:
                    dve.wait_ge(parts_used, IN_BASE[layer] + 2 * c + 2)
                bank = ps[:, (2 * c + t) % 2, :]
                done = 2 * (IN_CHUNKS * layer + c) + t
                if done:
                    dve.wait_ge(rope_done, done)
                last = None
                for col, heads, tile in ROPE_GROUPS[c]:
                    if last is not None:
                        then(last)
                    src = bank[:, col:col + heads * HEAD].rearrange("p (h a n) -> p h a n", h=heads, a=2)
                    a = rope_a[:, 0:heads * HEAD].rearrange("p (h a n) -> p h a n", h=heads, a=2)
                    b = rope_b[:, 0:heads * HEAD].rearrange("p (h a n) -> p h a n", h=heads, a=2)
                    wide = [P, heads, HALF]
                    for s in range(2):
                        dve.tensor_tensor(a[:, :, s, :], src[:, :, s, :],
                                          cosF[:, t, s, :].unsqueeze(1).broadcast_to(wide), ALU.mult)
                        i = dve.tensor_tensor(b[:, :, s, :], src[:, :, 1 - s, :],
                                              sinS[:, t, s, :].unsqueeze(1).broadcast_to(wide), ALU.mult)
                    then(i)
                    last = dve.tensor_tensor(qk[:, t, tile * P:tile * P + heads * HEAD],
                                             rope_a[:, 0:heads * HEAD], rope_b[:, 0:heads * HEAD], ALU.add)
                    if tile == 4:
                        for h in range(2):
                            at = (tile + 1) * P + (1 - h) * HEAD
                            last = dve.tensor_tensor(qk[:, t, at:at + HEAD], rope_a[:, h * HEAD:h * HEAD + HEAD],
                                                     rope_b[:, h * HEAD:h * HEAD + HEAD], ALU.add)
                for col, n, to in V_GROUPS[c]:
                    last = dve.tensor_copy(v[:, t, to:to + n], bank[:, col:col + n])
                last.then_inc(rope_done, 1)

            def maxima(layer, i):
                u, par, q, m, t = UNITS * layer + i, i % 2, i % 4, i % 8, i // 8
                dve.wait_ge(s_ps, u + 1)
                raw = ps[:, 4 + 2 * par:6 + 2 * par, 0:SEQ]
                if m < 4:
                    h = N_WIN * layer + 2 * m
                    then(dve.tensor_tensor(scores[:, par], raw, mask[:, t, :].unsqueeze(1).broadcast_to([P, 2, SEQ]),
                                           ALU.add))
                    then(dve.reduce_max(mx[:, q, :], scores[:, par], AX_X))
                    then(dve.scalar_tensor_tensor(out=negm[:, q, :], in0=mx[:, q, :], scalar=-SCALE,
                                                  in1=negsink[:, h:h + 2], op0=ALU.mult, op1=ALU.min))
                    dve.tensor_tensor(sinkm[:, q, :], sinks[:, h:h + 2], negm[:, q, :],
                                      ALU.add).then_inc(max_done, 1)
                else:
                    then(dve.reduce_max(mx[:, q, :], raw, AX_X))
                    dve.tensor_scalar(negm[:, q, :], mx[:, q, :], -SCALE, None, ALU.mult).then_inc(max_done, 1)

            def probabilities(layer, i):
                u, par, q, m = UNITS * layer + i, i % 2, i % 4, i % 8
                dve.wait_ge(exp_done, u + 1)
                if u >= 4:
                    dve.wait_ge(o_done, u - 3)
                if m < 4:
                    then(dve.tensor_tensor(den[:, q, :], sums[:, q, :], sinke[:, q, :], ALU.add))
                    dve.reciprocal(rec[:, q, :], den[:, q, :]).then_inc(probs_done, 1)
                else:
                    then(dve.reciprocal(rec[:, q, :], sums[:, q, :]))
                    then(dve.scalar_tensor_tensor(out=nl[:, q:q + 1], in0=sums[:, q, 0:1],
                                                  scalar=rec[:, q, 1:2], in1=neglam[:, layer:layer + 1],
                                                  op0=ALU.mult, op1=ALU.mult))
                    dve.scalar_tensor_tensor(out=E[:, par, 0, :], in0=E[:, par, 1, :], scalar=nl[:, q:q + 1],
                                             in1=E[:, par, 0, :], op0=ALU.mult, op1=ALU.add).then_inc(probs_done, 1)

            def head_out(layer, i):
                u, par, q, m, t = UNITS * layer + i, i % 2, i % 4, i % 8, i // 8
                dve.wait_ge(o_ps, u + 1)
                dst = xn[:, t, m * P:m * P + P]
                if m < 4:
                    i = dve.tensor_tensor(dst.rearrange("p (h n) -> p h n", h=2),
                                          ps[:, par, 0:P].rearrange("p (h n) -> p h n", h=2),
                                          rec[:, q, :].unsqueeze(2).broadcast_to([P, 2, HEAD]), ALU.mult)
                else:
                    i = dve.tensor_scalar(dst, ps[:, par, 0:P], rec[:, q, 0:1], None, ALU.mult)
                i.then_inc(o_done, 1)

            def attention(layer):
                for m in range(1, QK_TILES // 2, 2):
                    dve.wait_ge(qkT_ps, 7 * layer + m + 1)
                    dve.tensor_copy(qkT[:, 2 * m:2 * m + 2, :],
                                    ps[:, 3, :].rearrange("p (m n) -> p m n", m=2)).then_inc(qkT_odd, 1)
                for i in range(UNITS + 3):
                    if i < UNITS:
                        maxima(layer, i)
                    if 1 <= i <= UNITS:
                        probabilities(layer, i - 1)
                    if i >= 3:
                        head_out(layer, i - 3)
                    for k, (of, n) in enumerate(ADA_LATER[layer]):
                        if n % 4 == 3 and ADA_STEP[k] + 1 == i:
                            mod_round(of, n // 4)
                dve.wait_ge(dsq_done, NT * N_DIFF * (layer + 1))
                dve.tensor_scalar(ms_d[:], ssq_d[:], 1.0 / P, EPS, ALU.mult, ALU.add).then_inc(dms_done, 1)
                if ADA_STEP[len(ADA_LATER[layer]) - 1] == UNITS + 2:
                    mod_round(ADA_LATER[layer][-1][0], ADA_LATER[layer][-1][1] // 4)
                mod_columns(layer + 1)
                dve.wait_ge(drstd_done, layer + 1)
                for t in range(NT):
                    for h in range(N_DIFF):
                        o = xn[:, t, WIN_WIDTH + h * P:WIN_WIDTH + h * P + P]
                        n = N_DIFF * t + h
                        dve.scalar_tensor_tensor(out=o, in0=o, scalar=rstd_d[:, n:n + 1], in1=subgs[:, layer, :],
                                                 op0=ALU.mult, op1=ALU.mult).then_inc(mix_done, 1)

            def mixed(layer):
                for c in range(OUT_CHUNKS):
                    for t in range(NT):
                        if t == 0:
                            dve.wait_ge(wo_ps, OUT_CHUNKS * layer + c + 1)
                        else:
                            dve.wait_ge(parts_used, OUT_BASE[layer] + 2 * c + 2)
                        cols = slice(512 * c, 512 * c + 512)
                        then(dve.tensor_tensor(tmp[:, t, :], ps[:, 4 + 2 * c + t, :], gate[:, 0, cols], ALU.mult))
                        dve.tensor_tensor(x[:, t, cols], x[:, t, cols], tmp[:, t, :], ALU.add).then_inc(x_mixed, 1)

            def blocks(base, first, nu, summed=None, earlier=None, later=None, ahead=None):
                def part(b, i):
                    low(b * PARTS + (base + i), i // 2, i // 2, (i % 2) * PART, PART)

                def gated(b, i):
                    dve.wait_ge(silu_done, b * nu + (U0[nu] + i + 1))
                    dve.tensor_tensor(act_sb[:, i % 2, :], sg[:, i % 2, :], ps[:, 4 + i % 2, HB:2 * HB],
                                      ALU.mult).then_inc(act_done, 1)

                def turned(b, i):
                    dve.wait_ge(at_hi, b * nu + (U0[nu] + i + 1))
                    dve.tensor_tensor(aTl[:, i % 2, :, :],
                                      ps[:, 6 + i % 2, 0:2 * P].rearrange("p (k n) -> p k n", k=2),
                                      aTh[:, i % 2, :, :].bitcast(F32), ALU.subtract).then_inc(at_lo, 1)

                def one(b, is_first, is_last):
                    if is_first:
                        for i in range(4):
                            part(b, i)
                        gated(b, 0)
                        if earlier:
                            earlier()
                        part(b, 4)
                    else:
                        part(b, 4)
                        part(b, 5)
                        gated(b, 0)
                    for i in range(1, nu - 1):
                        turned(b, i - 1)
                        gated(b, i)
                    turned(b, nu - 2)
                    if is_first:
                        part(b, 5)
                    if not is_last:
                        part(b + 1, 0)
                    gated(b, nu - 1)
                    if is_first and summed:
                        summed()
                    if not is_last:
                        part(b + 1, 1)
                    turned(b, nu - 1)
                    if is_first and later:
                        later()
                    if is_last and ahead:
                        ahead()
                    if not is_last:
                        part(b + 1, 2)
                        part(b + 1, 3)

                one(first + 0, True, False)
                with dve.Fori(0, NB - 2) as j:
                    one(first + (j + 1), False, False)
                one(first + (NB - 1), False, True)

            def dense_out():
                dve.wait_ge(parts_used, FF_BASE[0] + NB * PARTS)
                for t in range(NT):
                    for h in range(2):
                        cols = slice(512 * h, 512 * h + 512)
                        then(dve.tensor_tensor(tmp[:, h, :], ps[:, 2 * t + h, :], gate[:, 1, cols], ALU.mult))
                        dve.tensor_tensor(x[:, t, cols], x[:, t, cols], tmp[:, h, :], ALU.add).then_inc(x_ffn, 1)

            def route():
                dve.wait_ge(logit_ps, 1)
                dve.tensor_copy(lgT[:], ps[0:N_EXP, 4, 0:SEQ]).then_inc(logits_copied, 1)
                dve.wait_ge(logit_ps, 2)
                then(dve.tensor_copy(lg[:], ps[:, 6, 0:NT * N_EXP].rearrange("p (t e) -> p t e", t=NT)))
                for t in range(NT):
                    then(dve.max(mv[:, t, :], lg[:, t, :]))
                    then(dve.max_index(mi[:, t, :], mv[:, t, :], lg[:, t, :]))
                then(dve.tensor_copy(mf[:], mi[:]))
                dve.tensor_tensor(dlt[:], mv[:, :, 1], mv[:, :, 0], ALU.subtract).then_inc(gap_ready, 1)
                for t in range(NT):
                    for r in range(2):
                        i = dve.tensor_scalar(oh[:, t, r, :], iota_row[:, 0:N_EXP], mf[:, t, r:r + 1], None,
                                              ALU.is_equal)
                then(i)
                dve.tensor_tensor(chosen[:], oh[:, :, 0, :], oh[:, :, 1, :], ALU.add).then_inc(chosen_ready, 1)
                dve.wait_ge(gap_exp, 1)
                then(dve.tensor_scalar(den2[:], edl[:], 1.0, None, ALU.add))
                then(dve.reciprocal(w12[:, 0, :], den2[:]))
                then(dve.tensor_tensor(w12[:, 1, :], w12[:, 0, :], edl[:], ALU.mult))
                for t in range(NT):
                    then(dve.tensor_scalar(wtmp[:, t, :], oh[:, t, 0, :], w12[:, 0, t:t + 1], None, ALU.mult))
                    then(dve.scalar_tensor_tensor(out=wS[:, t, 0:N_EXP], in0=oh[:, t, 1, :], scalar=w12[:, 1, t:t + 1],
                                                  in1=wtmp[:, t, :], op0=ALU.mult, op1=ALU.add))
                dve.wait_ge(pos_ps, 1)
                for t in range(NT):
                    then(dve.scalar_tensor_tensor(out=wtmp[:, t, :], in0=ps[:, 5, t * N_EXP:t * N_EXP + N_EXP],
                                                  scalar=1.0, in1=chosen[:, t, :], op0=ALU.add, op1=ALU.mult))
                    then(dve.tensor_scalar(posS[:, t, 0:N_EXP], wtmp[:, t, :], -1.0, None, ALU.add))
                then(dve.tensor_scalar(over[:], ps[:, 5, 2 * N_EXP:3 * N_EXP], float(P), None, ALU.is_gt))
                then(dve.memset(rank[:, 0:1], 0.0))
                for e in range(N_EXP):
                    then(dve.tensor_tensor(rank[:, e + 1:e + 2], rank[:, e:e + 1], over[:, e:e + 1], ALU.add))
                then(dve.memset(tabf[:], 0.0))
                for o in range(MAX_OVER):
                    s = N_EXP + o
                    then(dve.scalar_tensor_tensor(out=sel[:, o, :], in0=rank[:, 0:N_EXP], scalar=float(o),
                                                  in1=over[:], op0=ALU.is_equal, op1=ALU.mult))
                    for t in range(NT):
                        dve.tensor_tensor(prod[:, t, :], sel[:, o, :], posS[:, t, 0:N_EXP], ALU.mult)
                        dve.tensor_tensor(prod[:, NT + t, :], sel[:, o, :], wS[:, t, 0:N_EXP], ALU.mult)
                    then(dve.tensor_tensor(prod[:, 4, :], sel[:, o, :], iota_row[:, 0:N_EXP], ALU.mult))
                    dve.reduce_sum(posr[:], prod[:, 0:NT, :], AX_X)
                    dve.reduce_sum(wS[:, :, s], prod[:, NT:2 * NT, :], AX_X)
                    then(dve.reduce_sum(tabf[:, 0, o:o + 1], prod[:, 4, :], AX_X))
                    dve.tensor_scalar(posS[:, :, s], posr[:], -float(P), None, ALU.add)
                    then(dve.tensor_scalar(tabf[:, 1, o:o + 1], rank[:, N_EXP:N_EXP + 1], float(o), None, ALU.is_gt))
                then(dve.tensor_copy(tabf[:, 1, MAX_OVER:MAX_OVER + 1], rank[:, N_EXP:N_EXP + 1]))
                dve.memset(posS[:, :, N_SLOT:], -1.0)
                then(dve.memset(wS[:, :, N_SLOT:], 0.0))
                dve.tensor_copy(table[:], tabf[:]).then_inc(table_ready, 1)

            def picks(dst, s, weighted):
                for t in range(NT):
                    if weighted:
                        i = dve.tensor_scalar(dst[:, t, :], iota_row[:], posS[:, t, bass.ds(s, 1)],
                                              wS[:, t, bass.ds(s, 1)], ALU.is_equal, ALU.mult)
                    else:
                        i = dve.tensor_scalar(dst[:, t, :], iota_row[:], posS[:, t, bass.ds(s, 1)], None, ALU.is_equal)
                return i

            def input_low():
                dve.tensor_tensor(hTl[:, :, 0:P], xsT[:], hTh[:, :, 0:P].bitcast(F32),
                                  ALU.subtract).then_inc(slot_lo, 1)

            def gated_output(n):
                dve.wait_ge(parts_used, n * (NB * PARTS) + FF_BASE[1])
                for h in range(2):
                    i = dve.tensor_tensor(ysb[:, 512 * h:512 * h + 512], ps[:, h, :],
                                          gate[:, 1, 512 * h:512 * h + 512], ALU.mult)
                i.then_inc(y_ready, 1)

            def add_to_x(n):
                for i in range(4):
                    t, cols = 1 - i // 2, slice(512 * (i % 2), 512 * (i % 2) + 512)
                    dve.wait_ge(comb_ps, n * 4 + (i - 3))
                    dve.wait_ge(x_added, n * 4)
                    dve.tensor_tensor(x[:, t, cols], x[:, t, cols], ps[:, i, :], ALU.add).then_inc(x_added, 1)

            def slot(s, follows):
                def next_rows():
                    dve.wait_ge(gather_ps, s + 1)
                    picks(pick, s + 1, False).then_inc(pick_ready, 1)
                    picks(pickw, s, True).then_inc(pickw_ready, 1)

                def next_input():
                    dve.wait_ge(slot_hi, s + 2)
                    input_low()

                blocks(FF_BASE[1], s * NB, 2,
                       summed=(lambda: add_to_x(s)) if follows else None,
                       earlier=(lambda: gated_output(s)) if follows else None,
                       later=next_rows, ahead=next_input)

            columns()
            dve.wait_ge(x_loaded, 16 * NT)
            normalise(0)
            setup()
            for layer in range(DEPTH):
                if not layer:
                    mod_round(0, 0)
                    mod_columns(0)
                else:
                    for c in range(2):
                        straight("in", layer, c)
                    dense_out()
                    normalise(2 * layer)
                split_transposed(3 * layer, 0)
                if not layer:
                    for c in range(2):
                        straight("in", layer, c)
                for c in range(IN_CHUNKS):
                    for t in range(NT):
                        rope(layer, c, t)
                    if c + 2 < IN_CHUNKS:
                        straight("in", layer, c + 2)
                    else:
                        straight("out", layer, c + 2 - IN_CHUNKS)
                attention(layer)
                split_transposed(3 * layer + 1, None)
                dve.wait_ge(gates_ready, 4 * layer + 4)
                mixed(layer)
                dve.wait_ge(x_mixed, 4 * layer + 4)
                normalise(2 * layer + 1)
                split_transposed(3 * layer + 2, 1)
                if not layer:
                    blocks(FF_BASE[0], 0, 4)
                else:
                    dve.wait_ge(rw_hi, 1)
                    dve.tensor_tensor(rwl[:], rw[:], rwh[:].bitcast(F32), ALU.subtract).then_inc(rw_lo, 1)
                    route()
            picks(pick, 0, False).then_inc(pick_ready, 1)
            dve.memset(done_mark[:], 0.0).then_inc(x_added, 4)
            dve.wait_ge(slot_hi, 1)
            input_low()
            slot(0, False)
            with dve.Fori(0, N_EXP - 1) as s:
                slot(s + 1, True)
            dve.wait_ge(table_ready, 1)
            with dve.Fori(0, MAX_OVER) as o:
                used = dve.value_load(table[0:1, 1, bass.ds(o, 1)], min_val=0, max_val=1)
                with dve.If(used > 0):
                    slot(o + N_EXP, True)
            extra = dve.value_load(table[0:1, 1, MAX_OVER:MAX_OVER + 1], min_val=0, max_val=MAX_OVER)
            gated_output(extra + N_EXP)
            add_to_x(extra + N_EXP)
            dve.memset(done_mark[:], 0.0).then_inc(moe_done, 1)
            dve.wait_ge(moe_done, 1)
            dve.wait_ge(late_loaded, 32)
            normalise(4)

        @block.tensor
        def _(pe):
            def ada_chunk(layer, n):
                slot, _, loaded = plan[("ada", layer, n)]
                r, q = n // 4, n % 4
                pe.wait_ge(w_loaded[slot], loaded)
                if q == 0 and layer + r:
                    pe.wait_ge(mod_ready, 3 * layer + r)
                for kk in range(2):
                    k = 2 * q + kk
                    for g in range(4):
                        mm = pe.matmul(ps[32 * g:32 * g + 32, 2, :], c_rep[:, k, :],
                                       W[:, slot, kk * 2048 + g * 512:kk * 2048 + g * 512 + 512],
                                       start=(k == 0), stop=(k == KD - 1))
                mm.then_inc(ada_used, 1)

            def mod_columns(n):
                rounds = ((0,), (1, 2, 0), (1, 2))[n]
                pe.wait_ge(mod_ready, (1, 4, 6)[n])
                for r in rounds:
                    for i in range(4):
                        mm = pe.matmul(ps[:, 3, 16 * r + i:16 * r + i + 13:4], modrow[:, r, i * P:i * P + P],
                                       ident[:, 0:P:32], start=True, stop=True)
                mm.then_inc(cols_ps, 1)

            def gates(layer):
                for i, chunk in enumerate((4, 5, 10, 11)):
                    g, r = chunk % 4, chunk // 4
                    pe.matmul(ps[:, 4 + i, :], ones[32 * g:32 * g + 1, :], modrow[32 * g:32 * g + 1, r, :],
                              start=True, stop=True).then_inc(gates_ps, 1)

            def transpose_all(n):
                for kk in range(KD // 2):
                    if kk >= 2:
                        pe.wait_ge(tr_copied, 4 * n + kk - 1)
                    for h in range(2):
                        for t in range(NT):
                            at = (2 * kk + h) * P
                            mm = pe.transpose(ps[:, 2 + kk % 2, h * SEQ + t * P:h * SEQ + t * P + P],
                                              xn[:, t, at:at + P], ident[:])
                    mm.then_inc(tr_ps, 1)

            def wait_part(q):
                pe.wait_ge(hi_done, q + 1)
                pe.wait_ge(lo_done, q + 1)
                pe.wait_ge(lop_done, q + 1)

            def three(dst, stat_hi, stat_lo, hi, lo, start, stop):
                pe.matmul(dst, stat_hi, hi, start=start, stop=False, skip_group_check=True)
                pe.matmul(dst, stat_hi, lo, start=False, stop=False, skip_group_check=True)
                return pe.matmul(dst, stat_lo, hi, start=False, stop=stop, skip_group_check=True)

            def project(kind, layer, c, split=None):
                parts = list(straight_parts(kind, layer, c))
                hslot, n = parts[0][2], parts[0][4] // 4
                hi, lo = (h[:, 0:KD * n].rearrange("p (k n) -> p k n", k=KD) for h in halves(hslot))
                for t in range(NT):
                    if kind == "in":
                        i = 2 * c + t
                        if i >= 2:
                            pe.wait_ge(rope_done, 2 * IN_CHUNKS * layer + i - 1)
                        bank = i % 2
                    else:
                        bank = 4 + 2 * c + t
                    tok = slice(t * P, t * P + P)
                    for k in range(KD):
                        if t == 0 and k % 4 == 0:
                            wait_part(parts[k // 4][0])
                        if t == 0 and c == 0 and k % 2 == 0:
                            pe.wait_ge(tr_lo, 4 * split + k // 2 + 1)
                        mm = three(ps[:, bank, 0:n], hTh[:, k, tok], hTl[:, k, tok], hi[:, k, :], lo[:, k, :],
                                   k == 0, k == KD - 1)
                        if t and k % 4 == 3:
                            mm.then_inc(parts_used, 1)
                    if t == 0:
                        mm.then_inc(proj_ps if kind == "in" else wo_ps, 1)

            def attention(layer):
                pe.wait_ge(rope_done, 2 * IN_CHUNKS * (layer + 1))
                for m in range(QK_TILES // 2):
                    if m >= 2:
                        s, per = (qkT_even, 4) if m % 2 == 0 else (qkT_odd, 3)
                        pe.wait_ge(s, per * layer + m // 2)
                    for h in range(2):
                        for t in range(NT):
                            mm = pe.transpose(ps[:, 2 + m % 2, h * SEQ + t * P:h * SEQ + t * P + P],
                                              qk[:, t, (2 * m + h) * P:(2 * m + h) * P + P], ident[:])
                    mm.then_inc(qkT_ps, 1)
                pe.wait_ge(qkT_even, 4 * layer + 4)
                pe.wait_ge(qkT_odd, 3 * layer + 3)
                for i in range(UNITS + 3):
                    if i < UNITS:
                        u, par, m, t = UNITS * layer + i, i % 2, i % 8, i // 8
                        if i >= 2:
                            pe.wait_ge(exp_done, u - 1)
                        for h in range(2):
                            if m < 4:
                                q_tile, k_tile = m, 4 + (m // 2 + h) % 2
                            else:
                                q_tile, k_tile = 2 + m, 6 + m
                            rows = slice(HEAD * h, HEAD * h + HEAD)
                            mm = pe.matmul(ps[:, 4 + 2 * par + h, 0:SEQ], qkT[rows, q_tile, t * P:t * P + P],
                                           qkT[rows, k_tile, :], start=True, stop=True)
                        mm.then_inc(s_ps, 1)
                    if 2 <= i <= UNITS + 1:
                        u, par, m = UNITS * layer + i - 2, i % 2, (i - 2) % 8
                        pe.wait_ge(probs_done, u + 1)
                        if i >= 3:
                            pe.wait_ge(pt_done, u)
                        for n in range(4 if m < 4 else 2):
                            mm = pe.transpose(ps[:, 3, n * P:n * P + P],
                                              E[:, par, n // 2, (n % 2) * P:(n % 2) * P + P], ident[:])
                        mm.then_inc(pt_ps, 1)
                    if i >= 3:
                        u, par, m = UNITS * layer + i - 3, (i - 3) % 2, (i - 3) % 8
                        pe.wait_ge(pt_done, u + 1)
                        if i >= 5:
                            pe.wait_ge(o_done, u - 1)
                        for h in range(2 if m < 4 else 1):
                            width = HEAD if m < 4 else P
                            col = (m // 2) * HEAD if m < 4 else P + (m - 4) * P
                            for kt in range(NT):
                                mm = pe.matmul(ps[:, par, h * width:h * width + width], PT[:, par, 2 * h + kt, :],
                                               v[:, kt, col:col + width], start=(kt == 0), stop=(kt == NT - 1))
                        mm.then_inc(o_ps, 1)
                    for k, (of, n) in enumerate(ADA_LATER[layer]):
                        if ADA_STEP[k] == i:
                            ada_chunk(of, n)
                mod_columns(layer + 1)
                gates(layer)

            def gate_up(i, nu, ks, base, b, is_first):
                half, t = (i // 2, i % 2) if nu == 4 else (i, 0)
                tok = slice(t * P, t * P + P)
                cols = slice(half * HB, half * HB + HB)
                for k in ks:
                    if i == 0 and k % 2 == 0:
                        wait_part(b * PARTS + (base + k // 2))
                        if is_first and nu == 4:
                            pe.wait_ge(tr_lo, 4 * 2 + k // 2 + 1)
                    mm = three(ps[:, 4 + i % 2, :].rearrange("p (g n) -> p g n", g=2), hTh[:, k, tok], hTl[:, k, tok],
                               hg_ff[0][:, k // 4, k % 4, :, cols], hg_ff[1][:, k // 4, k % 4, :, cols],
                               k == 0, k == KD - 1)
                    if i == nu - 1 and k % 2 == 1:
                        mm.then_inc(parts_used, 1)
                    elif i < nu - 1 and k == KD - 1:
                        mm.then_inc(gu_ps, 1)

            def turn(i, nu, b):
                pe.wait_ge(act_done, b * nu + (U0[nu] + i + 1))
                for n in range(2):
                    mm = pe.transpose(ps[:, 6 + i % 2, n * P:n * P + P], act_sb[:, i % 2, n * P:n * P + P], ident[:])
                mm.then_inc(at_ps, 1)

            def down(i, nu, ns, base, b, is_first):
                half, t = (i // 2, i % 2) if nu == 4 else (i, 0)
                if 0 in ns:
                    pe.wait_ge(at_hi, b * nu + (U0[nu] + i + 1))
                    pe.wait_ge(at_lo, b * nu + (U0[nu] + i + 1))
                    if i % (nu // 2) == 0:
                        wait_part(b * PARTS + (base + 4 + half))
                for n in ns:
                    k = 2 * half + n
                    for h in range(2):
                        cols = slice(512 * h, 512 * h + 512)
                        mm = three(ps[:, 2 * t + h, :], aTh[:, i % 2, n, :], aTl[:, i % 2, n, :],
                                   hd_ff[0][:, k, cols], hd_ff[1][:, k, cols], is_first and k == 0, False)
                if i == nu - 1 or (i == nu - 2 and ns == ((1,) if nu == 2 else (0,))):
                    mm.then_inc(parts_used, 1)

            def blocks(base, first, nu, summed=None, rows=None, gathering=None):
                def one(b, is_first, is_last):
                    if is_last and rows:
                        rows()
                    gate_up(0, nu, range(KD), base, b, is_first)
                    if is_last and gathering:
                        gathering()
                    for i in range(1, nu):
                        gate_up(i, nu, range(0, KD // 2), base, b, is_first)
                        turn(i - 1, nu, b)
                        gate_up(i, nu, range(KD // 2, KD), base, b, is_first)
                        if i < nu - 1:
                            down(i - 1, nu, (0, 1), base, b, is_first)
                    if is_first and summed:
                        summed()
                    down(nu - 2, nu, (0,), base, b, is_first)
                    turn(nu - 1, nu, b)
                    down(nu - 2, nu, (1,), base, b, is_first)
                    down(nu - 1, nu, (0, 1), base, b, is_first)

                one(first + 0, True, False)
                with pe.Fori(0, NB - 2) as j:
                    one(first + (j + 1), False, False)
                one(first + (NB - 1), False, True)

            def route():
                pe.wait_ge(rw_lo, 1)
                for k in range(KD):
                    if k % 2 == 0:
                        pe.wait_ge(tr_lo, 4 * 5 + k // 2 + 1)
                    for i, (w, a) in enumerate(((rwh, hTh), (rwl, hTh), (rwh, hTl), (rwl, hTl))):
                        mm = pe.matmul(ps[0:N_EXP, 4, 0:SEQ], w[:, k, :], a[:, k, :],
                                       start=(k == 0 and i == 0), stop=(k == KD - 1 and i == 3))
                mm.then_inc(logit_ps, 1)
                pe.wait_ge(logits_copied, 1)
                for t in range(NT):
                    mm = pe.transpose(ps[:, 6, t * N_EXP:t * N_EXP + N_EXP], lgT[:, t * P:t * P + P],
                                      ident[0:N_EXP, 0:N_EXP])
                mm.then_inc(logit_ps, 1)
                pe.wait_ge(chosen_ready, 1)
                at = [slice(i * N_EXP, i * N_EXP + N_EXP) for i in range(3)]
                pe.matmul(ps[:, 5, at[0]], before[:], chosen[:, 0, :], start=True, stop=True)
                for i, first in ((1, ones), (2, ones)):
                    pe.matmul(ps[:, 5, at[i]], first[:], chosen[:, 0, :], start=True, stop=False)
                    mm = pe.matmul(ps[:, 5, at[i]], (before if i == 1 else ones)[:], chosen[:, 1, :],
                                   start=False, stop=True)
                mm.then_inc(pos_ps, 1)

            def gather(n):
                pe.wait_ge(pick_ready, n)
                for k in range(KD):
                    for t in range(NT):
                        mm = pe.matmul(ps[:, 2 + k // 4, (k % 4) * P:(k % 4) * P + P], xn[:, t, k * P:k * P + P],
                                       pick[:, t, :], start=(t == 0), stop=(t == NT - 1))
                mm.then_inc(gather_ps, 1)

            def combine(n):
                pe.wait_ge(pickT_ready, n)
                pe.wait_ge(y_ready, n)
                for i in range(4):
                    cols = slice(512 * (i % 2), 512 * (i % 2) + 512)
                    pe.matmul(ps[:, i, :], pickT[:, 1 - i // 2, :], ysb[:, cols],
                              start=True, stop=True).then_inc(comb_ps, 1)

            def slot(s, follows):
                def summed():
                    combine(s)
                    pe.wait_ge(x_added, s * 4 + 2)

                def rows():
                    pe.wait_ge(pickw_ready, s + 1)
                    pe.wait_ge(x_added, s * 4 + 4)
                    for t in range(NT):
                        mm = pe.transpose(ps[:, 2, t * P:t * P + P], pickw[:, t, :], ident[:])
                    mm.then_inc(pickT_ps, 1)

                def gathering():
                    pe.wait_ge(pickT_ready, s + 1)
                    gather(s + 2)

                pe.wait_ge(slot_lo, s + 1)
                blocks(FF_BASE[1], s * NB, 2, summed if follows else None, rows, gathering)

            pe.wait_ge(setup_done, SETUP)
            pe.wait_ge(vec_silu, 1)
            pe.transpose(ps[:, 3, 0:40], vecrows[:], ident[0:40, 0:40]).then_inc(vec_ps, 1)
            pe.wait_ge(vec_cols, 1)
            for layer in range(DEPTH):
                if not layer:
                    for n in range(ADA_FIRST):
                        ada_chunk(0, n)
                    mod_columns(0)
                    pe.wait_ge(cols_ready, 1)
                pe.wait_ge(xn_done, 4 * layer + 2)
                transpose_all(3 * layer)
                for c in range(IN_CHUNKS):
                    project("in", layer, c, 3 * layer)
                attention(layer)
                pe.wait_ge(mix_done, NT * N_DIFF * (layer + 1))
                transpose_all(3 * layer + 1)
                pe.wait_ge(gates_ready, 4 * layer + 4)
                for c in range(OUT_CHUNKS):
                    project("out", layer, c, 3 * layer + 1)
                pe.wait_ge(xn_done, 4 * layer + 4)
                transpose_all(3 * layer + 2)
                if not layer:
                    blocks(FF_BASE[0], 0, 4)
                else:
                    route()
            gather(1)
            slot(0, False)
            with pe.Fori(0, N_EXP - 1) as s:
                slot(s + 1, True)
            pe.wait_ge(table_ready, 1)
            with pe.Fori(0, MAX_OVER) as o:
                used = pe.value_load(table[0:1, 1, bass.ds(o, 1)], min_val=0, max_val=1)
                with pe.If(used > 0):
                    slot(o + N_EXP, True)
            extra = pe.value_load(table[0:1, 1, MAX_OVER:MAX_OVER + 1], min_val=0, max_val=MAX_OVER)
            combine(extra + N_EXP)


_INS = ["x", "c", "positions", "inv_freq", "ada_w", "ada_b", "norm_mix_g", "norm_ffn_g", "w_in", "w_out",
        "sink", "lam_q1", "lam_k1", "lam_q2", "lam_k2", "subln_g", "ffn_w_gate", "ffn_w_up", "ffn_w_down",
        "router_w", "moe_w_gate", "moe_w_up", "moe_w_down", "final_g"]


def kernel(**inputs):
    import concourse.bacc as _bacc
    from concourse.bass_utils import run_bass_kernel_spmd as _run

    nc = _bacc.Bacc("TRN2", target_bir_lowering=False, num_devices=1, dynamic_dma_scratch_size=1024)
    freq = 1.0 / (10000.0 ** (np.arange(0, HEAD, 2, dtype=np.float32) / HEAD))
    data = dict(inputs, inv_freq=freq.astype(np.float32).reshape(1, HALF))
    arrays, args = {}, []
    for name in _INS:
        a = np.ascontiguousarray(data[name])
        arrays[f"in_{name}_dram"] = a
        args.append(nc.dram_tensor(f"in_{name}_dram", a.shape, mybir.dt.from_np(a.dtype), kind="ExternalInput").ap())
    out = nc.dram_tensor("out_0_dram", (1, SEQ, D), F32, kind="ExternalOutput").ap()
    build(nc, *args, out)
    r = _run(nc, [arrays], core_ids=[0])
    return r.results[0]["out_0_dram"]
```

```python
import math
from contextlib import ExitStack

import numpy as np

import concourse.bass as bass
from concourse import mybir

ALU = mybir.AluOpType
ACT = mybir.ActivationFunctionType
AX_X = mybir.AxisListType.X
F32 = mybir.dt.float32
F32R = mybir.dt.float32r
I32 = mybir.dt.int32
U32 = mybir.dt.uint32

P = 128
D = 1024
SEQ = 256
DEPTH = 2
NT = SEQ // P
KD = D // P
HEAD = 64
HALF = HEAD // 2
EPS = 1e-6
N_WIN = 8
N_DIFF = 4
WIN_WIDTH = 512
IN_COLS = 2304
D_FF = 3584
BLOCK = 512
NB = D_FF // BLOCK
HB = BLOCK // 2
N_EXP = 8
MAX_OVER = 3
N_SLOT = N_EXP + MAX_OVER
SCALE = HEAD ** -0.5
MASKED = -1e30
ROUNDER = 12582912.0
TWO_PI_PARTS = (6.28125, 0.0019350051879882812, 3.0199159819567e-07)

CH = 4096
PART = CH // 2
PARTS = 6
IN_CHUNKS = 5
OUT_CHUNKS = 2
ADA_CHUNKS = 12
RING = 3
ADA_FIRST = 4
ADA_LATER = [[(0, n) for n in range(ADA_FIRST, ADA_CHUNKS)] + [(1, n) for n in range(ADA_FIRST)],
             [(1, n) for n in range(ADA_FIRST, ADA_CHUNKS)]]
ADA_STEP = [0, 0, 1] + [2 * (i - 2) for i in range(3, ADA_CHUNKS)]

IN_PARTS, OUT_PARTS = 2 * IN_CHUNKS, 2 * OUT_CHUNKS
IN_BASE = [0, IN_PARTS + OUT_PARTS + NB * PARTS]
OUT_BASE = [b + IN_PARTS for b in IN_BASE]
FF_BASE = [b + OUT_PARTS for b in OUT_BASE]

SPREAD = 4
UNITS = 16
ROPE_GROUPS = [[(0, 8, 0)], [(0, 2, 4), (256, 4, 6)], [(0, 8, 8)], [(0, 4, 12)], []]
V_GROUPS = [[], [(128, 128, 0)], [], [(256, 256, 128)], [(0, 256, 384)]]
QK_TILES = 14


def pair(i):
    return (i + 4) % 8


def tiles_of(n):
    return (1, 0) if n == 2 * DEPTH else (0, 1)


class Count:

    def __init__(self, sem):
        self.sem, self.n = sem, 0

    def mark(self, instruction):
        instruction.then_inc(self.sem, 1)
        self.n += 1
        return self.n


def plan_ring():
    loads, holder, plan = [0] * RING, [None] * RING, {}

    def put(name, slot, holds):
        plan[name] = (slot, holder[slot], loads[slot] + 16)
        loads[slot] += 16
        holder[slot] = holds

    def mixer(layer, at):
        for c in range(IN_CHUNKS):
            put(("in", layer, c), (at + c) % RING, ("split", IN_BASE[layer] + 2 * c + 2))
        put(("out", layer, 0), (at + IN_CHUNKS) % RING, ("split", OUT_BASE[layer] + 2))
        for i, (of, n) in enumerate(ADA_LATER[layer]):
            put(("ada", of, n), (at + IN_CHUNKS + 1 + i) % RING, ("ada", ADA_CHUNKS * of + n + 1))
        put(("out", layer, 1), RING - 1, ("split", OUT_BASE[layer] + 4))

    for n in range(ADA_FIRST):
        put(("ada", 0, n), n % RING, ("ada", n + 1))
    mixer(0, ADA_FIRST)
    plan["dense"] = list(loads)
    for c, dmas in enumerate((2, 2, 1)):
        loads[c] += 16 * dmas * NB
        holder[c] = ("split", FF_BASE[0] + PARTS * (NB - 1) + 2 * c + 2)
    mixer(1, 0)
    plan["experts"] = list(loads)
    return plan


def build(nc, x_in, c_in, positions, inv_freq, ada_w, ada_b, mix_g, ffn_g, w_in, w_out, sink,
          lam_q1, lam_k1, lam_q2, lam_k2, subln_g, w_gate, w_up, w_down,
          router_w, moe_gate, moe_up, moe_down, final_g, out):
    plan = plan_ring()
    with ExitStack() as ctx:
        top = [(nc.sbuf_base + 63) // 64 * 64]

        def region(nbytes):
            at = top[0]
            top[0] += (nbytes + 31) // 32 * 32
            return at

        def place(name, shape, dtype, at=None):
            words = int(np.prod(shape[1:]))
            size = words * 4
            return nc.alloc_sbuf_tensor_at(name, shape, dtype, offset=region(size) if at is None else at)

        W = place("weights", [P, RING, CH], F32)
        Hg = place("weights_hi", [P, 2, CH], F32R)
        Lg = place("weights_lo", [P, 2, CH], F32R)
        at = region(2 * CH * 4)
        Hd = place("down_hi", [P, CH], F32R, at)
        Ld = place("down_lo", [P, CH], F32R, at + CH * 4)
        qk = place("qk", [P, NT, QK_TILES * P], F32, at)
        qkT = place("qkT", [P, QK_TILES, SEQ], F32, at + NT * QK_TILES * P * 4)
        x = place("x", [P, NT, D], F32)
        xn = place("xn", [P, NT, D], F32)
        hTh = place("hT_hi", [P, KD, SEQ], F32R)
        hTl = place("hT_lo", [P, KD, SEQ], F32R)
        at = region(3 * 512 * 4)
        modrow = place("modrow", [P, 3, 512], F32, at)
        ysb = place("ysb", [P, D], F32, at)
        at = region(2 * D * 4)
        gate = place("gate", [P, 2, D], F32, at)
        xs_rows = place("xs_rows", [P, D], F32, at)
        fing = place("fing", [P, D], F32)
        at = at_work = region(17 * 1024)
        v = place("v", [P, NT, 640], F32, at)
        scores = place("scores", [P, 2, 2, SEQ], F32, at + 5120)
        rope_a = place("rope_a", [P, 512], F32, at + 5120)
        rope_b = place("rope_b", [P, 512], F32, at + 5120 + 2048)
        E = place("E", [P, 2, 2, SEQ], F32, at + 9216)
        tmp = place("tmp", [P, 2, 512], F32, at + 9216)
        PT = place("PT", [P, 2, 4, P], F32, at + 13312)
        lamv = place("lamv", [P, 4, DEPTH * HEAD], F32, at + 13312)
        subg = place("subg", [P, DEPTH, P], F32, at + 15360)
        vecrows = place("vecrows", [40, P], F32, at + 5120)
        ang = place("ang", [P, NT, HALF], F32, at + 16384)
        turns = place("turns", [P, NT, HALF], F32, at + 16640)
        arg = place("arg", [P, 2, NT, HALF], F32, at + 16896)
        sg = place("sg", [P, 2, HB], F32, at)
        act_sb = place("act", [P, 2, HB], F32, at + 2048)
        aTh = place("actT_hi", [P, 2, 2, P], F32R, at + 4096)
        aTl = place("actT_lo", [P, 2, 2, P], F32R, at + 6144)
        xsT = place("xsT", [P, KD, P], F32, at + 8192)
        pick = place("pick", [P, NT, P], F32, at + 12288)
        pickw = place("pickw", [P, NT, P], F32, at + 13312)
        pickT = place("pickT", [P, NT, P], F32, at + 14336)
        ident = place("ident", [P, P], F32)
        iota_row = place("iota_row", [P, P], F32)
        ones = place("ones", [P, P], F32)
        before = place("before", [P, P], F32)
        mask = place("mask", [P, NT, SEQ], F32)
        vcols = place("vcols", [P, 40], F32)
        c_rep = place("c_rep", [P, KD, 32], F32)
        pos_i = place("pos_i", [P, NT], I32)
        pos_f = place("pos_f", [P, NT], F32)
        inv = place("inv", [P, HALF], F32)
        cosF = place("cosF", [P, NT, 2, HALF], F32)
        sinS = place("sinS", [P, NT, 2, HALF], F32)
        sinks = place("sinks", [P, DEPTH * N_WIN], F32)
        negsink = place("negsink", [P, DEPTH * N_WIN], F32)
        lams = place("lams", [P, 2, DEPTH], F32)
        lame = place("lame", [P, 2, DEPTH], F32)
        neglam = place("neglam", [P, DEPTH], F32)
        subgs = place("subgs", [P, DEPTH, P], F32)
        rw = place("rw", [P, KD, N_EXP], F32)
        rwh = place("rwh", [P, KD, N_EXP], F32R)
        rwl = place("rwl", [P, KD, N_EXP], F32R)
        modc = place("modc", [P, DEPTH, 6, KD], F32)
        A = place("A", [P, DEPTH, 2, KD], F32)
        half_neg = place("half_neg", [P, 8], F32)
        ssq = place("ssq", [P, NT], F32)
        ms = place("ms", [P, NT], F32)
        rstd = place("rstd", [P, NT], F32)
        ssq_d = place("ssq_d", [P, NT * N_DIFF], F32)
        ms_d = place("ms_d", [P, NT * N_DIFF], F32)
        rstd_d = place("rstd_d", [P, NT * N_DIFF], F32)
        mx = place("mx", [P, 4, 2], F32)
        negm = place("negm", [P, 4, 2], F32)
        sinkm = place("sinkm", [P, 4, 2], F32)
        sinke = place("sinke", [P, 4, 2], F32)
        sums = place("sums", [P, 4, 2], F32)
        den = place("den", [P, 4, 2], F32)
        rec = place("rec", [P, 4, 2], F32)
        nl = place("nl", [P, 4], F32)
        lgT = place("lgT", [N_EXP, SEQ], F32, at_work + 5120)
        lg = place("lg", [P, NT, N_EXP], F32)
        mv = place("mv", [P, NT, 8], F32)
        mi = place("mi", [P, NT, 8], U32)
        mf = place("mf", [P, NT, 8], F32)
        oh = place("oh", [P, NT, 2, N_EXP], F32)
        dlt = place("dlt", [P, NT], F32)
        edl = place("edl", [P, NT], F32)
        den2 = place("den2", [P, NT], F32)
        w12 = place("w12", [P, 2, NT], F32)
        chosen = place("chosen", [P, NT, N_EXP], F32)
        wtmp = place("wtmp", [P, NT, N_EXP], F32)
        posS = place("posS", [P, NT, N_SLOT + 1], F32)
        wS = place("wS", [P, NT, N_SLOT + 1], F32)
        over = place("over", [P, N_EXP], F32)
        rank = place("rank", [P, N_EXP + 1], F32)
        sel = place("sel", [P, MAX_OVER, N_EXP], F32)
        prod = place("prod", [P, 5, N_EXP], F32)
        posr = place("posr", [P, NT], F32)
        tabf = place("tabf", [P, 2, 4], F32)
        table = place("table", [P, 2, 4], I32)
        done_mark = place("done_mark", [P, 2 + NT], F32)
        assert top[0] <= nc.sbuf_usable_end, top[0]

        ps = ctx.enter_context(nc.psum_tensor("ps", [P, 8, 512], F32))

        def sem(name):
            return ctx.enter_context(nc.semaphore(name))

        w_loaded = [sem(f"w_loaded{i}") for i in range(RING)]
        rows_loaded, x_loaded = sem("rows_loaded"), sem("x_loaded")
        consts_loaded, late_loaded = sem("consts_loaded"), sem("late_loaded")
        bias_loaded, table_ready = sem("bias_loaded"), sem("table_ready")
        setup_done, vec_silu, vec_ps, vec_cols = sem("setup_done"), sem("vec_silu"), sem("vec_ps"), sem("vec_cols")
        arg_ready, sin_done, lam_dot, lam_exp = sem("arg_ready"), sem("sin_done"), sem("lam_dot"), sem("lam_exp")
        hi_done, lo_done, lop_done, parts_used = sem("hi_done"), sem("lo_done"), sem("lop_done"), sem("parts_used")
        ada_used, mod_ready, cols_ps, cols_ready = sem("ada_used"), sem("mod_ready"), sem("cols_ps"), sem("cols_ready")
        gates_ps, gates_ready = sem("gates_ps"), sem("gates_ready")
        sq_done, ms_done, rstd_done, xn_done = sem("sq_done"), sem("ms_done"), sem("rstd_done"), sem("xn_done")
        tr_ps, tr_copied, tr_hi, tr_lo = sem("tr_ps"), sem("tr_copied"), sem("tr_hi"), sem("tr_lo")
        proj_ps, rope_done = sem("proj_ps"), sem("rope_done")
        qkT_ps, qkT_even, qkT_odd = sem("qkT_ps"), sem("qkT_even"), sem("qkT_odd")
        s_ps, max_done, exp_done, probs_done = sem("s_ps"), sem("max_done"), sem("exp_done"), sem("probs_done")
        pt_ps, pt_done, o_ps, o_done = sem("pt_ps"), sem("pt_done"), sem("o_ps"), sem("o_done")
        dsq_done, dms_done, drstd_done, mix_done = sem("dsq_done"), sem("dms_done"), sem("drstd_done"), sem("mix_done")
        wo_ps, x_mixed = sem("wo_ps"), sem("x_mixed")
        gu_ps, silu_done, act_done = sem("gu_ps"), sem("silu_done"), sem("act_done")
        at_ps, at_hi, at_lo = sem("at_ps"), sem("at_hi"), sem("at_lo")
        x_ffn, tile_ps = sem("x_ffn"), sem("tile_ps")
        rw_hi, rw_lo, logit_ps, logits_copied = (
            sem("rw_hi"), sem("rw_lo"), sem("logit_ps"), sem("logits_copied"))
        gap_ready, gap_exp, chosen_ready, pos_ps = (
            sem("gap_ready"), sem("gap_exp"), sem("chosen_ready"), sem("pos_ps"))
        pick_ready, gather_ps, xs_ready = sem("pick_ready"), sem("gather_ps"), sem("xs_ready")
        rows_ps, rows_copied = sem("rows_ps"), sem("rows_copied")
        slot_hi, slot_lo, pickw_ready = sem("slot_hi"), sem("slot_lo"), sem("pickw_ready")
        pickT_ps, pickT_ready, y_ready = sem("pickT_ps"), sem("pickT_ready"), sem("y_ready")
        comb_ps, x_added, moe_done = sem("comb_ps"), sem("x_added"), sem("moe_done")
        dve_step, out_ready, out_written = sem("dve_step"), sem("out_ready"), sem("out_written")

        def bias_loads(layer, rounds):
            src = ada_b[layer].rearrange("(r g n) -> g r n", r=3, g=4)
            return [(modrow[32 * g:32 * g + 32, rounds, :], src[g][rounds].partition_broadcast(32))
                    for g in range(4)]

        row_loads = [
            (vecrows[0:KD, :], c_in[0].rearrange("(k p) -> k p", p=P)),
            (vecrows[KD:3 * KD, :], mix_g.rearrange("l (k p) -> (l k) p", p=P)),
            (vecrows[3 * KD:5 * KD, :], ffn_g.rearrange("l (k p) -> (l k) p", p=P)),
        ]
        const_loads = [
            (pos_i[:], positions[0].rearrange("(t p) -> p t", p=P)),
            (inv[:], inv_freq[0].partition_broadcast(P)),
            (sinks[:], sink.rearrange("l h -> (l h)").partition_broadcast(P)),
            (subg[:], subln_g.rearrange("l n -> (l n)").partition_broadcast(P)),
        ] + [(lamv[:, i, :], lam.rearrange("l n -> (l n)").partition_broadcast(P))
             for i, lam in enumerate((lam_q1, lam_k1, lam_q2, lam_k2))]
        CONSTS = 16 * len(const_loads)
        SETUP = 9

        ada_v = ada_w.rearrange("l (q k p) (r n) -> l r q p k n", k=2, p=P, r=3)
        in_v = w_in.rearrange("l (k p) n -> l p k n", p=P)
        out_v = w_out.rearrange("l (k p) n -> l p k n", p=P)

        def ff_views(g, u, d):
            return (g.rearrange("e (k p) (j n) -> e j p k n", p=P, n=BLOCK),
                    u.rearrange("e (k p) (j n) -> e j p k n", p=P, n=BLOCK),
                    d.rearrange("e (j k p) n -> e j p k n", p=P, k=BLOCK // P))

        dense_v, moe_v = ff_views(w_gate, w_up, w_down), ff_views(moe_gate[0], moe_up[0], moe_down[0])

        hg_ff = [t[:].rearrange("p c (k g n) -> p c k g n", k=4, g=2) for t in (Hg, Lg)]
        hd_ff = [t[:].rearrange("p (k n) -> p k n", n=D) for t in (Hd, Ld)]

        def low_columns(off, n, pool):
            return slice(off + n * 11 // 16, off + n) if pool else slice(off, off + n * 11 // 16)

        def halves(hslot):
            return (Hg[:, hslot, :], Lg[:, hslot, :]) if hslot < 2 else (Hd[:], Ld[:])

        def straight_parts(kind, layer, c):
            base = IN_BASE[layer] + 2 * c + (IN_PARTS if kind == "out" else 0)
            n = PART if kind == "out" or c < IN_CHUNKS - 1 else PART // 2
            i = c + (IN_CHUNKS if kind == "out" else 0)
            hslot = 2 if (kind, c) == ("out", 1) else i % 2
            for h in range(2):
                if hslot == 2:
                    freed = 0
                elif i >= 2:
                    freed = base + h - 3
                elif layer:
                    freed = FF_BASE[0] + PARTS * (NB - 1) + 2 * i + h + 1
                else:
                    freed = 0
                yield base + h, plan[(kind, layer, c)][0], hslot, h * n, n, freed

        block = ctx.enter_context(nc.Block())

        NEW_KINDS = [[(0, (0, 2))], [(0, (2, 6)), (1, (0, 2))], [(1, (2, 6))]]

        GU0 = {4: 0, 2: 3 * NB}
        U0 = {4: 0, 2: 4 * NB}

        @block.sync
        def _(sp):
            def free(holder):
                if holder is None:
                    return
                what, value = holder
                if what == "ada":
                    sp.wait_ge(ada_used, value)
                else:
                    sp.wait_ge(hi_done, value)
                    sp.wait_ge(lo_done, value)
                    sp.wait_ge(lop_done, value)

            def load(name, dst, src):
                slot, holder, _ = plan[name]
                free(holder)
                sp.dma_start(dst, src).then_inc(w_loaded[slot], 16)

            def ada(chunks):
                for layer, n in chunks:
                    slot = plan[("ada", layer, n)][0]
                    load(("ada", layer, n), W[:, slot, :].rearrange("p (k n) -> p k n", k=2),
                         ada_v[layer, n // 4, n % 4])

            def columns_in(layer):
                for c in range(IN_CHUNKS):
                    n = 512 if c < IN_CHUNKS - 1 else 256
                    slot = plan[("in", layer, c)][0]
                    load(("in", layer, c), W[:, slot, 0:KD * n].rearrange("p (k n) -> p k n", k=KD),
                         in_v[layer, :, :, 512 * c:512 * c + n])

            def columns_out(layer, c):
                slot = plan[("out", layer, c)][0]
                load(("out", layer, c), W[:, slot, :].rearrange("p (k n) -> p k n", k=KD),
                     out_v[layer, :, :, 512 * c:512 * c + 512])

            def mixer(layer):
                columns_in(layer)
                columns_out(layer, 0)
                ada(ADA_LATER[layer])
                columns_out(layer, 1)

            def blocks(views, e, base, first):
                gate_v, up_v, down_v = views
                with sp.Fori(0, NB) as j:
                    for c in range(2):
                        value = (first + j) * PARTS + (base - PARTS + 2 * c + 2)
                        sp.wait_ge(hi_done, value)
                        sp.wait_ge(lo_done, value)
                        sp.wait_ge(lop_done, value)
                        dst = W[:, c, :].rearrange("p (k g n) -> p k g n", k=4, g=2)
                        for g, view in enumerate((gate_v, up_v)):
                            src = view[bass.ds(e, 1), bass.ds(j, 1), :, 4 * c:4 * c + 4, :]
                            sp.dma_start(dst[:, :, g, :], src.rearrange("a b p k n -> p (a b k) n")).then_inc(
                                w_loaded[c], 16)
                    value = (first + j) * PARTS + base
                    sp.wait_ge(hi_done, value)
                    sp.wait_ge(lo_done, value)
                    sp.wait_ge(lop_done, value)
                    src = down_v[bass.ds(e, 1), bass.ds(j, 1), :, :, :]
                    sp.dma_start(W[:, 2, :].rearrange("p (k n) -> p k n", n=D),
                                 src.rearrange("a b p k n -> p (a b k) n")).then_inc(w_loaded[2], 16)

            for dst, src in row_loads:
                sp.dma_start(dst, src).then_inc(rows_loaded, 16)
            ada([(0, n) for n in range(ADA_FIRST)])
            mixer(0)
            sp.wait_ge(ada_used, ADA_CHUNKS + ADA_FIRST)
            blocks(dense_v, 0, FF_BASE[0], 0)
            mixer(1)
            sp.wait_ge(ada_used, 2 * ADA_CHUNKS)
            with sp.Fori(0, N_EXP) as s:
                blocks(moe_v, s, FF_BASE[1], s * NB)
            sp.wait_ge(table_ready, 1)
            with sp.Fori(0, MAX_OVER) as o:
                used = sp.value_load(table[0:1, 1, bass.ds(o, 1)], min_val=0, max_val=1)
                with sp.If(used > 0):
                    e = sp.value_load(table[0:1, 0, bass.ds(o, 1)], min_val=0, max_val=N_EXP - 1)
                    blocks(moe_v, e, FF_BASE[1], (o + N_EXP) * NB)
            for i, t in enumerate(tiles_of(2 * DEPTH)):
                sp.wait_ge(out_ready, i + 1)
                sp.dma_start(out[0, t * P:t * P + P, :], xn[:, t, :]).then_inc(out_written, 16)
            sp.wait_ge(out_written, 16 * NT)

        @block.gpsimd
        def _(pool):
            pool.memset(ident[:], 0.0).then_inc(setup_done, 1)
            pool.memset(mask[:], 0.0).then_inc(setup_done, 1)
            pool.memset(ones[:], 1.0).then_inc(setup_done, 1)
            pool.memset(half_neg[:], -0.5).then_inc(setup_done, 1)
            pool.wait_ge(setup_done, 4)
            pool.affine_select(out=ident[:], in_=ident[:], compare_op=ALU.not_equal, fill=1.0, base=0,
                               pattern=[[-1, P]], channel_multiplier=1).then_inc(setup_done, 1)
            pool.affine_select(out=before[:], in_=ones[:], compare_op=ALU.is_gt, fill=0.0, base=0,
                               pattern=[[1, P]], channel_multiplier=-1).then_inc(setup_done, 1)
            pool.affine_select(out=mask[:, 0, P:], in_=mask[:, 0, P:], compare_op=ALU.is_ge, fill=MASKED,
                               base=0, pattern=[[-1, P]], channel_multiplier=1).then_inc(setup_done, 1)
            pool.affine_select(out=mask[:, 1, :P], in_=mask[:, 1, :P], compare_op=ALU.is_ge, fill=MASKED,
                               base=0, pattern=[[1, P]], channel_multiplier=-1).then_inc(setup_done, 1)
            pool.iota(iota_row[:], pattern=[[1, P]], base=0, channel_multiplier=0,
                      allow_small_or_imprecise_dtypes=True).then_inc(setup_done, 1)

            def low(q, wslot, hslot, off, n):
                at = low_columns(off, n, True)
                hi, lo = halves(hslot)
                pool.wait_ge(hi_done, q + 1)
                pool.tensor_tensor(lo[:, at], W[:, wslot, at], hi[:, at].bitcast(F32),
                                   ALU.subtract).then_inc(lop_done, 1)

            def straight(kind, layer, c):
                for q, wslot, hslot, off, n, _ in straight_parts(kind, layer, c):
                    low(q, wslot, hslot, off, n)

            def low_part(base, b, i):
                low(b * PARTS + (base + i), i // 2, i // 2, (i % 2) * PART, PART)

            def blocks(base, first):
                with pool.Fori(0, NB - 1) as j:
                    for i in range(4, PARTS):
                        low_part(base, first + j, i)
                    for i in range(4):
                        low_part(base, first + (j + 1), i)
                for i in range(4, PARTS):
                    low_part(base, first + (NB - 1), i)

            def first_parts(base, b):
                for i in range(4):
                    low_part(base, b, i)

            def norm(n):
                for i, t in enumerate(tiles_of(n)):
                    pool.wait_ge(ms_done, NT * n + i + 1)
                    pool.tensor_tensor(rstd[:, t:t + 1], ms[:, t:t + 1], half_neg[:, 0:1], ALU.pow).then_inc(
                        rstd_done, 1)

            for layer in range(DEPTH):
                if layer:
                    straight("in", layer, 0)
                norm(2 * layer)
                for c in range(1 if layer else 0, IN_CHUNKS):
                    straight("in", layer, c)
                straight("out", layer, 0)
                for t in range(NT):
                    pool.wait_ge(dms_done, NT * layer + t + 1)
                    four = slice(N_DIFF * t, N_DIFF * t + N_DIFF)
                    pool.tensor_tensor(rstd_d[:, four], ms_d[:, four], half_neg[:, four],
                                       ALU.pow).then_inc(drstd_done, 1)
                straight("out", layer, 1)
                first_parts(FF_BASE[layer], 0)
                norm(2 * layer + 1)
                if layer == 0:
                    blocks(FF_BASE[0], 0)
            with pool.Fori(0, N_EXP - 1) as s:
                blocks(FF_BASE[1], s * NB)
                first_parts(FF_BASE[1], s * NB + NB)
            blocks(FF_BASE[1], (N_EXP - 1) * NB)
            pool.wait_ge(table_ready, 1)
            with pool.Fori(0, MAX_OVER) as o:
                used = pool.value_load(table[0:1, 1, bass.ds(o, 1)], min_val=0, max_val=1)
                with pool.If(used > 0):
                    first_parts(FF_BASE[1], (o + N_EXP) * NB)
                    blocks(FF_BASE[1], (o + N_EXP) * NB)
            norm(4)

        @block.scalar
        def _(act):
            for t in range(NT):
                act.dma_start(x[:, t, :], x_in[0, t * P:t * P + P, :]).then_inc(x_loaded, 16)
            for dst, src in bias_loads(0, slice(0, 1)):
                act.dma_start(dst, src).then_inc(bias_loaded, 16)
            for dst, src in const_loads:
                act.dma_start(dst, src, allow_slow_non_contiguous=True).then_inc(consts_loaded, 16)
            act.wait_ge(rows_loaded, 16 * len(row_loads))
            act.activation(vecrows[0:KD, :], vecrows[0:KD, :], ACT.Silu).then_inc(vec_silu, 1)

            def high(q, wslot, hslot, off, n, loaded, freed):
                act.wait_ge(w_loaded[wslot], loaded)
                if not isinstance(freed, int) or freed > 0:
                    act.wait_ge(parts_used, freed)
                act.activation(halves(hslot)[0][:, off:off + n], W[:, wslot, off:off + n],
                               ACT.Copy).then_inc(hi_done, 1)

            def straight(kind, layer, c):
                for q, wslot, hslot, off, n, freed in straight_parts(kind, layer, c):
                    high(q, wslot, hslot, off, n, plan[(kind, layer, c)][2], freed)

            def square(n):
                done, first, step = ((x_loaded, 16 * NT, 0), (x_mixed, 3, 1), (x_ffn, 2, 2), (x_mixed, 7, 1),
                                     (moe_done, 1, 1))[n]
                for i, t in enumerate(tiles_of(n)):
                    act.wait_ge(done, first + i * step)
                    act.activation(xn[:, t, :], x[:, t, :], ACT.Square,
                                   accum_out=ssq[:, t:t + 1]).then_inc(sq_done, 1)

            def split_transposed(n):
                for kk in range(KD // 2):
                    act.wait_ge(tr_copied, 4 * n + kk + 1)
                    act.activation(hTh[:, 2 * kk:2 * kk + 2, :],
                                   tmp[:, kk % 2, :].rearrange("p (k n) -> p k n", k=2),
                                   ACT.Copy).then_inc(tr_hi, 1)

            def gates(layer):
                for i in range(4):
                    act.wait_ge(gates_ps, 4 * layer + i + 1)
                    act.activation(gate[:, i // 2, (i % 2) * 512:(i % 2) * 512 + 512], ps[:, 4 + i, :],
                                   ACT.Copy).then_inc(gates_ready, 1)

            def attention(layer):
                for m in range(0, QK_TILES // 2, 2):
                    act.wait_ge(qkT_ps, 7 * layer + m + 1)
                    act.activation(qkT[:, 2 * m:2 * m + 2, :], ps[:, 2, :].rearrange("p (m n) -> p m n", m=2),
                                   ACT.Copy).then_inc(qkT_even, 1)
                for i in range(UNITS + 2):
                    if i % 8 == 0 and i:
                        t = i // 8 - 1
                        act.wait_ge(o_done, UNITS * layer + 8 * t + 4)
                        for h in range(N_DIFF):
                            at = WIN_WIDTH + h * P
                            act.activation(qk[:, t, h * P:h * P + P], xn[:, t, at:at + P], ACT.Square,
                                           accum_out=ssq_d[:, N_DIFF * t + h:N_DIFF * t + h + 1]).then_inc(dsq_done, 1)
                    if i < UNITS:
                        u, par, q, m = UNITS * layer + i, i % 2, i % 4, pair(i)
                        act.wait_ge(max_done, u + 1)
                        if i >= 2:
                            act.wait_ge(pt_ps, u - 1)
                        for h in range(2):
                            src = scores[:, par, h, :] if m < 4 else ps[:, 4 + 2 * par + h, 0:SEQ]
                            e = act.activation(E[:, par, h, :], src, ACT.Exp, bias=negm[:, q, h:h + 1],
                                               scale=SCALE, accum_out=sums[:, q, h:h + 1])
                        if m < 4:
                            e = act.activation(sinke[:, q, :], sinkm[:, q, :], ACT.Exp)
                        e.then_inc(exp_done, 1)
                    if i >= 2:
                        u, par, m = UNITS * layer + i - 2, i % 2, pair(i - 2)
                        n = 4 if m < 4 else 2
                        act.wait_ge(pt_ps, u + 1)
                        if i >= 4:
                            act.wait_ge(o_ps, u - 1)
                        act.activation(PT[:, par, 0:n, :], ps[:, 3, 0:n * P].rearrange("p (k n) -> p k n", k=n),
                                       ACT.Copy).then_inc(pt_done, 1)

            def high_part(base, loads, b, i):
                per = 32 if i < 4 else 16
                high(None, i // 2, i // 2, (i % 2) * PART, PART,
                     b * per + (loads[i // 2] + per), b * PARTS + (base + i - 5))

            def blocks(base, first, loads, nu, split=True, follows=False, ahead=None, mid=None, last=None):
                part = lambda b, i: high_part(base, loads, b, i)

                def silu(b, i):
                    if i < nu - 1:
                        act.wait_ge(gu_ps, b * (nu - 1) + (GU0[nu] + i + 1))
                    else:
                        act.wait_ge(parts_used, b * PARTS + (base + 4))
                    act.activation(sg[:, i % 2, :], ps[:, 4 + i % 2, 0:HB], ACT.Silu).then_inc(silu_done, 1)

                def turned(b, i):
                    act.wait_ge(at_ps, b * nu + (U0[nu] + i + 1))
                    act.activation(aTh[:, i % 2, :, :],
                                   ps[:, 6 + i % 2, 0:2 * P].rearrange("p (k n) -> p k n", k=2),
                                   ACT.Copy).then_inc(at_hi, 1)

                def one(b, is_first, is_last):
                    whole = is_first and not split
                    more = follows or not is_last
                    if whole:
                        for i in range(4):
                            part(b, i)
                        silu(b, 0)
                        part(b, 4)
                    else:
                        part(b, 4)
                        part(b, 5)
                        if is_last and ahead:
                            ahead()
                        silu(b, 0)
                    if is_last and mid:
                        mid()
                    for i in range(1, nu - 1):
                        turned(b, i - 1)
                        silu(b, i)
                    if whole:
                        turned(b, nu - 2)
                        part(b, 5)
                    if more:
                        part(b + 1, 0)
                    if not whole:
                        turned(b, nu - 2)
                    if more:
                        part(b + 1, 1)
                    silu(b, nu - 1)
                    if is_last and last:
                        last()
                    if more and not is_last:
                        part(b + 1, 2)
                    turned(b, nu - 1)
                    if more and is_last:
                        part(b + 1, 2)
                    if more:
                        part(b + 1, 3)

                one(first + 0, True, False)
                with act.Fori(0, NB - 2) as j:
                    one(first + (j + 1), False, False)
                one(first + (NB - 1), False, True)

            def gathered(n):
                act.wait_ge(gather_ps, n)
                for k in range(KD):
                    a = act.activation(xsT[:, k, :], ps[:, 2 + k // 4, (k % 4) * P:(k % 4) * P + P], ACT.Identity,
                                       bias=modc[:, 1, 3, k:k + 1], scale=A[:, 1, 1, k:k + 1])
                a.then_inc(xs_ready, 1)
                act.wait_ge(xs_ready, n)

            def input_high():
                act.activation(hTh[:, :, 0:P], xsT[:], ACT.Copy).then_inc(slot_hi, 1)

            def slot(s, split, follows):
                def turned_rows():
                    act.wait_ge(pickT_ps, s + 1)
                    act.activation(pickT[:], ps[:, 2, 0:NT * P].rearrange("p (t n) -> p t n", t=NT),
                                   ACT.Copy).then_inc(pickT_ready, 1)
                    act.wait_ge(slot_lo, s + 1)

                blocks(FF_BASE[1], s * NB, plan["experts"], 2, split, follows,
                       turned_rows, lambda: gathered(s + 2), input_high)

            square(0)
            act.wait_ge(arg_ready, 1)
            act.activation(cosF[:, :, 0, :], arg[:, 1], ACT.Sin).then_inc(sin_done, 1)
            act.activation(cosF[:, :, 1, :], arg[:, 1], ACT.Sin).then_inc(sin_done, 1)
            act.activation(sinS[:, :, 1, :], arg[:, 0], ACT.Sin).then_inc(sin_done, 1)
            act.wait_ge(lam_dot, 1)
            act.activation(lame[:], lams[:], ACT.Exp).then_inc(lam_exp, 1)
            for layer in range(DEPTH):
                straight("in", layer, 0)
                if layer:
                    square(2 * layer)
                split_transposed(3 * layer)
                for c in range(1, IN_CHUNKS):
                    straight("in", layer, c)
                    if not layer and c == 1:
                        for dst, src in bias_loads(0, slice(1, 3)):
                            act.dma_start(dst, src).then_inc(bias_loaded, 16)
                        act.dma_start(rw[:], router_w[0].rearrange("(k p) e -> p k e", p=P)).then_inc(late_loaded, 16)
                        act.dma_start(fing[:], final_g.partition_broadcast(P)).then_inc(late_loaded, 16)
                straight("out", layer, 0)
                if not layer:
                    act.wait_ge(cols_ps, 1)
                    act.wait_ge(bias_loaded, 128)
                    for dst, src in bias_loads(1, slice(0, 1)):
                        act.dma_start(dst, src).then_inc(bias_loaded, 16)
                attention(layer)
                split_transposed(3 * layer + 1)
                gates(layer)
                if not layer:
                    act.wait_ge(late_loaded, 32)
                    act.activation(rwh[:], rw[:], ACT.Copy).then_inc(rw_hi, 1)
                    act.wait_ge(cols_ps, 2)
                    for dst, src in bias_loads(1, slice(1, 3)):
                        act.dma_start(dst, src).then_inc(bias_loaded, 16)
                straight("out", layer, 1)
                act.wait_ge(parts_used, OUT_BASE[layer])
                for i in range(4):
                    high_part(FF_BASE[layer], plan["experts" if layer else "dense"], 0, i)
                square(2 * layer + 1)
                split_transposed(3 * layer + 2)
                if not layer:
                    blocks(FF_BASE[0], 0, plan["dense"], 4)
                else:
                    act.wait_ge(gap_ready, 1)
                    act.activation(edl[:], dlt[:], ACT.Exp).then_inc(gap_exp, 1)
            gathered(1)
            input_high()
            slot(0, True, True)
            with act.Fori(0, N_EXP - 2) as s:
                slot(s + 1, True, True)
            slot(N_EXP - 1, True, False)
            act.wait_ge(table_ready, 1)
            with act.Fori(0, MAX_OVER) as o:
                used = act.value_load(table[0:1, 1, bass.ds(o, 1)], min_val=0, max_val=1)
                with act.If(used > 0):
                    slot(o + N_EXP, False, False)
            square(4)

        @block.vector
        def _(dve):
            step = Count(dve_step)

            def then(instruction):
                dve.wait_ge(dve_step, step.mark(instruction))

            def low(q, wslot, hslot, off, n):
                at = low_columns(off, n, False)
                hi, lo = halves(hslot)
                dve.wait_ge(hi_done, q + 1)
                dve.tensor_tensor(lo[:, at], W[:, wslot, at], hi[:, at].bitcast(F32),
                                  ALU.subtract).then_inc(lo_done, 1)

            def straight(kind, layer, c):
                for q, wslot, hslot, off, n, _ in straight_parts(kind, layer, c):
                    low(q, wslot, hslot, off, n)

            def setup():
                dve.wait_ge(consts_loaded, CONSTS)
                then(dve.tensor_copy(pos_f[:], pos_i[:]))
                for t in range(NT):
                    i = dve.tensor_scalar(ang[:, t, :], inv[:], pos_f[:, t:t + 1], None, ALU.mult)
                then(i)
                for which, quarter in ((0, 0.0), (1, 0.25)):
                    then(dve.tensor_scalar(turns[:], ang[:], 1.0 / (2 * math.pi), quarter, ALU.mult, ALU.add))
                    then(dve.tensor_scalar(turns[:], turns[:], ROUNDER, None, ALU.add))
                    then(dve.tensor_scalar(turns[:], turns[:], -ROUNDER, None, ALU.add))
                    src = ang[:]
                    for part in TWO_PI_PARTS:
                        then(dve.scalar_tensor_tensor(out=arg[:, which], in0=turns[:], scalar=-part, in1=src,
                                                      op0=ALU.mult, op1=ALU.add))
                        src = arg[:, which]
                    then(dve.tensor_scalar(arg[:, which], src, quarter * 2 * math.pi, None, ALU.add))
                    i = dve.tensor_scalar(arg[:, which], src, 3.1415925, -3.1415925, ALU.min, ALU.max)
                    if which:
                        i.then_inc(arg_ready, 1)
                    else:
                        then(i)
                for i in range(2):
                    then(dve.tensor_tensor(lamv[:, 2 * i, :], lamv[:, 2 * i, :], lamv[:, 2 * i + 1, :], ALU.mult))
                    last = dve.reduce_sum(lams[:, i, :], lamv[:, 2 * i, :].rearrange("p (l n) -> p l n", l=DEPTH), AX_X)
                last.then_inc(lam_dot, 1)
                dve.wait_ge(lam_exp, 1)
                then(dve.tensor_tensor(neglam[:], lame[:, 1, :], lame[:, 0, :], ALU.subtract))
                for layer in range(DEPTH):
                    start = 0.8 - 0.6 * math.exp(-0.3 * layer)
                    dve.tensor_scalar(neglam[:, layer:layer + 1], neglam[:, layer:layer + 1], -start, None, ALU.add)
                    dve.tensor_scalar(subgs[:, layer, :], subg[:, layer, :], 1.0 - start, None, ALU.mult)
                dve.tensor_scalar(negsink[:], sinks[:], -1.0, None, ALU.mult)
                dve.wait_ge(sin_done, 3)
                then(dve.tensor_scalar(sinS[:, :, 0, :], sinS[:, :, 1, :], -1.0, None, ALU.mult))

            def columns():
                dve.wait_ge(vec_ps, 1)
                then(dve.tensor_copy(vcols[:], ps[:, 3, 0:40]))
                dve.tensor_copy(c_rep[:], vcols[:, 0:KD].unsqueeze(2).broadcast_to([P, KD, 32])).then_inc(vec_cols, 1)

            def mod_round(layer, r):
                dve.wait_ge(ada_used, ADA_CHUNKS * layer + 4 * r + 4)
                dve.wait_ge(bias_loaded, 64 * (1 + 2 * layer + (1 if r else 0)))
                dve.tensor_tensor(modrow[:, r, :], ps[:, 2, :], modrow[:, r, :], ALU.add).then_inc(mod_ready, 1)

            def mod_columns(n):
                dve.wait_ge(cols_ps, n + 1)
                for layer, (a, b) in NEW_KINDS[n]:
                    i = dve.tensor_copy(modc[:, layer, a:b], ps[:, 0, KD * a:KD * b].rearrange(
                        "p (a k) -> p a k", a=b - a))
                then(i)
                for layer, (a, b) in NEW_KINDS[n]:
                    f = 0 if a == 0 else 1
                    g = KD * (1 + 2 * f + layer)
                    i = dve.scalar_tensor_tensor(out=A[:, layer, f, :], in0=modc[:, layer, 3 * f + 1, :], scalar=1.0,
                                                 in1=vcols[:, g:g + KD], op0=ALU.add, op1=ALU.mult)
                i.then_inc(cols_ready, 1)
                dve.wait_ge(cols_ready, n + 1)

            def normalise(n):
                for i, t in enumerate(tiles_of(n)):
                    dve.wait_ge(sq_done, NT * n + i + 1)
                    dve.tensor_scalar(ms[:, t:t + 1], ssq[:, t:t + 1], 1.0 / D, EPS, ALU.mult,
                                      ALU.add).then_inc(ms_done, 1)
                for i, t in enumerate(tiles_of(n)):
                    dve.wait_ge(rstd_done, NT * n + i + 1)
                    if n < 4:
                        dve.tensor_scalar(xn[:, t, :], x[:, t, :], rstd[:, t:t + 1], None, ALU.mult).then_inc(xn_done, 1)
                    else:
                        dve.scalar_tensor_tensor(out=xn[:, t, :], in0=x[:, t, :], scalar=rstd[:, t:t + 1],
                                                 in1=fing[:], op0=ALU.mult, op1=ALU.mult).then_inc(out_ready, 1)

            def split_transposed(n, f):
                for kk in range(KD // 2 + 1):
                    if kk < KD // 2:
                        dve.wait_ge(tr_ps, 4 * n + kk + 1)
                        if kk >= 2:
                            dve.wait_ge(tr_hi, 4 * n + kk - 1)
                            dve.wait_ge(tr_lo, 4 * n + kk - 1)
                        if f is None:
                            i = dve.tensor_copy(tmp[:, kk % 2, :], ps[:, 2 + kk % 2, :])
                        else:
                            for h in range(2):
                                k = 2 * kk + h
                                i = dve.tensor_scalar(tmp[:, kk % 2, h * SEQ:h * SEQ + SEQ],
                                                      ps[:, 2 + kk % 2, h * SEQ:h * SEQ + SEQ],
                                                      A[:, n // 3, f, k:k + 1], modc[:, n // 3, 3 * f, k:k + 1],
                                                      ALU.mult, ALU.add)
                        i.then_inc(tr_copied, 1)
                    if kk:
                        kp = kk - 1
                        dve.wait_ge(tr_hi, 4 * n + kp + 1)
                        dve.tensor_tensor(hTl[:, 2 * kp:2 * kp + 2, :],
                                          tmp[:, kp % 2, :].rearrange("p (k n) -> p k n", k=2),
                                          hTh[:, 2 * kp:2 * kp + 2, :].bitcast(F32), ALU.subtract).then_inc(tr_lo, 1)

            def rope(layer, c, t):
                if t == 0:
                    dve.wait_ge(proj_ps, IN_CHUNKS * layer + c + 1)
                else:
                    dve.wait_ge(parts_used, IN_BASE[layer] + 2 * c + 2)
                bank = ps[:, (2 * c + t) % 2, :]
                done = 2 * (IN_CHUNKS * layer + c) + t
                if done:
                    dve.wait_ge(rope_done, done)
                last = None
                for col, heads, tile in ROPE_GROUPS[c]:
                    if last is not None:
                        then(last)
                    src = bank[:, col:col + heads * HEAD].rearrange("p (h a n) -> p h a n", h=heads, a=2)
                    a = rope_a[:, 0:heads * HEAD].rearrange("p (h a n) -> p h a n", h=heads, a=2)
                    b = rope_b[:, 0:heads * HEAD].rearrange("p (h a n) -> p h a n", h=heads, a=2)
                    wide = [P, heads, HALF]
                    for s in range(2):
                        dve.tensor_tensor(a[:, :, s, :], src[:, :, s, :],
                                          cosF[:, t, s, :].unsqueeze(1).broadcast_to(wide), ALU.mult)
                        i = dve.tensor_tensor(b[:, :, s, :], src[:, :, 1 - s, :],
                                              sinS[:, t, s, :].unsqueeze(1).broadcast_to(wide), ALU.mult)
                    then(i)
                    last = dve.tensor_tensor(qk[:, t, tile * P:tile * P + heads * HEAD],
                                             rope_a[:, 0:heads * HEAD], rope_b[:, 0:heads * HEAD], ALU.add)
                    if tile == 4:
                        for h in range(2):
                            at = (tile + 1) * P + (1 - h) * HEAD
                            last = dve.tensor_tensor(qk[:, t, at:at + HEAD], rope_a[:, h * HEAD:h * HEAD + HEAD],
                                                     rope_b[:, h * HEAD:h * HEAD + HEAD], ALU.add)
                for col, n, to in V_GROUPS[c]:
                    last = dve.tensor_copy(v[:, t, to:to + n], bank[:, col:col + n])
                last.then_inc(rope_done, 1)

            def maxima(layer, i):
                u, par, q, m, t = UNITS * layer + i, i % 2, i % 4, pair(i), i // 8
                dve.wait_ge(s_ps, u + 1)
                raw = ps[:, 4 + 2 * par:6 + 2 * par, 0:SEQ]
                if m < 4:
                    h = N_WIN * layer + 2 * m
                    then(dve.tensor_tensor(scores[:, par], raw, mask[:, t, :].unsqueeze(1).broadcast_to([P, 2, SEQ]),
                                           ALU.add))
                    then(dve.reduce_max(mx[:, q, :], scores[:, par], AX_X))
                    then(dve.scalar_tensor_tensor(out=negm[:, q, :], in0=mx[:, q, :], scalar=-SCALE,
                                                  in1=negsink[:, h:h + 2], op0=ALU.mult, op1=ALU.min))
                    dve.tensor_tensor(sinkm[:, q, :], sinks[:, h:h + 2], negm[:, q, :],
                                      ALU.add).then_inc(max_done, 1)
                else:
                    then(dve.reduce_max(mx[:, q, :], raw, AX_X))
                    dve.tensor_scalar(negm[:, q, :], mx[:, q, :], -SCALE, None, ALU.mult).then_inc(max_done, 1)

            def probabilities(layer, i):
                u, par, q, m = UNITS * layer + i, i % 2, i % 4, pair(i)
                dve.wait_ge(exp_done, u + 1)
                if u >= 4:
                    dve.wait_ge(o_done, u - 3)
                if m < 4:
                    then(dve.tensor_tensor(den[:, q, :], sums[:, q, :], sinke[:, q, :], ALU.add))
                    dve.reciprocal(rec[:, q, :], den[:, q, :]).then_inc(probs_done, 1)
                else:
                    then(dve.reciprocal(rec[:, q, :], sums[:, q, :]))
                    then(dve.scalar_tensor_tensor(out=nl[:, q:q + 1], in0=sums[:, q, 0:1],
                                                  scalar=rec[:, q, 1:2], in1=neglam[:, layer:layer + 1],
                                                  op0=ALU.mult, op1=ALU.mult))
                    dve.scalar_tensor_tensor(out=E[:, par, 0, :], in0=E[:, par, 1, :], scalar=nl[:, q:q + 1],
                                             in1=E[:, par, 0, :], op0=ALU.mult, op1=ALU.add).then_inc(probs_done, 1)

            def head_out(layer, i):
                u, par, q, m, t = UNITS * layer + i, i % 2, i % 4, pair(i), i // 8
                dve.wait_ge(o_ps, u + 1)
                dst = xn[:, t, m * P:m * P + P]
                if m < 4:
                    i = dve.tensor_tensor(dst.rearrange("p (h n) -> p h n", h=2),
                                          ps[:, par, 0:P].rearrange("p (h n) -> p h n", h=2),
                                          rec[:, q, :].unsqueeze(2).broadcast_to([P, 2, HEAD]), ALU.mult)
                else:
                    i = dve.tensor_scalar(dst, ps[:, par, 0:P], rec[:, q, 0:1], None, ALU.mult)
                i.then_inc(o_done, 1)

            def attention(layer):
                for m in range(1, QK_TILES // 2, 2):
                    dve.wait_ge(qkT_ps, 7 * layer + m + 1)
                    dve.tensor_copy(qkT[:, 2 * m:2 * m + 2, :],
                                    ps[:, 3, :].rearrange("p (m n) -> p m n", m=2)).then_inc(qkT_odd, 1)
                for i in range(UNITS + 3):
                    if i < UNITS:
                        maxima(layer, i)
                    if 1 <= i <= UNITS:
                        probabilities(layer, i - 1)
                    if i >= 3:
                        head_out(layer, i - 3)
                    if i % 8 == 1 and i > 1:
                        t = i // 8 - 1
                        dve.wait_ge(dsq_done, N_DIFF * (NT * layer + t + 1))
                        four = slice(N_DIFF * t, N_DIFF * t + N_DIFF)
                        dve.tensor_scalar(ms_d[:, four], ssq_d[:, four], 1.0 / P, EPS, ALU.mult,
                                          ALU.add).then_inc(dms_done, 1)
                    if i % 8 == 2 and i > 2:
                        t = i // 8 - 1
                        dve.wait_ge(drstd_done, NT * layer + t + 1)
                        for h in range(N_DIFF):
                            o = xn[:, t, WIN_WIDTH + h * P:WIN_WIDTH + h * P + P]
                            n = N_DIFF * t + h
                            dve.scalar_tensor_tensor(out=o, in0=o, scalar=rstd_d[:, n:n + 1],
                                                     in1=subgs[:, layer, :], op0=ALU.mult,
                                                     op1=ALU.mult).then_inc(mix_done, 1)
                    for k, (of, n) in enumerate(ADA_LATER[layer]):
                        if n % 4 == 3 and ADA_STEP[k] + 1 == i:
                            mod_round(of, n // 4)
                if ADA_STEP[len(ADA_LATER[layer]) - 1] == UNITS + 2:
                    mod_round(ADA_LATER[layer][-1][0], ADA_LATER[layer][-1][1] // 4)

            def mixed(layer):
                low_part(FF_BASE[layer], 0, 0)
                low_part(FF_BASE[layer], 0, 1)
                for c in range(OUT_CHUNKS):
                    for t in range(NT):
                        if t == 0:
                            dve.wait_ge(wo_ps, OUT_CHUNKS * layer + c + 1)
                        else:
                            dve.wait_ge(parts_used, OUT_BASE[layer] + 2 * c + 2)
                        cols = slice(512 * c, 512 * c + 512)
                        then(dve.tensor_tensor(tmp[:, t, :], ps[:, 4 + 2 * c + t, :], gate[:, 0, cols], ALU.mult))
                        dve.tensor_tensor(x[:, t, cols], x[:, t, cols], tmp[:, t, :], ALU.add).then_inc(x_mixed, 1)
                    if c == 0:
                        low_part(FF_BASE[layer], 0, 2)
                        low_part(FF_BASE[layer], 0, 3)

            def low_part(base, b, i):
                low(b * PARTS + (base + i), i // 2, i // 2, (i % 2) * PART, PART)

            def blocks(base, first, nu, split=True, follows=False, summed=None, earlier=None, later=None,
                       spread=None, ahead=None):
                part = lambda b, i: low_part(base, b, i)

                def gated(b, i):
                    dve.wait_ge(silu_done, b * nu + (U0[nu] + i + 1))
                    dve.tensor_tensor(act_sb[:, i % 2, :], sg[:, i % 2, :], ps[:, 4 + i % 2, HB:2 * HB],
                                      ALU.mult).then_inc(act_done, 1)

                def turned(b, i):
                    dve.wait_ge(at_hi, b * nu + (U0[nu] + i + 1))
                    dve.tensor_tensor(aTl[:, i % 2, :, :],
                                      ps[:, 6 + i % 2, 0:2 * P].rearrange("p (k n) -> p k n", k=2),
                                      aTh[:, i % 2, :, :].bitcast(F32), ALU.subtract).then_inc(at_lo, 1)

                def one(b, is_first, is_last, j=None):
                    whole = is_first and not split
                    more = follows or not is_last
                    if whole:
                        for i in range(4):
                            part(b, i)
                        gated(b, 0)
                        if earlier:
                            earlier()
                        part(b, 4)
                    else:
                        part(b, 4)
                        if is_first and earlier:
                            earlier()
                        part(b, 5)
                        gated(b, 0)
                        if spread and j is not None:
                            spread(j)
                    for i in range(1, nu - 1):
                        turned(b, i - 1)
                        gated(b, i)
                    turned(b, nu - 2)
                    if whole:
                        part(b, 5)
                    if more:
                        part(b + 1, 0)
                    gated(b, nu - 1)
                    if is_first and summed:
                        summed()
                    if more:
                        part(b + 1, 1)
                    turned(b, nu - 1)
                    if is_first and later:
                        later()
                    if is_last and ahead:
                        ahead()
                    if more:
                        part(b + 1, 2)
                        part(b + 1, 3)

                one(first + 0, True, False)
                with dve.Fori(0, SPREAD) as j:
                    one(first + (j + 1), False, False, j)
                for n in range(SPREAD + 1, NB - 1):
                    one(first + n, False, False)
                one(first + (NB - 1), False, True)

            def dense_out():
                for t in range(NT):
                    if t == 0:
                        dve.wait_ge(tile_ps, 1)
                    else:
                        dve.wait_ge(parts_used, FF_BASE[0] + NB * PARTS)
                    for h in range(2):
                        cols = slice(512 * h, 512 * h + 512)
                        then(dve.tensor_tensor(tmp[:, h, :], ps[:, 2 * t + h, :], gate[:, 1, cols], ALU.mult))
                        dve.tensor_tensor(x[:, t, cols], x[:, t, cols], tmp[:, h, :], ALU.add).then_inc(x_ffn, 1)

            def picks(dst, s, weighted):
                for t in range(NT):
                    if weighted:
                        i = dve.tensor_scalar(dst[:, t, :], iota_row[:], posS[:, t, bass.ds(s, 1)],
                                              wS[:, t, bass.ds(s, 1)], ALU.is_equal, ALU.mult)
                    else:
                        i = dve.tensor_scalar(dst[:, t, :], iota_row[:], posS[:, t, bass.ds(s, 1)], None, ALU.is_equal)
                return i

            def route():
                dve.wait_ge(logit_ps, 1)
                dve.tensor_copy(lgT[:], ps[0:N_EXP, 4, 0:SEQ]).then_inc(logits_copied, 1)
                dve.wait_ge(logit_ps, 2)
                then(dve.tensor_copy(lg[:], ps[:, 6, 0:NT * N_EXP].rearrange("p (t e) -> p t e", t=NT)))
                for t in range(NT):
                    i = dve.max(mv[:, t, :], lg[:, t, :])
                then(i)
                for t in range(NT):
                    i = dve.max_index(mi[:, t, :], mv[:, t, :], lg[:, t, :])
                then(i)
                then(dve.tensor_copy(mf[:], mi[:]))
                dve.tensor_tensor(dlt[:], mv[:, :, 1], mv[:, :, 0], ALU.subtract).then_inc(gap_ready, 1)
                for t in range(NT):
                    for r in range(2):
                        i = dve.tensor_scalar(oh[:, t, r, :], iota_row[:, 0:N_EXP], mf[:, t, r:r + 1], None,
                                              ALU.is_equal)
                then(i)
                dve.tensor_tensor(chosen[:], oh[:, :, 0, :], oh[:, :, 1, :], ALU.add).then_inc(chosen_ready, 1)
                dve.wait_ge(gap_exp, 1)
                then(dve.tensor_scalar(den2[:], edl[:], 1.0, None, ALU.add))
                then(dve.reciprocal(w12[:, 0, :], den2[:]))
                then(dve.tensor_tensor(w12[:, 1, :], w12[:, 0, :], edl[:], ALU.mult))
                for t in range(NT):
                    then(dve.tensor_scalar(wtmp[:, t, :], oh[:, t, 0, :], w12[:, 0, t:t + 1], None, ALU.mult))
                    then(dve.scalar_tensor_tensor(out=wS[:, t, 0:N_EXP], in0=oh[:, t, 1, :], scalar=w12[:, 1, t:t + 1],
                                                  in1=wtmp[:, t, :], op0=ALU.mult, op1=ALU.add))
                dve.wait_ge(pos_ps, 1)
                for t in range(NT):
                    i = dve.scalar_tensor_tensor(out=wtmp[:, t, :], in0=ps[:, 5, t * N_EXP:t * N_EXP + N_EXP],
                                                 scalar=1.0, in1=chosen[:, t, :], op0=ALU.add, op1=ALU.mult)
                then(i)
                then(dve.tensor_scalar(posS[:, :, 0:N_EXP], wtmp[:], -1.0, None, ALU.add))
                picks(pick, 0, False).then_inc(pick_ready, 1)
                then(dve.tensor_scalar(over[:], ps[:, 5, 2 * N_EXP:3 * N_EXP], float(P), None, ALU.is_gt))
                then(dve.memset(rank[:, 0:1], 0.0))
                for e in range(N_EXP):
                    then(dve.tensor_tensor(rank[:, e + 1:e + 2], rank[:, e:e + 1], over[:, e:e + 1], ALU.add))
                then(dve.memset(tabf[:], 0.0))
                for o in range(MAX_OVER):
                    s = N_EXP + o
                    then(dve.scalar_tensor_tensor(out=sel[:, o, :], in0=rank[:, 0:N_EXP], scalar=float(o),
                                                  in1=over[:], op0=ALU.is_equal, op1=ALU.mult))
                    for t in range(NT):
                        dve.tensor_tensor(prod[:, t, :], sel[:, o, :], posS[:, t, 0:N_EXP], ALU.mult)
                        dve.tensor_tensor(prod[:, NT + t, :], sel[:, o, :], wS[:, t, 0:N_EXP], ALU.mult)
                    then(dve.tensor_tensor(prod[:, 4, :], sel[:, o, :], iota_row[:, 0:N_EXP], ALU.mult))
                    dve.reduce_sum(posr[:], prod[:, 0:NT, :], AX_X)
                    dve.reduce_sum(wS[:, :, s], prod[:, NT:2 * NT, :], AX_X)
                    then(dve.reduce_sum(tabf[:, 0, o:o + 1], prod[:, 4, :], AX_X))
                    dve.tensor_scalar(posS[:, :, s], posr[:], -float(P), None, ALU.add)
                    then(dve.tensor_scalar(tabf[:, 1, o:o + 1], rank[:, N_EXP:N_EXP + 1], float(o), None, ALU.is_gt))
                then(dve.tensor_copy(tabf[:, 1, MAX_OVER:MAX_OVER + 1], rank[:, N_EXP:N_EXP + 1]))
                dve.memset(posS[:, :, N_SLOT:], -1.0)
                then(dve.memset(wS[:, :, N_SLOT:], 0.0))
                dve.tensor_copy(table[:], tabf[:]).then_inc(table_ready, 1)

            def input_low():
                dve.tensor_tensor(hTl[:, :, 0:P], xsT[:], hTh[:, :, 0:P].bitcast(F32),
                                  ALU.subtract).then_inc(slot_lo, 1)

            def gated_output(n):
                dve.wait_ge(parts_used, n * (NB * PARTS) + FF_BASE[1])
                for h in range(2):
                    i = dve.tensor_tensor(ysb[:, 512 * h:512 * h + 512], ps[:, h, :],
                                          gate[:, 1, 512 * h:512 * h + 512], ALU.mult)
                i.then_inc(y_ready, 1)

            def add_to_x(n, marks=False):
                for i in range(4):
                    t, cols = 1 - i // 2, slice(512 * (i % 2), 512 * (i % 2) + 512)
                    dve.wait_ge(comb_ps, n * 4 + (i - 3))
                    dve.wait_ge(x_added, n * 4)
                    dve.tensor_tensor(x[:, t, cols], x[:, t, cols], ps[:, i, :], ALU.add).then_inc(x_added, 1)
                    if marks and i % 2:
                        dve.memset(done_mark[:, t + 2:t + 3], 0.0).then_inc(moe_done, 1)

            def slot(s, first, split, follows):
                def next_rows():
                    dve.wait_ge(gather_ps, s + 1)
                    picks(pick, s + 1, False).then_inc(pick_ready, 1)
                    picks(pickw, s, True).then_inc(pickw_ready, 1)

                def spread(j):
                    dve.wait_ge(rows_ps, s * SPREAD + (j + 1))
                    dve.tensor_copy(xs_rows[:, bass.ds(j * (D // SPREAD), D // SPREAD)],
                                    ps[:, 2, 0:D // SPREAD]).then_inc(rows_copied, 1)

                def next_input():
                    dve.wait_ge(slot_hi, s + 2)
                    input_low()

                blocks(FF_BASE[1], s * NB, 2, split, follows,
                       summed=None if first else lambda: add_to_x(s),
                       earlier=None if first else lambda: gated_output(s),
                       later=next_rows, spread=spread, ahead=next_input)

            columns()
            dve.wait_ge(x_loaded, 16 * NT)
            normalise(0)
            setup()
            for layer in range(DEPTH):
                first = [part[:-1] for part in straight_parts("in", layer, 0)]
                if not layer:
                    mod_round(0, 0)
                    mod_columns(0)
                else:
                    dense_out()
                    normalise(2 * layer)
                low(*first[0])
                split_transposed(3 * layer, 0)
                low(*first[1])
                straight("in", layer, 1)
                for c in range(IN_CHUNKS):
                    for t in range(NT):
                        rope(layer, c, t)
                    if c + 2 < IN_CHUNKS:
                        straight("in", layer, c + 2)
                    elif c + 2 == IN_CHUNKS:
                        straight("out", layer, 0)
                attention(layer)
                split_transposed(3 * layer + 1, None)
                mod_columns(layer + 1)
                straight("out", layer, 1)
                dve.wait_ge(gates_ready, 4 * layer + 4)
                mixed(layer)
                dve.wait_ge(x_mixed, 4 * layer + 4)
                normalise(2 * layer + 1)
                split_transposed(3 * layer + 2, 1)
                if not layer:
                    dve.wait_ge(rw_hi, 1)
                    dve.tensor_tensor(rwl[:], rw[:], rwh[:].bitcast(F32), ALU.subtract).then_inc(rw_lo, 1)
                    blocks(FF_BASE[0], 0, 4)
                else:
                    route()
            dve.memset(done_mark[:, 0:1], 0.0).then_inc(x_added, 4)
            dve.memset(done_mark[:, 1:2], 0.0).then_inc(rows_copied, 1)
            dve.wait_ge(slot_hi, 1)
            input_low()
            slot(0, True, True, True)
            with dve.Fori(0, N_EXP - 2) as s:
                slot(s + 1, False, True, True)
            slot(N_EXP - 1, False, True, False)
            dve.wait_ge(table_ready, 1)
            with dve.Fori(0, MAX_OVER) as o:
                used = dve.value_load(table[0:1, 1, bass.ds(o, 1)], min_val=0, max_val=1)
                with dve.If(used > 0):
                    slot(o + N_EXP, False, False, False)
            extra = dve.value_load(table[0:1, 1, MAX_OVER:MAX_OVER + 1], min_val=0, max_val=MAX_OVER)
            gated_output(extra + N_EXP)
            add_to_x(extra + N_EXP, marks=True)
            dve.wait_ge(late_loaded, 32)
            normalise(4)

        @block.tensor
        def _(pe):
            def ada_chunk(layer, n):
                slot, _, loaded = plan[("ada", layer, n)]
                r, q = n // 4, n % 4
                pe.wait_ge(w_loaded[slot], loaded)
                if q == 0 and layer + r:
                    pe.wait_ge(mod_ready, 3 * layer + r)
                for kk in range(2):
                    k = 2 * q + kk
                    for g in range(4):
                        mm = pe.matmul(ps[32 * g:32 * g + 32, 2, :], c_rep[:, k, :],
                                       W[:, slot, kk * 2048 + g * 512:kk * 2048 + g * 512 + 512],
                                       start=(k == 0), stop=(k == KD - 1))
                mm.then_inc(ada_used, 1)

            def mod_columns(n):
                rounds = ((0,), (1, 2, 0), (1, 2))[n]
                pe.wait_ge(mod_ready, (1, 4, 6)[n])
                for r in rounds:
                    for i in range(4):
                        mm = pe.matmul(ps[:, 0, 16 * r + i:16 * r + i + 13:4], modrow[:, r, i * P:i * P + P],
                                       ident[:, 0:P:32], start=True, stop=True)
                mm.then_inc(cols_ps, 1)

            def gates(layer):
                for i, chunk in enumerate((4, 5, 10, 11)):
                    g, r = chunk % 4, chunk // 4
                    pe.matmul(ps[:, 4 + i, :], ones[32 * g:32 * g + 1, :], modrow[32 * g:32 * g + 1, r, :],
                              start=True, stop=True).then_inc(gates_ps, 1)

            def transpose_all(n):
                for kk in range(KD // 2):
                    if kk >= 2:
                        pe.wait_ge(tr_copied, 4 * n + kk - 1)
                    for h in range(2):
                        for t in range(NT):
                            at = (2 * kk + h) * P
                            mm = pe.transpose(ps[:, 2 + kk % 2, h * SEQ + t * P:h * SEQ + t * P + P],
                                              xn[:, t, at:at + P], ident[:])
                    mm.then_inc(tr_ps, 1)

            def wait_part(q):
                pe.wait_ge(hi_done, q + 1)
                pe.wait_ge(lo_done, q + 1)
                pe.wait_ge(lop_done, q + 1)

            def three(dst, stat_hi, stat_lo, hi, lo, start, stop):
                pe.matmul(dst, stat_hi, hi, start=start, stop=False, skip_group_check=True)
                pe.matmul(dst, stat_hi, lo, start=False, stop=False, skip_group_check=True)
                return pe.matmul(dst, stat_lo, hi, start=False, stop=stop, skip_group_check=True)

            def project(kind, layer, c, split=None):
                parts = list(straight_parts(kind, layer, c))
                hslot, n = parts[0][2], parts[0][4] // 4
                hi, lo = (h[:, 0:KD * n].rearrange("p (k n) -> p k n", k=KD) for h in halves(hslot))
                for t in range(NT):
                    if kind == "in":
                        i = 2 * c + t
                        if i >= 2:
                            pe.wait_ge(rope_done, 2 * IN_CHUNKS * layer + i - 1)
                        bank = i % 2
                    else:
                        bank = 4 + 2 * c + t
                    tok = slice(t * P, t * P + P)
                    for k in range(KD):
                        if t == 0 and k % 4 == 0:
                            wait_part(parts[k // 4][0])
                        if t == 0 and c == 0 and k % 2 == 0:
                            pe.wait_ge(tr_lo, 4 * split + k // 2 + 1)
                        mm = three(ps[:, bank, 0:n], hTh[:, k, tok], hTl[:, k, tok], hi[:, k, :], lo[:, k, :],
                                   k == 0, k == KD - 1)
                        if t and k % 4 == 3:
                            mm.then_inc(parts_used, 1)
                    if t == 0:
                        mm.then_inc(proj_ps if kind == "in" else wo_ps, 1)

            def attention(layer):
                pe.wait_ge(rope_done, 2 * IN_CHUNKS * (layer + 1))
                for m in range(QK_TILES // 2):
                    if m >= 2:
                        s, per = (qkT_even, 4) if m % 2 == 0 else (qkT_odd, 3)
                        pe.wait_ge(s, per * layer + m // 2)
                    for h in range(2):
                        for t in range(NT):
                            mm = pe.transpose(ps[:, 2 + m % 2, h * SEQ + t * P:h * SEQ + t * P + P],
                                              qk[:, t, (2 * m + h) * P:(2 * m + h) * P + P], ident[:])
                    mm.then_inc(qkT_ps, 1)
                pe.wait_ge(qkT_even, 4 * layer + 4)
                pe.wait_ge(qkT_odd, 3 * layer + 3)
                for i in range(UNITS + 3):
                    if i < UNITS:
                        u, par, m, t = UNITS * layer + i, i % 2, pair(i), i // 8
                        if i >= 2:
                            pe.wait_ge(exp_done, u - 1)
                        for h in range(2):
                            if m < 4:
                                q_tile, k_tile = m, 4 + (m // 2 + h) % 2
                            else:
                                q_tile, k_tile = 2 + m, 6 + m
                            rows = slice(HEAD * h, HEAD * h + HEAD)
                            mm = pe.matmul(ps[:, 4 + 2 * par + h, 0:SEQ], qkT[rows, q_tile, t * P:t * P + P],
                                           qkT[rows, k_tile, :], start=True, stop=True)
                        mm.then_inc(s_ps, 1)
                    for k, (of, n) in enumerate(ADA_LATER[layer]):
                        if ADA_STEP[k] == i:
                            ada_chunk(of, n)
                    if 2 <= i <= UNITS + 1:
                        u, par, m = UNITS * layer + i - 2, i % 2, pair(i - 2)
                        pe.wait_ge(probs_done, u + 1)
                        if i >= 3:
                            pe.wait_ge(pt_done, u)
                        for n in range(4 if m < 4 else 2):
                            mm = pe.transpose(ps[:, 3, n * P:n * P + P],
                                              E[:, par, n // 2, (n % 2) * P:(n % 2) * P + P], ident[:])
                        mm.then_inc(pt_ps, 1)
                    if i >= 3:
                        u, par, m = UNITS * layer + i - 3, (i - 3) % 2, pair(i - 3)
                        pe.wait_ge(pt_done, u + 1)
                        if i >= 5:
                            pe.wait_ge(o_done, u - 1)
                        for h in range(2 if m < 4 else 1):
                            width = HEAD if m < 4 else P
                            col = (m // 2) * HEAD if m < 4 else P + (m - 4) * P
                            for kt in range(NT):
                                mm = pe.matmul(ps[:, par, h * width:h * width + width], PT[:, par, 2 * h + kt, :],
                                               v[:, kt, col:col + width], start=(kt == 0), stop=(kt == NT - 1))
                        mm.then_inc(o_ps, 1)

            def gate_up(i, nu, ks, base, b, is_first):
                half, t = (i // 2, i % 2) if nu == 4 else (i, 0)
                tok = slice(t * P, t * P + P)
                cols = slice(half * HB, half * HB + HB)
                for k in ks:
                    if i == 0 and k % 2 == 0:
                        wait_part(b * PARTS + (base + k // 2))
                        if is_first and nu == 4:
                            pe.wait_ge(tr_lo, 4 * 2 + k // 2 + 1)
                    mm = three(ps[:, 4 + i % 2, :].rearrange("p (g n) -> p g n", g=2), hTh[:, k, tok], hTl[:, k, tok],
                               hg_ff[0][:, k // 4, k % 4, :, cols], hg_ff[1][:, k // 4, k % 4, :, cols],
                               k == 0, k == KD - 1)
                    if i == nu - 1 and k % 2 == 1:
                        mm.then_inc(parts_used, 1)
                    elif i < nu - 1 and k == KD - 1:
                        mm.then_inc(gu_ps, 1)

            def turn(i, nu, b):
                pe.wait_ge(act_done, b * nu + (U0[nu] + i + 1))
                for n in range(2):
                    mm = pe.transpose(ps[:, 6 + i % 2, n * P:n * P + P], act_sb[:, i % 2, n * P:n * P + P], ident[:])
                mm.then_inc(at_ps, 1)

            def down(i, nu, ns, base, b, is_first, is_last=False):
                half, t = (i // 2, i % 2) if nu == 4 else (i, 0)
                if 0 in ns:
                    pe.wait_ge(at_hi, b * nu + (U0[nu] + i + 1))
                    pe.wait_ge(at_lo, b * nu + (U0[nu] + i + 1))
                    if i % (nu // 2) == 0:
                        wait_part(b * PARTS + (base + 4 + half))
                for n in ns:
                    k = 2 * half + n
                    for h in range(2):
                        cols = slice(512 * h, 512 * h + 512)
                        mm = three(ps[:, 2 * t + h, :], aTh[:, i % 2, n, :], aTl[:, i % 2, n, :],
                                   hd_ff[0][:, k, cols], hd_ff[1][:, k, cols], is_first and k == 0, False)
                if i == nu - 1 or (i == nu - 2 and ns == ((1,) if nu == 2 else (0,))):
                    mm.then_inc(parts_used, 1)
                elif is_last and i == nu - 2:
                    mm.then_inc(tile_ps, 1)

            def blocks(base, first, nu, summed=None, spread=None, rows=None, gathering=None):
                def one(b, is_first, is_last, j=None):
                    if is_last and rows:
                        rows()
                    gate_up(0, nu, range(KD), base, b, is_first)
                    if spread and j is not None:
                        spread(j)
                    if is_last and gathering:
                        gathering()
                    for i in range(1, nu):
                        gate_up(i, nu, range(0, KD // 2), base, b, is_first)
                        turn(i - 1, nu, b)
                        gate_up(i, nu, range(KD // 2, KD), base, b, is_first)
                        if i < nu - 1:
                            down(i - 1, nu, (0, 1), base, b, is_first)
                    if is_first and summed:
                        summed()
                    down(nu - 2, nu, (0,), base, b, is_first)
                    turn(nu - 1, nu, b)
                    down(nu - 2, nu, (1,), base, b, is_first, is_last)
                    down(nu - 1, nu, (0, 1), base, b, is_first)

                one(first + 0, True, False)
                with pe.Fori(0, SPREAD) as j:
                    one(first + (j + 1), False, False, j)
                for n in range(SPREAD + 1, NB - 1):
                    one(first + n, False, False)
                one(first + (NB - 1), False, True)

            def route():
                pe.wait_ge(rw_lo, 1)
                for k in range(KD):
                    if k % 2 == 0:
                        pe.wait_ge(tr_lo, 4 * 5 + k // 2 + 1)
                    for i, (w, a) in enumerate(((rwh, hTh), (rwl, hTh), (rwh, hTl), (rwl, hTl))):
                        mm = pe.matmul(ps[0:N_EXP, 4, 0:SEQ], w[:, k, :], a[:, k, :],
                                       start=(k == 0 and i == 0), stop=(k == KD - 1 and i == 3))
                mm.then_inc(logit_ps, 1)
                pe.wait_ge(logits_copied, 1)
                for t in range(NT):
                    mm = pe.transpose(ps[:, 6, t * N_EXP:t * N_EXP + N_EXP], lgT[:, t * P:t * P + P],
                                      ident[0:N_EXP, 0:N_EXP])
                mm.then_inc(logit_ps, 1)
                pe.wait_ge(chosen_ready, 1)
                at = [slice(i * N_EXP, i * N_EXP + N_EXP) for i in range(3)]
                pe.matmul(ps[:, 5, at[0]], before[:], chosen[:, 0, :], start=True, stop=True)
                for i, first in ((1, ones), (2, ones)):
                    pe.matmul(ps[:, 5, at[i]], first[:], chosen[:, 0, :], start=True, stop=False)
                    mm = pe.matmul(ps[:, 5, at[i]], (before if i == 1 else ones)[:], chosen[:, 1, :],
                                   start=False, stop=True)
                mm.then_inc(pos_ps, 1)

            def gather(n):
                pe.wait_ge(pick_ready, n)
                for k in range(KD):
                    for t in range(NT):
                        mm = pe.matmul(ps[:, 2 + k // 4, (k % 4) * P:(k % 4) * P + P], xn[:, t, k * P:k * P + P],
                                       pick[:, t, :], start=(t == 0), stop=(t == NT - 1))
                mm.then_inc(gather_ps, 1)

            def combine(n):
                pe.wait_ge(pickT_ready, n)
                pe.wait_ge(y_ready, n)
                for i in range(4):
                    cols = slice(512 * (i % 2), 512 * (i % 2) + 512)
                    pe.matmul(ps[:, i, :], pickT[:, 1 - i // 2, :], ysb[:, cols],
                              start=True, stop=True).then_inc(comb_ps, 1)

            def slot(s, follows):
                def summed():
                    combine(s)
                    pe.wait_ge(x_added, s * 4 + 2)

                def rows():
                    pe.wait_ge(pickw_ready, s + 1)
                    pe.wait_ge(x_added, s * 4 + 4)
                    pe.wait_ge(rows_copied, s * SPREAD + (SPREAD + 1))
                    for t in range(NT):
                        mm = pe.transpose(ps[:, 2, t * P:t * P + P], pickw[:, t, :], ident[:])
                    mm.then_inc(pickT_ps, 1)

                def spread(j):
                    pe.wait_ge(pick_ready, s + 2)
                    pe.wait_ge(x_added, s * 4 + 4)
                    pe.wait_ge(rows_copied, s * SPREAD + (j + 1))
                    for t in range(NT):
                        mm = pe.matmul(ps[:, 2, 0:D // SPREAD], pick[:, t, :],
                                       xn[:, t, bass.ds(j * (D // SPREAD), D // SPREAD)],
                                       start=(t == 0), stop=(t == NT - 1))
                    mm.then_inc(rows_ps, 1)

                def gathering():
                    pe.wait_ge(pickT_ready, s + 1)
                    for k in range(KD):
                        mm = pe.transpose(ps[:, 2 + k // 4, (k % 4) * P:(k % 4) * P + P],
                                          xs_rows[:, k * P:k * P + P], ident[:])
                    mm.then_inc(gather_ps, 1)

                pe.wait_ge(slot_lo, s + 1)
                blocks(FF_BASE[1], s * NB, 2, summed if follows else None, spread, rows, gathering)

            pe.wait_ge(setup_done, SETUP)
            pe.wait_ge(vec_silu, 1)
            pe.transpose(ps[:, 3, 0:40], vecrows[:], ident[0:40, 0:40]).then_inc(vec_ps, 1)
            pe.wait_ge(vec_cols, 1)
            for layer in range(DEPTH):
                if not layer:
                    for n in range(ADA_FIRST):
                        ada_chunk(0, n)
                    mod_columns(0)
                    pe.wait_ge(cols_ready, 1)
                pe.wait_ge(xn_done, 4 * layer + 2)
                transpose_all(3 * layer)
                for c in range(IN_CHUNKS):
                    project("in", layer, c, 3 * layer)
                attention(layer)
                pe.wait_ge(mix_done, NT * N_DIFF * (layer + 1))
                pe.wait_ge(o_done, UNITS * (layer + 1))
                pe.wait_ge(mod_ready, (4, 6)[layer])
                transpose_all(3 * layer + 1)
                mod_columns(layer + 1)
                gates(layer)
                pe.wait_ge(gates_ready, 4 * layer + 4)
                for c in range(OUT_CHUNKS):
                    project("out", layer, c, 3 * layer + 1)
                pe.wait_ge(xn_done, 4 * layer + 4)
                transpose_all(3 * layer + 2)
                if not layer:
                    blocks(FF_BASE[0], 0, 4)
                else:
                    route()
            gather(1)
            slot(0, False)
            with pe.Fori(0, N_EXP - 1) as s:
                slot(s + 1, True)
            pe.wait_ge(table_ready, 1)
            with pe.Fori(0, MAX_OVER) as o:
                used = pe.value_load(table[0:1, 1, bass.ds(o, 1)], min_val=0, max_val=1)
                with pe.If(used > 0):
                    slot(o + N_EXP, True)
            extra = pe.value_load(table[0:1, 1, MAX_OVER:MAX_OVER + 1], min_val=0, max_val=MAX_OVER)
            combine(extra + N_EXP)


_INS = ["x", "c", "positions", "inv_freq", "ada_w", "ada_b", "norm_mix_g", "norm_ffn_g", "w_in", "w_out",
        "sink", "lam_q1", "lam_k1", "lam_q2", "lam_k2", "subln_g", "ffn_w_gate", "ffn_w_up", "ffn_w_down",
        "router_w", "moe_w_gate", "moe_w_up", "moe_w_down", "final_g"]


def kernel(**inputs):
    import concourse.bacc as _bacc
    from concourse.bass_utils import run_bass_kernel_spmd as _run

    nc = _bacc.Bacc("TRN2", target_bir_lowering=False, num_devices=1, dynamic_dma_scratch_size=1024)
    freq = 1.0 / (10000.0 ** (np.arange(0, HEAD, 2, dtype=np.float32) / HEAD))
    data = dict(inputs, inv_freq=freq.astype(np.float32).reshape(1, HALF))
    arrays, args = {}, []
    for name in _INS:
        a = np.ascontiguousarray(data[name])
        arrays[f"in_{name}_dram"] = a
        args.append(nc.dram_tensor(f"in_{name}_dram", a.shape, mybir.dt.from_np(a.dtype), kind="ExternalInput").ap())
    out = nc.dram_tensor("out_0_dram", (1, SEQ, D), F32, kind="ExternalOutput").ap()
    build(nc, *args, out)
    r = _run(nc, [arrays], core_ids=[0])
    return r.results[0]["out_0_dram"]
```
